# Optimizing a Trainium2 kernel written in Bass

```python
import math
import jax, jax.numpy as jnp
from jax import lax
import numpy as np

D_MODEL = 1024
BATCH = 1
SEQ = 1024
DEPTH = 1
DEC_BATCH = 1
DEC_SEQ = 512
PAST_LEN = 128

D_S5 = D_MODEL // 2
S5_GROUP = 16
S5_GROUPS = D_S5 // S5_GROUP
S5_STATE = 64
N_DIR = 2
D_CONV = D_MODEL // 2
CONV_WIDTH = 3
N_MEM = 256
XATTN_HEADS = 4
XATTN_HEAD_DIM = D_MODEL // XATTN_HEADS
D_FF = -(-8 * D_MODEL // (3 * 256)) * 256
N_GATES = 2
D_IN = D_S5 + 3 * D_CONV + N_GATES * D_MODEL
EPS = 1e-6
DT_MIN = 1e-3
DT_MAX = 1e-1

kernel_name = "hybrid_s5_shortconv_memxattn_encoder"

def rmsnorm(x, g):
    xf = x.astype(jnp.float32)
    r = lax.rsqrt(jnp.mean(xf * xf, axis=-1, keepdims=True) + EPS)
    return (xf * r * g.astype(jnp.float32)).astype(x.dtype)

def s5_combine(e1, e2):
    a1, b1 = e1
    a2, b2 = e2
    return a1 * a2, a2 * b1 + b2

def s5_direction(u, a_re, a_im, log_dt, b_re, b_im, c_re, c_im, reverse):
    f32 = jnp.float32
    A = lax.complex(a_re.astype(f32), a_im.astype(f32))
    dt = jnp.exp(log_dt.astype(f32))[:, None]
    A_bar = jnp.exp(A * dt)
    Bm = lax.complex(b_re.astype(f32), b_im.astype(f32))
    B_bar = ((A_bar - 1.0) / A)[..., None] * Bm
    Cm = lax.complex(c_re.astype(f32), c_im.astype(f32))
    bu = jnp.einsum("gnp,blgp->blgn", B_bar, u.astype(jnp.complex64))
    a = jnp.broadcast_to(A_bar, bu.shape)
    _, h = lax.associative_scan(s5_combine, (a, bu), reverse=reverse, axis=1)
    return jnp.einsum("gpn,blgn->blgp", Cm, h).real

def hybrid_mixer(xn, w_in, b_gate, s5_a_re, s5_a_im, s5_log_dt, s5_b_re, s5_b_im,
                 s5_c_re, s5_c_im, s5_d, w_glu_a, w_glu_b, conv_w, w_conv_out, w_o):
    f32 = jnp.float32
    bsz, L, _ = xn.shape
    proj = jnp.einsum("bld,de->ble", xn, w_in)
    u_s5, x_c, gate_b, gate_c, g = jnp.split(
        proj, [D_S5, D_S5 + D_CONV, D_S5 + 2 * D_CONV, D_S5 + 3 * D_CONV], axis=-1)
    gates = jax.nn.sigmoid((g + b_gate).astype(f32))

    u = u_s5.astype(f32).reshape(bsz, L, S5_GROUPS, S5_GROUP)
    y = (s5_direction(u, s5_a_re[0], s5_a_im[0], s5_log_dt[0], s5_b_re[0], s5_b_im[0],
                      s5_c_re[0], s5_c_im[0], reverse=False)
         + s5_direction(u, s5_a_re[1], s5_a_im[1], s5_log_dt[1], s5_b_re[1], s5_b_im[1],
                        s5_c_re[1], s5_c_im[1], reverse=True))
    y = y.reshape(bsz, L, D_S5) + s5_d.astype(f32) * u_s5.astype(f32)
    y = jax.nn.gelu(y).astype(xn.dtype)
    s5_out = (y @ w_glu_a) * jax.nn.sigmoid(y @ w_glu_b)

    z = gate_c * x_c
    zp = jnp.pad(z, ((0, 0), (1, 1), (0, 0)))
    zc = conv_w[0] * zp[:, :-2] + conv_w[1] * zp[:, 1:-1] + conv_w[2] * zp[:, 2:]
    conv_out = (gate_b * zc) @ w_conv_out

    merged = gates[..., :D_MODEL] * s5_out.astype(f32) + gates[..., D_MODEL:] * conv_out.astype(f32)
    return merged.astype(xn.dtype) @ w_o

def memory_cross_attention(hn, mem, norm_mem_g, w_q, w_kv, w_xo):
    bsz, L, _ = hn.shape
    mn = rmsnorm(mem, norm_mem_g)
    q = (hn @ w_q).reshape(bsz, L, XATTN_HEADS, XATTN_HEAD_DIM)
    k, v = jnp.split(mn @ w_kv, 2, axis=-1)
    k = k.reshape(bsz, N_MEM, XATTN_HEADS, XATTN_HEAD_DIM)
    v = v.reshape(bsz, N_MEM, XATTN_HEADS, XATTN_HEAD_DIM)
    s = jnp.einsum("blhd,bmhd->bhlm", q, k).astype(jnp.float32) * (XATTN_HEAD_DIM ** -0.5)
    p = jax.nn.softmax(s, axis=-1).astype(v.dtype)
    o = jnp.einsum("bhlm,bmhd->blhd", p, v).reshape(bsz, L, D_MODEL)
    return o @ w_xo

def swiglu(hn, w_gate_up, w_down):
    gate, up = jnp.split(hn @ w_gate_up, 2, axis=-1)
    return (jax.nn.silu(gate) * up) @ w_down

def trunk(x, mem, norm_mix_g, w_in, b_gate, s5_a_re, s5_a_im, s5_log_dt, s5_b_re, s5_b_im,
          s5_c_re, s5_c_im, s5_d, w_glu_a, w_glu_b, conv_w, w_conv_out, w_o,
          norm_xattn_g, norm_mem_g, w_q, w_kv, w_xo, norm_ffn_g, w_gate_up, w_down,
          norm_final_g):
    h = x
    for l in range(DEPTH):
        xn = rmsnorm(h, norm_mix_g[l])
        h = h + hybrid_mixer(xn, w_in[l], b_gate[l], s5_a_re[l], s5_a_im[l], s5_log_dt[l],
                             s5_b_re[l], s5_b_im[l], s5_c_re[l], s5_c_im[l], s5_d[l],
                             w_glu_a[l], w_glu_b[l], conv_w[l], w_conv_out[l], w_o[l])
        hn = rmsnorm(h, norm_xattn_g[l])
        h = h + memory_cross_attention(hn, mem, norm_mem_g[l], w_q[l], w_kv[l], w_xo[l])
        hn = rmsnorm(h, norm_ffn_g[l])
        h = h + swiglu(hn, w_gate_up[l], w_down[l])
    return rmsnorm(h, norm_final_g)

def setup_inputs(seed: int = 0) -> dict:
    key = jax.random.key(seed)
    ks = jax.random.split(key, 32)
    f32 = jnp.float32
    nrm = lambda k, shape, scale: jax.random.normal(k, shape, f32) * scale
    gain = lambda k, shape: 1.0 + 0.02 * jax.random.normal(k, shape, f32)
    sd = (DEPTH, N_DIR, S5_GROUPS, S5_STATE)
    n_idx = jnp.arange(S5_STATE, dtype=f32)
    return {
        "x_prompt": nrm(ks[0], (BATCH, SEQ, D_MODEL), 1.0),
        "x_sample": nrm(ks[1], (DEC_BATCH, DEC_SEQ, D_MODEL), 1.0),
        "mem_prompt": nrm(ks[2], (BATCH, N_MEM, D_MODEL), 1.0),
        "mem_sample": nrm(ks[3], (DEC_BATCH, N_MEM, D_MODEL), 1.0),
        "norm_mix_g": gain(ks[4], (DEPTH, D_MODEL)),
        "w_in": nrm(ks[5], (DEPTH, D_MODEL, D_IN), D_MODEL ** -0.5),
        "b_gate": nrm(ks[6], (DEPTH, N_GATES * D_MODEL), 0.01),
        "s5_a_re": -0.5 + 0.01 * jax.random.normal(ks[7], sd, f32),
        "s5_a_im": math.pi * n_idx + 0.01 * jax.random.normal(ks[8], sd, f32),
        "s5_log_dt": jax.random.uniform(ks[9], (DEPTH, N_DIR, S5_GROUPS), f32,
                                        math.log(DT_MIN), math.log(DT_MAX)),
        "s5_b_re": nrm(ks[10], sd + (S5_GROUP,), (2 * S5_GROUP) ** -0.5),
        "s5_b_im": nrm(ks[11], sd + (S5_GROUP,), (2 * S5_GROUP) ** -0.5),
        "s5_c_re": nrm(ks[12], (DEPTH, N_DIR, S5_GROUPS, S5_GROUP, S5_STATE), (2 * S5_STATE) ** -0.5),
        "s5_c_im": nrm(ks[13], (DEPTH, N_DIR, S5_GROUPS, S5_GROUP, S5_STATE), (2 * S5_STATE) ** -0.5),
        "s5_d": nrm(ks[14], (DEPTH, D_S5), 1.0),
        "w_glu_a": nrm(ks[15], (DEPTH, D_S5, D_MODEL), D_S5 ** -0.5),
        "w_glu_b": nrm(ks[16], (DEPTH, D_S5, D_MODEL), D_S5 ** -0.5),
        "conv_w": nrm(ks[17], (DEPTH, CONV_WIDTH, D_CONV), CONV_WIDTH ** -0.5),
        "w_conv_out": nrm(ks[18], (DEPTH, D_CONV, D_MODEL), D_CONV ** -0.5),
        "w_o": nrm(ks[19], (DEPTH, D_MODEL, D_MODEL), D_MODEL ** -0.5),
        "norm_xattn_g": gain(ks[20], (DEPTH, D_MODEL)),
        "norm_mem_g": gain(ks[21], (DEPTH, D_MODEL)),
        "w_q": nrm(ks[22], (DEPTH, D_MODEL, D_MODEL), D_MODEL ** -0.5),
        "w_kv": nrm(ks[23], (DEPTH, D_MODEL, 2 * D_MODEL), D_MODEL ** -0.5),
        "w_xo": nrm(ks[24], (DEPTH, D_MODEL, D_MODEL), D_MODEL ** -0.5),
        "norm_ffn_g": gain(ks[25], (DEPTH, D_MODEL)),
        "w_gate_up": nrm(ks[26], (DEPTH, D_MODEL, 2 * D_FF), D_MODEL ** -0.5),
        "w_down": nrm(ks[27], (DEPTH, D_FF, D_MODEL), D_FF ** -0.5),
        "norm_final_g": gain(ks[28], (D_MODEL,)),
    }

def reference(x_prompt, x_sample, mem_prompt, mem_sample, norm_mix_g, w_in, b_gate,
              s5_a_re, s5_a_im, s5_log_dt, s5_b_re, s5_b_im, s5_c_re, s5_c_im, s5_d,
              w_glu_a, w_glu_b, conv_w, w_conv_out, w_o, norm_xattn_g, norm_mem_g,
              w_q, w_kv, w_xo, norm_ffn_g, w_gate_up, w_down, norm_final_g):
    weights = (norm_mix_g, w_in, b_gate, s5_a_re, s5_a_im, s5_log_dt, s5_b_re, s5_b_im,
               s5_c_re, s5_c_im, s5_d, w_glu_a, w_glu_b, conv_w, w_conv_out, w_o,
               norm_xattn_g, norm_mem_g, w_q, w_kv, w_xo, norm_ffn_g, w_gate_up, w_down,
               norm_final_g)
    y_prompt = trunk(x_prompt, mem_prompt, *weights)
    y_sample = trunk(x_sample, mem_sample, *weights)
    return (y_prompt, y_sample)


_drawn_inputs = setup_inputs


def setup_inputs(seed=0):
    import zlib

    import numpy as np

    out = dict(_drawn_inputs(seed))
    spreads = {}
    factors = {'norm_mix_g': 3.078,
     'b_gate': 8.0,
     's5_a_re': 64.0,
     's5_a_im': 28.424,
     's5_log_dt': 28.944,
     's5_b_re': 39.84,
     's5_b_im': 39.76,
     's5_c_re': 39.848,
     's5_c_im': 39.696,
     'norm_xattn_g': 8.0,
     'norm_mem_g': 8.0,
     'norm_ffn_g': 15.174,
     'norm_final_g': 7.449}
    for name, (base, spread) in spreads.items():
        noise = np.random.default_rng([zlib.crc32(name.encode()), seed]).standard_normal(out[name].shape)
        drawn = base * np.exp(spread * noise) if base else spread * noise
        out[name] = __import__('jax').numpy.asarray(drawn.astype(out[name].dtype))
    for name, factor in factors.items():
        out[name] = (out[name] * factor).astype(out[name].dtype)
    return out
```

```python
import math

import concourse.bass as bass
from concourse import mybir

F32 = mybir.dt.float32
F32R = mybir.dt.float32r
I32 = mybir.dt.int32
ALU = mybir.AluOpType
ACT = mybir.ActivationFunctionType
AX = mybir.AxisListType

P = 128
D = 1024
KT = D // P
T_PROMPT, T_SAMPLE = 1024, 512
T = T_PROMPT + T_SAMPLE
BLK = 512
NB = T // BLK
NMEM = 256
M2 = 2 * NMEM
HEADS, HD = 4, 256
DH = 512
HT = DH // P
DFF = 2816
FT = DFF // P
EPS = 1e-6
SCALE = HD ** -0.5
GROUPS, GP, NS = 32, 16, 64
GD = 2 * GROUPS
C = 8
NC = T // C
NCP, NCS = T_PROMPT // C, T_SAMPLE // C
SLOTS = NC + 2
SLOT_S = NCP + 1
LAGS = 2 * C - 1
NPOW = C + 1

SLOTW = 1024
RING = 6

STAGES = [("kv", 16, 1), ("u", 4, 3), ("conv", 12, 3), ("co", 4, 6), ("gate", 16, 3), ("glu", 8, 6),
          ("wo", 8, 3), ("q", 8, 3), ("xo", 8, 3)]
SLOT0, RES0 = {}, {}
_n = _q = 0
for _name, _slots, _per in STAGES:
    SLOT0[_name], RES0[_name] = _n, _q
    _n += _slots
    _q += _slots * _per
SLOT0["ffn"], RES0["ffn"] = _n, _q
CHUNKS = FT // 2
CH_SLOTS, CH_RES = 6, 4 * NB + 2 * 4 * NB
NSLOT = _n + CHUNKS * CH_SLOTS

LOG2E = 1.4426950408889634
LN2_HI, LN2_LO = 0.693359375, -2.12194440e-4
SCAN_STEPS = NCP
ROUND = 12582912.0
TWO_PI = (6.28125, 0.0019350051879882812, 3.0199159819185e-07)


class Count:

    def __init__(self, sem):
        self.sem, self.n, self.raised = sem, 0, 0

    def up(self, ins, k=1):
        ins.then_inc(self.sem, k)
        self.n = self.n + k
        self.raised += k
        return self.n

    def enter(self, i, each):
        self.base, self.each, self.raised = self.n, each, 0
        self.n = self.base + i * each

    def leave(self, times):
        assert self.raised == self.each, (self.raised, self.each)
        self.n = self.base + times * self.each


def build(nc, io, scratch):
    base = 2048
    assert nc.sbuf_base <= base

    off = [base]

    def keep(name, shape, dt=F32):
        t = nc.alloc_sbuf_tensor_at(name, [P] + shape, dt, offset=off[0])
        off[0] += -(-4 * math.prod(shape) // 32) * 32
        return t

    XN = keep("XN", [2, KT, T], F32R)
    WR = keep("WR", [2, SLOTW])
    WHI = keep("WHI", [2, SLOTW], F32R)
    WLO = keep("WLO", [2, SLOTW], F32R)
    RB = keep("RB", [T])
    ones = keep("ones", [P])
    ident = keep("ident", [P])
    gains = keep("gains", [5, KT])
    bgate = keep("bgate", [2 * KT])
    bcol = keep("bcol", [2])
    convw = keep("convw", [HT, 3])
    epsc = keep("epsc", [1])
    sgn = keep("sgn", [2])
    rcol = keep("rcol", [4])
    LR = keep("LR", [GD])
    LI = keep("LI", [GD])
    s5d = keep("s5d", [GROUPS])
    smx = keep("smx", [2, 4])
    snm = keep("snm", [2, 4])
    ssm = keep("ssm", [2, 4])
    sri = keep("sri", [2, 4])
    w0 = off[0]
    K = 1024

    def at(name, kb, shape, dt=F32):
        assert w0 + kb * K + 4 * math.prod(shape) <= nc.sbuf_usable_end, name
        return nc.alloc_sbuf_tensor_at(name, [P] + shape, dt, offset=w0 + int(kb * K))

    MN = at("MN", 0, [2, KT, M2], F32R)
    MEM = at("MEM", 32, [KT, M2])
    XS = at("XS", 48, [2, T])
    SQ = at("SQ", 60, [2, T])
    ACC = at("ACC", 72, [T])
    MACC = at("MACC", 78, [M2])
    MSQ = at("MSQ", 80, [2, M2])
    KVS = at("KVS", 32, [2, M2])
    RM = at("RM", 84, [M2])
    PA = at("PA", 88, [16, GD])
    BX, BY, CX, CY, BBX, BBY = (at(n, 36 + 2 * i, [GROUPS, GP]) for i, n in
                                enumerate(("BX", "BY", "CX", "CY", "BBX", "BBY")))
    PVR, PVI, PWR, PWI = (at(n, 64.5 + 2.25 * i, [NPOW, GD]) for i, n in
                          enumerate(("PVR", "PVI", "PWR", "PWI")))
    PR, PI = at("PR", 76, [NPOW, GD]), at("PI", 78.25, [NPOW, GD])
    TB = at("TB", 76, [2, 4 * NPOW * GP])
    TC = at("TC", 80.5, [2, 4 * NPOW * GP])
    TX = at("TX", 85, [4 * NPOW * GP])
    UB = at("UB", 48, [2, C, NC])
    CIN = at("CIN", 0, [HT, 2, T], F32R)
    XC = at("XC", 48, [T + 1])
    Z = at("Z", 54.25, [T + 3])
    TT = at("TT", 60.5, [2, BLK])
    COS = at("COS", 48, [2, T])
    H = at("H", 0, [SLOTS, GD])
    U = at("U", 48.5, [GROUPS, NC])
    VN = at("VN", 72.5, [2, 4, P])
    WK = at("WK", 76.5, [2, 4, P])
    BBL = at("BBL", 80.5, [2, 4, GP])
    VT = at("VT", 81, [2, 4 * P])
    LL = at("LL", 85, [2, 2, LAGS * GP])
    DM = at("DM", 89, [GROUPS, GP])
    S1, S2 = at("S1", 91, [2, GD]), at("S2", 91.5, [2, GD])
    TG = at("TG", 72.5, [2, BLK])
    GS = at("GS", 76.5, [2, T])
    WO = at("WO", 72.5, [2, 4, P])
    ML = at("ML", 76.5, [2, 2, P])
    YS = at("YS", 78.5, [2, 2 * NC])
    YHL = at("YHL", 0, [2, HT, T], F32R)
    YL = at("YL", 48, [2, C, NC])
    G1L, G2L, COL = at("G1L", 48, [2, T]), at("G2L", 60, [2, T]), at("COL", 72, [2, T])
    SB = at("SB", 84, [T])
    HR = at("HR", 0, [KT, T])
    SQ2 = at("SQ2", 48, [2, T])
    ACC2 = at("ACC2", 82, [T])
    QS = at("QS", 66, [2, T])
    XR = at("XR", 66, [2, T])
    QL = at("QL", 48, [2, 2, BLK])
    KL = at("KL", 56, [2, 2, NMEM])
    VL = at("VL", 60, [2, 2, 2, P])
    PB = at("PB", 64, [2, 4, NMEM])
    PT = at("PT", 72, [2, 2, BLK])
    AF = at("AF", 48, [2, 2, T], F32R)
    SG = at("SG", 72, [T])
    TF = at("TF", 78, [2, BLK])
    YO = at("YO", 48, [2, T])

    U_d, CO_d, G_d, V_d, W_d, BB_d, L_d, M_d, Y_d, KV_d, Q_d = (
        scratch[k] for k in ("U", "CO", "G", "V", "W", "BB", "L", "M", "Y", "KV", "Q"))
    K_d = KV_d[0:KT]
    VV_d = KV_d[KT:2 * KT].rearrange("e p (m d) -> e p m d", d=P)

    PS = [nc.alloc_psum_tensor(f"bank{i}", [P, BLK], F32) for i in range(8)]

    sem = {}

    def S(name):
        if name not in sem:
            sem[name] = nc.alloc_semaphore(name)
        return sem[name]

    raw = [S("raw_even"), S("raw_odd")]
    whi, wlo = S("weights_hi"), S("weights_lo")
    res, evac = S("results"), S("evacuated")

    def loop(eng, times):
        return eng.Fori(0, times)

    block = nc.Block()
    block.__enter__()

    def zcols(b):
        return slice(b * BLK + (b == 2), (b + 1) * BLK + (b == 2))

    def blk(b):
        return slice(b * BLK, (b + 1) * BLK)

    def bank(q):
        return PS[(q - RES0["u"]) % RING]

    def one(a, i):
        return a[:, i] if isinstance(i, int) else a[:, bass.ds(i, 1)].rearrange(
            {3: "p o a -> p (o a)", 4: "p o a b -> p (o a) b"}[len(a.shape)])

    def tile_of(a, i):
        return a[i] if isinstance(i, int) else a[bass.ds(i, 1)].rearrange("o p t -> p (o t)")

    @block.sync
    def _(sp):
        def weights(n, parity, i=0):
            if not (isinstance(i, int) and n + 2 * i < 2):
                sp.wait_ge(wlo, n - 1 + 2 * i)
            sp.dma_start(WR[:, parity, :], tile_of(io["W_all"], n + 2 * i)).then_inc(raw[parity], 16)

        for j, name in enumerate(("a_re", "a_im", "log_dt")):
            sp.dma_start(PA[:, j, :], io[name]).then_inc(S("params_in"), 16)
        for dst, src in ((ones, "ones"), (gains, "gains"), (epsc, "eps"), (sgn, "sgn"), (ident, "ident"),
                         (bgate, "bgate"), (convw, "convw")):
            sp.dma_start(dst[:], io[src]).then_inc(S("consts_in"), 16)
        sp.dma_start(s5d[0:GP, :], io["s5_d"]).then_inc(S("consts_in"), 16)
        sp.dma_start(MEM[:, 0:4, :], io["memT"][:, 0:4, :]).then_inc(S("mem_in0"), 16)
        weights(0, 0)
        sp.dma_start(MEM[:, 4:8, :], io["memT"][:, 4:8, :]).then_inc(S("mem_in1"), 16)
        weights(1, 1)
        for k in range(2):
            sp.dma_start(XS[:, k, :], io["xT"][k]).then_inc(S(f"x_in{k}"), 16)

        def kv(i, more_x):
            for par in range(2):
                n = 2 * i + par
                weights(SLOT0["kv"] + par + 2, par, i)
                if more_x:
                    sp.wait_ge(S("x_lo"), n + 1)
                    sp.wait_ge(S("x_acc"), n + 1)
                    sp.dma_start(XS[:, par, :], tile_of(io["xT"], n + 2)).then_inc(S(f"x_in{par}"), 16)
                sp.wait_ge(evac, n + 1)
                sp.dma_start(tile_of(KV_d, n), KVS[:, par, :]).then_inc(S(f"kv_stored{par}"), 16)

        with loop(nc.sync, 3) as i:
            kv(i, True)
        with nc.sync.Fori(3, 8) as i:
            kv(i, False)
        for j in range(4):
            weights(SLOT0["u"] + j + 2, j % 2)
            sp.wait_ge(evac, RES0["u"] + NB * (j + 1))
            sp.dma_start(U_d[j * P:(j + 1) * P], UB[:, j % 2]).then_inc(S(f"u_stored{j % 2}"), 16)
        with loop(nc.sync, 6) as i:
            for par in range(2):
                weights(SLOT0["conv"] + par + 2, par, i)
        for j in range(4):
            weights(SLOT0["co"] + j + 2, j % 2)
            for e in range(2):
                sp.wait_ge(evac, RES0["co"] + 6 * j + 3 * (e + 1))
                sp.dma_start(CO_d[2 * j + e], COS[:, e, :]).then_inc(S(f"co_stored{e}"), 16)

        for e in range(2):
            sp.wait_ge(S(f"co_stored{e}"), 64)
        sp.wait_ge(S("tables_made"), 32)
        for par in range(2):
            sp.wait_ge(S(f"tables_stored{par}"), 2 * 4 * 32)
        sp.wait_ge(S("bb_stored"), 32)
        u_rows = U_d.rearrange("(g p) s c -> p s g c", p=GP)
        for s in range(C):
            sp.dma_start(U[GP * s:GP * (s + 1)], u_rows[:, s]).then_inc(S("u_in"), 16)

        def s5a_loads(it, par):
            g = bass.ds(2 * it, 2)
            sem_in = S(f"s5a_in{par}")
            sp.dma_start(VN[:, par], V_d[:, g, :, :].rearrange("p g d c -> p (g d) c")).then_inc(sem_in, 16)
            wk = WK[:, par].rearrange("p (g d) c -> p g d c", d=2)
            sp.dma_start(wk[:, :, 0], W_d[:, g, 0, 0:P]).then_inc(sem_in, 16)
            sp.dma_start(wk[:, :, 1], W_d[:, g, 1, GP:GP + P]).then_inc(sem_in, 16)
            bb = BBL[:, par].rearrange("p (g d) c -> p g d c", d=2)
            for d in range(2):
                sp.dma_start(bb[:, :, d], BB_d[d, :, g, :]).then_inc(sem_in, 16)

        def s5a(i, last=False):
            for par in range(2):
                it = 2 * i + par
                if not (last and par):
                    sp.wait_ge(S("states_bwd"), it)
                    s5a_loads(it + 1, 1 - par)
                sp.wait_ge(S("lags_staged"), it + 1)
                sp.dma_start(L_d[:, bass.ds(2 * it, 2), :], LL[0:GP, par].rearrange("p a b -> p a b")
                             ).then_inc(S(f"lags_stored{par}"), 16)

        s5a_loads(0, 0)
        with loop(nc.sync, 7) as i:
            s5a(i)
        s5a(7, last=True)
        for par in range(2):
            sp.wait_ge(S(f"lags_stored{par}"), 8 * 16)
        for s in range(C):
            sp.dma_start(M_d[GP * s:GP * (s + 1)],
                         L_d[:, :, (C - 1 - s) * GP:(C - 1 - s) * GP + P]).then_inc(S("m_stored"), 16)

        with loop(nc.sync, 8) as i:
            for par in range(2):
                weights(SLOT0["gate"] + par + 2, par, i)
                sp.wait_ge(S("gate_made"), 2 * NB * i + NB * (par + 1))
                sp.dma_start(tile_of(G_d, 2 * i + par), GS[:, par, :]).then_inc(S(f"gate_stored{par}"), 16)

        sp.wait_ge(S("m_stored"), 128)
        for par in range(2):
            sp.wait_ge(S(f"gate_stored{par}"), 128)

        def s5b_loads(it, par):
            g = bass.ds(2 * it, 2)
            wo = WO[:, par].rearrange("p (g d) c -> p g d c", d=2)
            sp.dma_start(wo[:, :, 0], W_d[:, g, 0, GP:GP + P]).then_inc(S(f"s5b_in{par}"), 16)
            sp.dma_start(wo[:, :, 1], W_d[:, g, 1, 0:P]).then_inc(S(f"s5b_in{par}"), 16)
            sp.dma_start(ML[:, par], M_d[:, g, :]).then_inc(S(f"s5b_in{par}"), 16)

        def s5b(i, last=False):
            for par in range(2):
                it = 2 * i + par
                if not (last and par):
                    sp.wait_ge(S("s5_out"), it)
                    s5b_loads(it + 1, 1 - par)
                sp.wait_ge(S("y_made"), it + 1)
                sp.dma_start(Y_d[:, bass.ds(2 * it, 2), :], YS[:, par, :].rearrange("p (g c) -> p g c", g=2)
                             ).then_inc(S(f"y_stored{par}"), 16)

        s5b_loads(0, 0)
        with loop(nc.sync, 7) as i:
            s5b(i)
        s5b(7, last=True)
        for par in range(2):
            sp.wait_ge(S(f"y_stored{par}"), 128)
        y_rows = Y_d.rearrange("(t p) g c -> g p t c", p=GP)
        for k in range(HT):
            if k >= 2:
                sp.wait_ge(S("y_lo"), k - 1)
            for g in range(P // GP):
                sp.dma_start(YL[GP * g:GP * (g + 1), k % 2], y_rows[8 * k + g]).then_inc(S(f"y_in{k % 2}"), 16)

        sp.wait_ge(S("y_lo"), HT)

        def glu_loads(j):
            b = j % 2
            if j >= 2:
                sp.wait_ge(S("merged_lo"), NB * (j - 1))
            for dst, src in ((COL, CO_d[j]), (G2L, G_d[KT + j]), (G1L, G_d[j])):
                sp.dma_start(dst[:, b], src).then_inc(S(f"glu_in{b}"), 16)

        glu_loads(0)
        for j in range(KT):
            weights(SLOT0["glu"] + j + 2, j % 2)
            if j + 1 < KT:
                glu_loads(j + 1)

        sp.wait_ge(S("merged_lo"), NB * KT)
        for k in range(2):
            sp.dma_start(XR[:, k, :], io["xT"][k]).then_inc(S(f"xr_in{k}"), 16)

        def wo(i, more_x):
            for par in range(2):
                weights(SLOT0["wo"] + par + 2, par, i)
                if more_x:
                    sp.wait_ge(evac, RES0["wo"] + NB * (par + 1) + 2 * NB * i)
                    sp.dma_start(XR[:, par, :], tile_of(io["xT"], 2 * i + par + 2)).then_inc(S(f"xr_in{par}"), 16)

        with loop(nc.sync, 3) as i:
            wo(i, True)
        wo(3, False)
        with loop(nc.sync, 4) as i:
            for par in range(2):
                weights(SLOT0["q"] + par + 2, par, i)
                sp.wait_ge(evac, RES0["q"] + NB * (par + 1) + 2 * NB * i)
                sp.dma_start(tile_of(Q_d, 2 * i + par), QS[:, par, :]).then_inc(S(f"q_stored{par}"), 16)

        for par in range(2):
            sp.wait_ge(S(f"q_stored{par}"), 64)
            sp.wait_ge(S(f"kv_stored{par}"), 128)
        for n in range(HEADS * NB):
            h, b = n // NB, n % NB
            m, par = b * BLK // T_PROMPT, n % 2
            if n >= 2:
                sp.wait_ge(S("att_out"), 2 * (n - 1))
            sem_in = S(f"att_in{par}")
            sp.dma_start(QL[:, par], Q_d[2 * h:2 * h + 2, :, blk(b)].rearrange("e p t -> p e t")).then_inc(sem_in, 16)
            sp.dma_start(KL[:, par], K_d[2 * h:2 * h + 2, :, m * NMEM:(m + 1) * NMEM].rearrange("e p m -> p e m")
                         ).then_inc(sem_in, 16)
            sp.dma_start(VL[:, par], VV_d[2 * h:2 * h + 2, :, 2 * m:2 * m + 2, :].rearrange("e p m d -> p e m d")
                         ).then_inc(sem_in, 16)
        with loop(nc.sync, 4) as i:
            for par in range(2):
                weights(SLOT0["xo"] + par + 2, par, i)
        with loop(nc.sync, (NSLOT - 2 - SLOT0["ffn"]) // 2) as i:
            for par in range(2):
                weights(SLOT0["ffn"] + par + 2, par, i)
        for k in range(KT):
            sp.wait_ge(S("y_out"), k + 1)
            sp.dma_start(io["yT"][k], YO[:, k % 2, :]).then_inc(S(f"out_stored{k % 2}"), 16)
        for par in range(2):
            sp.wait_ge(S(f"out_stored{par}"), 16 * KT // 2)

    @block.gpsimd
    def _(pool):
        step = Count(S("pool_step"))

        def then(ins):
            step.up(ins)
            pool.wait_ge(step.sem, step.n)

        def tt(out, a, b, op):
            then(nc.gpsimd.tensor_tensor(out, a, b, op))

        pool.wait_ge(S("consts_in"), 8 * 16)
        pool.wait_ge(S("params_made"), 1)
        pool.wait_ge(S("rms"), NB)
        AR, AI, CR, CI, CIS = (PA[:, j, :] for j in (3, 4, 5, 6, 7))
        T1, T2 = TX[:, 0:GD], TX[:, GD:2 * GD]
        plus, minus = sgn[:, 0:1], sgn[:, 1:2]
        step.up(nc.gpsimd.memset(PR[:, 0, :], 1.0))
        then(nc.gpsimd.memset(PI[:, 0, :], 0.0))
        for k in range(1, NPOW):
            tt(T1, PR[:, k - 1, :], AR, ALU.mult)
            tt(T2, PI[:, k - 1, :], AI, ALU.mult)
            tt(PR[:, k, :], T1, T2, ALU.subtract)
            tt(T1, PR[:, k - 1, :], AI, ALU.mult)
            tt(T2, PI[:, k - 1, :], AR, ALU.mult)
            tt(PI[:, k, :], T1, T2, ALU.add)
        for out, src, n, sign, down in ((PVR, PR, C, 1.0, 0), (PVI, PI, C, plus, 0),
                                        (PWR, PR, NPOW, minus, 1), (PWI, PI, NPOW, -1.0, 1)):
            for d in range(2):
                a = src[:, 0:n, d * GROUPS:(d + 1) * GROUPS]
                then(nc.gpsimd.tensor_scalar(out[:, 0:n, d * GROUPS:(d + 1) * GROUPS],
                                             a[:, ::-1, :] if d == down else a, sign, None, ALU.mult))
        then(nc.gpsimd.tensor_scalar(LR[:], PR[:, C, :], 1.0, None, ALU.mult))
        then(nc.gpsimd.tensor_scalar(LI[:], PI[:, C, :], minus, None, ALU.mult))
        then(nc.gpsimd.tensor_scalar(CIS, CI, plus, None, ALU.mult))

        for d in range(2):
            if d:
                pool.wait_ge(S("bb_stored"), 16)
            for dst, src in ((BX, "BX"), (BY, "BY"), (CX, "CX"), (CY, "CY")):
                pool.dma_start(dst[:], io[src][d]).then_inc(S("bc_in"), 16)
            pool.wait_ge(S("bc_in"), 64 * (d + 1))
            cr, ci = (a[:, d * GROUPS:(d + 1) * GROUPS].unsqueeze(2).to_broadcast([P, GROUPS, GP])
                      for a in (CR, CIS))
            bt = TX[:, 0:GROUPS * GP].rearrange("p (g q) -> p g q", q=GP)
            tt(bt, BY[:], ci, ALU.mult)
            tt(BBX[:], BX[:], cr, ALU.mult)
            tt(BBX[:], BBX[:], bt, ALU.add)
            tt(bt, BX[:], ci, ALU.mult)
            tt(BBY[:], BY[:], cr, ALU.mult)
            tt(BBY[:], BBY[:], bt, ALU.subtract)
            pool.dma_start(BB_d[d], BBX[:]).then_inc(S("bb_stored"), 16)

            with loop(nc.gpsimd, 4) as i:
                step.enter(i, 8)
                for par in range(2):
                    g0 = 8 * i + 4 * par
                    made = 16 * d + 4 * i + 2 * par

                    def powers(a, n):
                        a = a[:, 0:n, bass.ds(d * GROUPS + g0, 4)]
                        return a.rearrange("p k g -> p g k").unsqueeze(3).to_broadcast([P, 4, n, GP])

                    def values(a, n):
                        return a[:, bass.ds(g0, 4), :].unsqueeze(2).to_broadcast([P, 4, n, GP])

                    def cut(a, n):
                        return a[:, 0:4 * n * GP].rearrange("p (g k q) -> p g k q", g=4, q=GP)

                    v, w = cut(TB[:, par, :], C), cut(TC[:, par, :], NPOW)
                    pool.wait_ge(S(f"tables_stored{par}"), 32 * (4 * d + i))
                    tt(v, values(BBX, C), powers(PVR, C), ALU.mult)
                    tt(cut(TX, C), values(BBY, C), powers(PVI, C), ALU.mult)
                    nc.gpsimd.tensor_tensor(v, v, cut(TX, C), ALU.add).then_inc(S("tables_made"), 1)
                    pool.wait_ge(S("tables_made"), made + 1)
                    pool.dma_start(V_d[:, bass.ds(g0, 4), d, :],
                                   TB[:, par, 0:4 * P].rearrange("p (g c) -> p g c", g=4)
                                   ).then_inc(S(f"tables_stored{par}"), 16)
                    tt(w, values(CX, NPOW), powers(PWR, NPOW), ALU.mult)
                    tt(cut(TX, NPOW), values(CY, NPOW), powers(PWI, NPOW), ALU.mult)
                    nc.gpsimd.tensor_tensor(w, w, cut(TX, NPOW), ALU.add).then_inc(S("tables_made"), 1)
                    pool.wait_ge(S("tables_made"), made + 2)
                    pool.dma_start(W_d[:, bass.ds(g0, 4), d, :],
                                   TC[:, par, :].rearrange("p (g c) -> p g c", g=4)
                                   ).then_inc(S(f"tables_stored{par}"), 16)
                step.leave(4)
        with loop(nc.gpsimd, 4) as i:
            for b in range(2):
                pool.wait_ge(S(f"glu_in{b}"), 48 * (i + 1))
                nc.gpsimd.tensor_tensor(G2L[:, b, :], G2L[:, b, :], COL[:, b, :], ALU.mult
                                        ).then_inc(S("gated_conv"), 1)

    @block.tensor
    def _(pe):
        def product(out, w, x, first, last):
            pe_mm = nc.tensor.matmul
            pe_mm(out, w[1], x[0], start=first, stop=False)
            pe_mm(out, w[0], x[1], start=False, stop=False)
            return pe_mm(out, w[0], x[0], start=False, stop=last)

        def wts(par, c):
            return WHI[:, par, c * P:(c + 1) * P], WLO[:, par, c * P:(c + 1) * P]

        def xin(k, b):
            return XN[:, 0, k, blk(b)], XN[:, 1, k, blk(b)]

        def dense(q, i, each, par, tiles, ins):
            for r, (cols, b) in enumerate((t, b) for t in tiles for b in range(NB)):
                pe.wait_ge(evac, q + r - RING + 1 + each * i)
                for k, c in enumerate(cols):
                    last = product(bank(q + r)[:], wts(par, c), ins(k, b), k == 0, k == len(cols) - 1)
                last.then_inc(res, 1)

        def slots(name, times, tiles, ins, first=0):
            per = NB * len(tiles)
            with nc.tensor.Fori(first, times) as i:
                for par in range(2):
                    pe.wait_ge(wlo, SLOT0[name] + par + 1 + 2 * i)
                    dense(RES0[name] + per * par, i, 2 * per, par, tiles, ins)

        K8 = [list(range(KT))]
        K4 = [list(range(HT)), list(range(HT, 2 * HT))]

        def first_pair(name, ready, norm):
            q = RES0[name]
            pe.wait_ge(wlo, SLOT0[name] + 1)
            pe.wait_ge(evac, q)
            for k in range(KT):
                if ready:
                    pe.wait_ge(*ready(k))
                for b in range(NB):
                    last = product(bank(q + b)[:], wts(0, k), xin(k, b), k == 0, k == KT - 1)
                    if k == KT - 1:
                        last.then_inc(res, 1)
            if norm is not None:
                sums(norm, ACC2)
            pe.wait_ge(wlo, SLOT0[name] + 2)
            dense(q + NB, 0, 0, 1, K8, xin)

        def sums(norm, acc):
            if norm:
                pe.wait_ge(S("squares_added"), KT * norm)
            else:
                pe.wait_ge(S("x_acc"), KT)
            for b in range(NB):
                if b == 2:
                    pe.wait_ge(S("root"), NB * norm + 1)
                nc.tensor.matmul(PS[6 + b % 2][:], ones[:], acc[:, blk(b)], start=True, stop=True
                                 ).then_inc(S("sums"), 1)

        pe.wait_ge(S("consts_in"), 8 * 16)

        def key(i, par):
            n = 2 * i + par
            pe.wait_ge(wlo, n + 1)
            if not isinstance(i, int) or i:
                pe.wait_ge(evac, n - 1)
            for k in range(KT):
                last = product(PS[par][:], wts(par, k), (MN[:, 0, k, :], MN[:, 1, k, :]), k == 0, k == KT - 1)
            last.then_inc(res, 1)

        def value(i, par):
            n = 2 * i + par
            pe.wait_ge(wlo, n + 1)
            pe.wait_ge(evac, n - 1)
            for m in range(M2 // P):
                for k in range(KT):
                    rows = slice(m * P, (m + 1) * P)
                    last = product(PS[par][:, rows], (MN[:, 0, k, rows], MN[:, 1, k, rows]), wts(par, k),
                                   k == 0, k == KT - 1)
            last.then_inc(res, 1)

        pe.wait_ge(S("mem_lo"), KT)
        key(0, 0)
        pe.wait_ge(S("mem_acc"), KT)
        nc.tensor.matmul(PS[6][:], ones[:], MACC[:], start=True, stop=True).then_inc(S("mem_sums"), 1)
        for m in range(M2 // P):
            last = nc.tensor.matmul(PS[7][:, m:m + 1], MACC[:, m * P:(m + 1) * P], ones[:, 0:1],
                                    start=True, stop=True)
        last.then_inc(S("mem_sums"), 1)
        key(0, 1)
        with nc.tensor.Fori(1, 4) as i:
            key(i, 0)
            key(i, 1)
        pe.wait_ge(S("mem_root"), 2)
        sums(0, ACC)
        with nc.tensor.Fori(4, 8) as i:
            value(i, 0)
            value(i, 1)

        pe.wait_ge(evac, RES0["u"])
        first_pair("u", lambda k: (S("x_lo"), k + 1), None)
        slots("u", 2, K8, xin, first=1)
        slots("conv", 6, K8, xin)
        pe.wait_ge(S("cin_lo"), NB * HT)
        slots("co", 2, K4, lambda k, b: (CIN[:, k, 0, blk(b)], CIN[:, k, 1, blk(b)]))

        pe.wait_ge(evac, RES0["gate"])
        pe.wait_ge(S("u_in"), 128)

        def s5a(i):
            for par in range(2):
                it = 2 * i + par
                pe.wait_ge(S(f"s5a_in{par}"), 80 * (i + 1))
                for j in range(4):
                    last = nc.tensor.transpose(PS[par][:, j * P:(j + 1) * P], VN[:, par, j, :], ident[:])
                last.then_inc(S("v_turned"), 1)
                if not isinstance(i, int):
                    pe.wait_ge(S("lags_staged"), it - 1)
                for g in range(2):
                    out = PS[6 + par][0:GP, g * LAGS * GP:(g + 1) * LAGS * GP]
                    (bf, bb), (kf, kb) = ((a[:, par, 2 * g], a[:, par, 2 * g + 1]) for a in (BBL, WK))
                    z = (C - 1) * GP
                    nc.tensor.matmul(out[:, z:z + GP], bb, kb[:, z:], start=True, stop=False)
                    nc.tensor.matmul(out[:, z:z + GP], bf, kf[:, 0:GP], start=False, stop=True)
                    nc.tensor.matmul(out[:, 0:z], bb, kb[:, 0:z], start=True, stop=True)
                    last = nc.tensor.matmul(out[:, z + GP:], bf, kf[:, GP:], start=True, stop=True)
                last.then_inc(S("lags"), 1)
                pe.wait_ge(S("v_staged"), it + 1)
                if not isinstance(i, int):
                    pe.wait_ge(S("h_fwd"), 2 * (it - 1))
                    pe.wait_ge(S("h_bwd"), 2 * (it - 1))
                for g in range(2):
                    u = one(U, 2 * it + g)
                    last = nc.tensor.matmul(PS[2 + par][:, g * NC:(g + 1) * NC], VT[:, par, 2 * g * P:(2 * g + 1) * P],
                                            u, start=True, stop=True)
                last.then_inc(S("states_fwd"), 1)
                for g in range(2):
                    u = one(U, 2 * it + g)
                    out = PS[4 + par][:, g * NC:(g + 1) * NC]
                    w = VT[:, par, (2 * g + 1) * P:(2 * g + 2) * P]
                    last = nc.tensor.matmul(out, w, u, start=True, stop=True)
                last.then_inc(S("states_bwd"), 1)

        s5a(0)
        with nc.tensor.Fori(1, 8) as i:
            s5a(i)

        pe.wait_ge(S("v_staged"), 16)
        pe.wait_ge(S("h_fwd"), 32)
        pe.wait_ge(S("h_bwd"), 32)
        slots("gate", 8, K8, xin)

        pe.wait_ge(evac, RES0["glu"])
        pe.wait_ge(S("scan"), SCAN_STEPS * 5)

        def s5b(i):
            for par in range(2):
                it = 2 * i + par
                pe.wait_ge(S(f"s5b_in{par}"), 48 * (i + 1))
                if not isinstance(i, int):
                    pe.wait_ge(S("y_made"), it - 1)
                for g in range(2):
                    out = PS[par][:, g * NC:(g + 1) * NC]
                    u = one(U, 2 * it + g)
                    for c0, n, slot in ((0, NCP, 0), (NCP, NCS, SLOT_S)):
                        o = out[:, c0:c0 + n]
                        nc.tensor.matmul(o, ML[:, par, g, :], u[:, c0:c0 + n], start=True, stop=False)
                        for d in (1, 0):
                            h = H[:, slot:slot + n, bass.ds(d * GROUPS + 2 * it + g, 1)].rearrange("p s o -> p (s o)")
                            last = nc.tensor.matmul(o[:, ::-1] if d else o,
                                                    WO[:, par, 2 * g + d, :], h, start=False, stop=d == 0)
                last.then_inc(S("s5_out"), 1)

        s5b(0)
        with nc.tensor.Fori(1, 8) as i:
            s5b(i)

        pe.wait_ge(S("y_made"), 16)
        pe.wait_ge(S("y_lo"), HT)
        slots("glu", 4, K4, lambda k, b: (YHL[:, 0, k, blk(b)], YHL[:, 1, k, blk(b)]))
        pe.wait_ge(S("merged_lo"), NB * KT)
        slots("wo", 4, K8, xin)
        first_pair("q", lambda k: (S("hn_lo"), k + 1), 1)
        slots("q", 4, K8, xin, first=1)

        pe.wait_ge(evac, RES0["xo"])

        def scores(i, u):
            par, idx = u % 2, 2 * NB * i + u
            pe.wait_ge(S(f"att_in{par}"), 48 * (u // 2 + 1) + 48 * NB * i)
            if not (isinstance(i, int) and i == 0 and u < 2):
                pe.wait_ge(S("exps"), 4 * (idx - 1))
            for lt in range(4):
                out = PS[2 * par + lt // 2][:, (lt % 2) * NMEM:(lt % 2 + 1) * NMEM]
                for k in range(2):
                    last = nc.tensor.matmul(out, QL[:, par, k, lt * P:(lt + 1) * P], KL[:, par, k, :],
                                            start=k == 0, stop=k == 1)
                if lt % 2:
                    last.then_inc(S("scores"), 1)

        def weighted(i, u):
            par, idx = u % 2, 2 * NB * i + u
            pe.wait_ge(S("probs"), 4 * (idx + 1))
            for m in range(2):
                if not (isinstance(i, int) and i == 0 and u == 0):
                    pe.wait_ge(S("pt_staged"), 2 * idx)
                for lt in range(4):
                    last = nc.tensor.transpose(PS[4 + m][:, lt * P:(lt + 1) * P],
                                               PB[:, par, lt, m * P:(m + 1) * P], ident[:])
                last.then_inc(S("p_turned"), 1)
            pe.wait_ge(S("pt_staged"), 2 * (idx + 1))
            if not (isinstance(i, int) and i == 0 and u == 0):
                pe.wait_ge(S("o_lo"), 2 * idx)
            for e in range(2):
                for m in range(2):
                    last = nc.tensor.matmul(PS[6 + e][:], VL[:, par, e, m, :], PT[:, par, m, :],
                                            start=m == 0, stop=m == 1)
                last.then_inc(S("att_out"), 1)

        scores(0, 0)
        for u in range(1, 2 * NB):
            scores(0, u)
            weighted(0, u - 1)
        scores(1, 0)
        weighted(0, 2 * NB - 1)
        for u in range(1, 2 * NB):
            scores(1, u)
            weighted(1, u - 1)
        weighted(1, 2 * NB - 1)

        pe.wait_ge(S("o_lo"), 2 * HEADS * NB)
        pe.wait_ge(S("exps"), 4 * HEADS * NB)
        slots("xo", 4, K8, xin)

        def down(c, part, each_q):
            par = part
            q = RES0["ffn"] + 4 * NB + part * 4 * NB
            pe.wait_ge(wlo, SLOT0["ffn"] + 5 + part + CH_SLOTS * c)
            for e0 in (0, 2):
                for k in range(2):
                    for r, (e, b) in enumerate((e, b) for e in (e0, e0 + 1) for b in range(NB)):
                        n = q + 3 * e0 + r
                        if k == 0:
                            pe.wait_ge(evac, n - RING + 1 + CH_RES * c)
                        pe.wait_ge(S("act_lo"), NB * k + b + 1 + 2 * NB * c)
                        last = product(bank(n)[:], wts(par, 2 * e + k), (AF[:, 0, k, blk(b)], AF[:, 1, k, blk(b)]),
                                       k == 0, k == 1)
                        if k == 1:
                            last.then_inc(res, 1)

        def chunk(c):
            for f in range(4):
                if isinstance(c, int) and c == 0 and f < 2:
                    continue
                pe.wait_ge(wlo, SLOT0["ffn"] + f + 1 + CH_SLOTS * c)
                dense(RES0["ffn"] + NB * f, c, CH_RES, f % 2, K8, xin)
            down(c, 0, None)
            down(c, 1, None)

        first_pair("ffn", lambda k: (S("hn_lo"), KT + k + 1), 2)
        chunk(0)
        with nc.tensor.Fori(1, CHUNKS) as c:
            chunk(c)
        sums(3, ACC2)

    @block.scalar
    def _(act):
        def copy(out, in_, scale=1.0):
            return nc.scalar.activation(out, in_, ACT.Copy, scale=scale)

        def hi(m, q, i=0, each=0, di=1):
            par = m % 2
            act.wait_ge(raw[par], 16 * (m // 2 + 1) + 16 * di * i)
            act.wait_ge(res, q + each * i)
            copy(WHI[:, par, :], WR[:, par, :]).then_inc(whi, 1)

        def apart():
            act.wait_ge(whi, 1)

        def root(out, in_, n):
            return nc.scalar.activation(out, in_, ACT.Sqrt, scale=1.0 / D, bias=epsc[0:n, 0:1])

        def roots(norm):
            for b in range(NB):
                act.wait_ge(S("sums"), NB * norm + b + 1)
                root(RB[:, blk(b)], PS[6 + b % 2][:], P).then_inc(S("root"), 1)

        act.wait_ge(S("angles"), 2)
        nc.scalar.activation(PA[:, 9, :], PA[:, 9, :], ACT.Sin).then_inc(S("sines"), 1)
        nc.scalar.activation(PA[:, 10, :], PA[:, 10, :], ACT.Sin).then_inc(S("sines"), 1)

        act.wait_ge(S("consts_in"), 8 * 16)
        for k in range(KT):
            if k % 4 == 0:
                act.wait_ge(S(f"mem_in{k // 4}"), 16)
            copy(MN[:, 0, k, :], MEM[:, k, :], gains[:, 1, k:k + 1]).then_inc(S("mem_hi"), 1)
            if k >= 2:
                act.wait_ge(S("mem_acc"), k - 1)
            nc.scalar.activation(MSQ[:, k % 2, :], MEM[:, k, :], ACT.Square).then_inc(S("mem_sq"), 1)
        act.wait_ge(raw[0], 16)
        copy(WHI[:, 0, :], WR[:, 0, :]).then_inc(whi, 1)

        def x_tile(i, par):
            n = 2 * i + par
            act.wait_ge(S(f"x_in{par}"), 16 * (i + 1))
            apart()
            copy(one(XN[:, 0], n), XS[:, par, :], gains[:, 0, bass.ds(n, 1)]).then_inc(S("x_hi"), 1)
            if not isinstance(i, int):
                act.wait_ge(S("x_acc"), n - 1)
            nc.scalar.activation(SQ[:, par, :], XS[:, par, :], ACT.Square).then_inc(S("x_sq"), 1)

        act.wait_ge(raw[1], 16)
        copy(WHI[:, 1, :], WR[:, 1, :]).then_inc(whi, 1)
        act.wait_ge(S("mem_sums"), 1)
        root(RM[:], PS[6][:], P).then_inc(S("mem_root"), 1)
        act.wait_ge(S("mem_sums"), 2)
        root(rcol[:], PS[7][:, 0:4], P).then_inc(S("mem_root"), 1)
        x_tile(0, 0)
        hi(2, 1)
        x_tile(0, 1)
        with nc.scalar.Fori(1, 4) as i:
            hi(1, 0, i, 2)
            x_tile(i, 0)
            hi(2, 1, i, 2)
            x_tile(i, 1)
        roots(0)
        with nc.scalar.Fori(4, 8) as i:
            hi(1, 0, i, 2)
            hi(2, 1, i, 2)

        def hi_pair(name, i, each, par):
            hi(SLOT0[name] + par + 1, RES0[name] + each * par, i, 2 * each)

        for j in range(4):
            hi(SLOT0["u"] + j + 1, RES0["u"] + NB * j)

        with loop(nc.scalar, 2) as i:
            for par in range(2):
                act.wait_ge(S(f"kv_stored{par}"), 128 * i)
            act.wait_ge(S("tables_made"), 32 * i)
            for jj in range(2):
                j = 2 * i + jj
                for part in range(3):
                    m = 3 * jj + part
                    hi(SLOT0["conv"] + m + 1, RES0["conv"] + NB * m, i, 6 * NB, 3)
                    if part == 1:
                        act.wait_ge(S("z"), NB * (jj + 1) + 2 * NB * i)
                        apart()
                        copy(XC[:], Z[:, 1:T + 2], convw[:, bass.ds(j, 1), 1:2].rearrange("p o a -> p (o a)")
                             ).then_inc(S("tap1"), 1)
                    if part == 2:
                        for b in range(NB):
                            n = NB * jj + b
                            act.wait_ge(S("cin"), n + 1 + 2 * NB * i)
                            apart()
                            copy(one(CIN, j)[:, 0, blk(b)], TT[:, n % 2, :]).then_inc(S("cin_hi"), 1)
        with loop(nc.scalar, 2) as i:
            for par in range(2):
                hi_pair("co", i, 6, par)

        def states_away(it, src, d, signal):
            dst = H[:, :, bass.ds(d * GROUPS + 2 * it, 2)].rearrange("p s g -> p g s")
            src = src[:, 0:2 * NC].rearrange("p (g c) -> p g c", g=2)
            for lo, n, c in ((1, NCP, 0), (SLOT_S + 1, NCS, NCP)):
                copy(dst[:, :, lo:lo + n], src[:, :, c:c + n]).then_inc(signal, 1)

        def s5a(i):
            for par in range(2):
                it = 2 * i + par
                act.wait_ge(S("v_turned"), it + 1)
                if not isinstance(i, int):
                    act.wait_ge(S("states_bwd"), it - 1)
                copy(VT[:, par, :], PS[par][:]).then_inc(S("v_staged"), 1)
                act.wait_ge(S("states_fwd"), it + 1)
                apart()
                states_away(it, PS[2 + par], 0, S("h_fwd"))

        s5a(0)
        with nc.scalar.Fori(1, 8) as i:
            s5a(i)

        def gate(i):
            for par in range(2):
                hi_pair("gate", i, NB, par)
                act.wait_ge(S(f"gate_stored{par}"), 16 * i)
                copy(bcol[:, par:par + 1], bgate[:, bass.ds(2 * i + par, 1)]).then_inc(S("bias"), 1)
                act.wait_ge(S("bias"), 2 * i + par + 1)
                for b in range(NB):
                    n = NB * par + b
                    act.wait_ge(evac, RES0["gate"] + n + 1 + 2 * NB * i)
                    nc.scalar.activation(GS[:, par, blk(b)], TG[:, n % 2, :], ACT.Sigmoid, bias=bcol[:, par:par + 1]
                                         ).then_inc(S("gate_made"), 1)

        with loop(nc.scalar, 8) as i:
            gate(i)

        def s5b(i):
            for par in range(2):
                it = 2 * i + par
                act.wait_ge(S("s5_out"), it + 1)
                act.wait_ge(S(f"y_stored{par}"), 16 * i)
                nc.scalar.activation(YS[:, par, :], PS[par][:, 0:2 * NC], ACT.Gelu_apprx_tanh
                                     ).then_inc(S("y_made"), 1)

        with loop(nc.scalar, 8) as i:
            s5b(i)
        for k in range(HT):
            act.wait_ge(S(f"y_in{k % 2}"), 128 * (k // 2 + 1))
            copy(YHL[:, 0, k].rearrange("p (c t) -> p c t", t=C), YL[:, k % 2].rearrange("p t c -> p c t")
                 ).then_inc(S("y_hi"), 1)

        with loop(nc.scalar, 4) as i:
            for par in range(2):
                j = 2 * i + par
                hi_pair("glu", i, 6, par)
                for b in range(NB):
                    act.wait_ge(evac, RES0["glu"] + 6 * par + b + 1 + 12 * i)
                    nc.scalar.activation(SB[:, blk(b)], SB[:, blk(b)], ACT.Sigmoid).then_inc(S("glu_gate"), 1)
                for b in range(NB):
                    act.wait_ge(S("merged"), NB * par + b + 1 + 2 * NB * i)
                    apart()
                    copy(one(XN[:, 0], j)[:, blk(b)], SB[:, blk(b)]).then_inc(S("merged_hi"), 1)

        def residual(name, norm):
            def pair(i):
                for par in range(2):
                    j = 2 * i + par
                    hi_pair(name, i, NB, par)
                    act.wait_ge(evac, RES0[name] + NB * (par + 1) + 2 * NB * i)
                    if not isinstance(i, int):
                        act.wait_ge(S("squares_added"), KT * (norm - 1) + j - 1)
                        apart()
                    nc.scalar.activation(SQ2[:, par, :], one(HR, j), ACT.Square).then_inc(S("squares"), 1)
            pair(0)
            with nc.scalar.Fori(1, 4) as i:
                pair(i)

        def split_residual(norm):
            gain = gains[:, norm + 1, :]
            q = RES0["q"] if norm == 1 else RES0["ffn"]
            act.wait_ge(res, q)
            for k in range(KT):
                copy(XN[:, 0, k, :], HR[:, k, :], gain[:, k:k + 1]).then_inc(S("hn_hi"), 1)
            roots(norm)

        residual("wo", 1)
        split_residual(1)
        with loop(nc.scalar, 4) as i:
            for par in range(2):
                hi_pair("q", i, NB, par)

        def softmax(i, u):
            par, idx = u % 2, 2 * NB * i + u
            for lt in range(4):
                if lt % 2 == 0:
                    act.wait_ge(S("maxima"), 2 * idx + lt // 2 + 1)
                nc.scalar.activation(PB[:, par, lt, :], PS[2 * par + lt // 2][:, (lt % 2) * NMEM:(lt % 2 + 1) * NMEM],
                                     ACT.Exp, scale=SCALE, bias=snm[:, par, lt:lt + 1],
                                     accum_out=ssm[:, par, lt:lt + 1]).then_inc(S("exps"), 1)

        def outputs(i, u):
            par, idx = u % 2, 2 * NB * i + u
            h, b = 2 * i + u // NB, u % NB
            act.wait_ge(S("p_turned"), 2 * idx + 2)
            if not (isinstance(i, int) and i == 0 and u < 2):
                act.wait_ge(S("att_out"), 2 * (idx - 1))
            copy(PT[:, par, 1, :], PS[5][:]).then_inc(S("pt_staged"), 1)
            for e in range(2):
                act.wait_ge(S("att_out"), 2 * idx + e + 1)
                copy(one(XN[:, 0], 2 * h + e)[:, blk(b)], PS[6 + e][:]).then_inc(S("o_hi"), 1)

        softmax(0, 0)
        for u in range(1, 2 * NB):
            softmax(0, u)
            outputs(0, u - 1)
        softmax(1, 0)
        outputs(0, 2 * NB - 1)
        for u in range(1, 2 * NB):
            softmax(1, u)
            outputs(1, u - 1)
        outputs(1, 2 * NB - 1)

        residual("xo", 2)
        split_residual(2)

        def chunk(c, final=False):
            for f in range(4):
                hi(SLOT0["ffn"] + f + 1, RES0["ffn"] + NB * f, c, CH_RES, 3)
                kk = f // 2
                for b in range(NB):
                    if f % 2 == 0:
                        act.wait_ge(evac, RES0["ffn"] + NB * f + b + 1 + CH_RES * c)
                        nc.scalar.activation(SG[:, blk(b)], TF[:, b % 2, :], ACT.Silu).then_inc(S("silu"), 1)
                    else:
                        act.wait_ge(S("act"), NB * kk + b + 1 + 2 * NB * c)
                        copy(AF[:, 0, kk, blk(b)], TF[:, (b + 1) % 2, :]).then_inc(S("act_hi"), 1)
            for part in range(2):
                if not (final and part):
                    hi(SLOT0["ffn"] + 5 + part, RES0["ffn"] + 4 * NB * (part + 1), c, CH_RES, 3)

        with nc.scalar.Fori(0, CHUNKS - 1) as c:
            chunk(c)
        chunk(CHUNKS - 1, final=True)
        q = RES0["ffn"] + CHUNKS * CH_RES - KT * NB
        for k in range(KT):
            act.wait_ge(evac, q + NB * (k + 1))
            if k:
                act.wait_ge(S("squares_added"), 2 * KT + k)
            nc.scalar.activation(SG[:], HR[:, k, :], ACT.Square).then_inc(S("squares"), 1)
        roots(3)

    @block.vector
    def _(dve):
        step = Count(S("vector_step"))

        def then(ins):
            step.up(ins)
            dve.wait_ge(step.sem, step.n)

        V = nc.vector

        def tt(out, a, b, op):
            then(V.tensor_tensor(out, a, b, op))

        def ts(out, a, s1, s2, op0, op1=None):
            then(V.tensor_scalar(out, a, s1, s2, op0, op1) if op1 is not None
                 else V.tensor_scalar(out, a, s1, None, op0))

        def lo(m, di_i=0):
            par = m % 2
            dve.wait_ge(whi, m + 1 + di_i)
            V.tensor_tensor(WLO[:, par, :], WR[:, par, :], WHI[:, par, :].bitcast(F32), ALU.subtract
                            ).then_inc(wlo, 1)

        def rest(out, full, part):
            return V.tensor_tensor(out, full, part.bitcast(F32), ALU.subtract)

        def reciprocals(norm):
            for b in range(NB):
                dve.wait_ge(S("root"), NB * norm + b + 1)
                V.reciprocal(RB[:, blk(b)], RB[:, blk(b)]).then_inc(S("rms"), 1)
            dve.wait_ge(S("rms"), NB * (norm + 1))

        A_RE, A_IM, DT, AR, AI, CR, CI, CIS, E, X9, X10, X11, X12, X13, X14, X15 = (PA[:, j, :] for j in range(16))

        def exp_to(out, x):
            ts(X12, x, 0.5, -87.0, ALU.mult, ALU.max)
            ts(X12, X12, 88.0, None, ALU.min)
            ts(X13, X12, LOG2E, ROUND + 127.0, ALU.mult, ALU.add)
            ts(X14, X13, -(ROUND + 127.0), None, ALU.add)
            then(V.scalar_tensor_tensor(out=X12, in0=X14, scalar=-LN2_HI, in1=X12, op0=ALU.mult, op1=ALU.add))
            then(V.scalar_tensor_tensor(out=X12, in0=X14, scalar=-LN2_LO, in1=X12, op0=ALU.mult, op1=ALU.add))
            ts(X13.bitcast(I32), X13.bitcast(I32), 23, None, ALU.logical_shift_left)
            terms = 9
            ts(X15, X12, 1.0 / math.factorial(terms), None, ALU.mult)
            for n in range(terms - 1, 0, -1):
                then(V.scalar_tensor_tensor(out=X15, in0=X15, scalar=1.0 / math.factorial(n), in1=X12,
                                            op0=ALU.add, op1=ALU.mult))
            then(V.scalar_tensor_tensor(out=X15, in0=X15, scalar=1.0, in1=X13, op0=ALU.add, op1=ALU.mult))
            tt(out, X15, X15, ALU.mult)

        dve.wait_ge(S("params_in"), 48)
        exp_to(DT, DT)
        tt(AR, A_RE, DT, ALU.mult)
        tt(AI, A_IM, DT, ALU.mult)
        ts(X11, AI, 1.0 / (2 * math.pi), ROUND, ALU.mult, ALU.add)
        ts(X11, X11, -ROUND, None, ALU.add)
        for part in TWO_PI:
            then(V.scalar_tensor_tensor(out=AI, in0=X11, scalar=-part, in1=AI, op0=ALU.mult, op1=ALU.add))
        ts(AI, AI, 3.1415925, -3.1415925, ALU.min, ALU.max)
        V.tensor_scalar(X9, AI, 1.0, None, ALU.mult).then_inc(S("angles"), 1)
        V.tensor_scalar(X10, AI, 0.5, None, ALU.mult).then_inc(S("angles"), 1)
        exp_to(E, AR)
        dve.wait_ge(S("sines"), 2)
        tt(X10, X10, X10, ALU.mult)
        ts(X10, X10, -2.0, 1.0, ALU.mult, ALU.add)
        tt(AR, E, X10, ALU.mult)
        tt(AI, E, X9, ALU.mult)
        ts(X11, AR, -1.0, None, ALU.add)
        tt(X12, A_RE, A_RE, ALU.mult)
        tt(X13, A_IM, A_IM, ALU.mult)
        tt(X12, X12, X13, ALU.add)
        then(V.reciprocal(X12, X12))
        tt(X13, X11, A_RE, ALU.mult)
        tt(X14, AI, A_IM, ALU.mult)
        tt(X13, X13, X14, ALU.add)
        tt(CR, X13, X12, ALU.mult)
        tt(X13, AI, A_RE, ALU.mult)
        tt(X14, X11, A_IM, ALU.mult)
        tt(X13, X13, X14, ALU.subtract)
        V.tensor_tensor(CI, X13, X12, ALU.mult).then_inc(S("params_made"), 1)

        V.memset(MACC[:], 0.0).then_inc(S("cleared"), 1)
        V.memset(ACC[:], 0.0).then_inc(S("cleared"), 1)
        dve.wait_ge(S("cleared"), 2)
        dve.wait_ge(S("consts_in"), 8 * 16)
        for k in range(KT):
            dve.wait_ge(S("mem_hi"), k + 1)
            V.scalar_tensor_tensor(out=MN[:, 1, k, :], in0=MEM[:, k, :], scalar=gains[:, 1, k:k + 1],
                                   in1=MN[:, 0, k, :].bitcast(F32), op0=ALU.mult, op1=ALU.subtract
                                   ).then_inc(S("mem_lo"), 1)
            if k:
                dve.wait_ge(S("mem_acc"), k)
            dve.wait_ge(S("mem_sq"), k + 1)
            V.tensor_tensor(MACC[:], MACC[:], MSQ[:, k % 2, :], ALU.add).then_inc(S("mem_acc"), 1)
        lo(0)
        lo(1)

        def kv(i, par, values):
            n = 2 * i + par
            dve.wait_ge(res, n + 1)
            dve.wait_ge(S(f"kv_stored{par}"), 16 * i)
            if values:
                V.tensor_tensor(KVS[:, par, :].rearrange("p (m d) -> p m d", d=P),
                                PS[par][:].rearrange("p (m d) -> p m d", d=P),
                                rcol[:].unsqueeze(2).to_broadcast([P, M2 // P, P]), ALU.mult).then_inc(evac, 1)
            else:
                V.tensor_tensor(KVS[:, par, :], PS[par][:], RM[:], ALU.mult).then_inc(evac, 1)

        def x_tile(i, par):
            n = 2 * i + par
            dve.wait_ge(S("x_hi"), n + 1)
            V.scalar_tensor_tensor(out=one(XN[:, 1], n), in0=XS[:, par, :], scalar=gains[:, 0, bass.ds(n, 1)],
                                   in1=one(XN[:, 0], n).bitcast(F32), op0=ALU.mult, op1=ALU.subtract
                                   ).then_inc(S("x_lo"), 1)
            dve.wait_ge(S("x_sq"), n + 1)
            dve.wait_ge(S("x_acc"), n)
            V.tensor_tensor(ACC[:], ACC[:], SQ[:, par, :], ALU.add).then_inc(S("x_acc"), 1)

        dve.wait_ge(S("mem_root"), 1)
        V.reciprocal(RM[:], RM[:]).then_inc(S("mem_rms"), 1)
        dve.wait_ge(S("mem_root"), 2)
        V.reciprocal(rcol[:], rcol[:]).then_inc(S("mem_rms"), 1)
        dve.wait_ge(S("mem_rms"), 2)
        x_tile(0, 0)
        kv(0, 0, False)
        lo(2)
        x_tile(0, 1)
        kv(0, 1, False)
        with V.Fori(1, 4) as i:
            lo(1, 2 * i)
            x_tile(i, 0)
            kv(i, 0, False)
            lo(2, 2 * i)
            x_tile(i, 1)
            kv(i, 1, False)
        reciprocals(0)
        with V.Fori(4, 8) as i:
            lo(1, 2 * i)
            kv(i, 0, True)
            lo(2, 2 * i)
            kv(i, 1, True)

        def take(q, i=0, each=0):
            dve.wait_ge(res, q + 1 + each * i)
            return bank(q)[:]

        for j in range(4):
            lo(SLOT0["u"] + j + 1)
            if j >= 2:
                dve.wait_ge(S(f"u_stored{j % 2}"), 16)
            for b in range(NB):
                src = take(RES0["u"] + NB * j + b)
                V.tensor_tensor(UB[:, j % 2, :, b * 64:(b + 1) * 64].rearrange("p s c -> p c s"),
                                src.rearrange("p (c s) -> p c s", s=C),
                                RB[:, blk(b)].rearrange("p (c s) -> p c s", s=C), ALU.mult).then_inc(evac, 1)

        for par in range(2):
            dve.wait_ge(S(f"u_stored{par}"), 32)
        for col in (0, T_PROMPT + 1, T + 2):
            step.up(V.memset(Z[:, col:col + 1], 0.0))
        dve.wait_ge(step.sem, step.n)
        with loop(V, 2) as i:
            step.enter(i, 2)
            for jj in range(2):
                j = 2 * i + jj
                q = RES0["conv"] + 9 * jj
                each = 6 * NB
                lo(SLOT0["conv"] + 3 * jj + 1, 6 * i)
                for b in range(NB):
                    V.tensor_tensor(XC[:, zcols(b)], take(q + b, i, each), RB[:, blk(b)], ALU.mult
                                    ).then_inc(evac, 1)
                lo(SLOT0["conv"] + 3 * jj + 2, 6 * i)
                for b in range(NB):
                    V.tensor_tensor(TT[:, b % 2, :], take(q + 3 + b, i, each), RB[:, blk(b)], ALU.mult
                                    ).then_inc(evac, 1)
                    dve.wait_ge(evac, q + 4 + b + each * i)
                    V.tensor_tensor(Z[:, b * BLK + 1 + (b == 2):(b + 1) * BLK + 1 + (b == 2)], TT[:, b % 2, :],
                                    XC[:, zcols(b)], ALU.mult).then_inc(S("z"), 1)
                dve.wait_ge(S("z"), NB * (jj + 1) + 2 * NB * i)
                lo(SLOT0["conv"] + 3 * jj + 3, 6 * i)
                dve.wait_ge(S("tap1"), jj + 1 + 2 * i)
                tap = convw[:, bass.ds(j, 1), :].rearrange("p o a -> p (o a)")
                for w, z in ((0, 0), (2, 2)):
                    then(V.scalar_tensor_tensor(out=XC[:], in0=Z[:, z:z + T + 1], scalar=tap[:, w:w + 1],
                                                in1=XC[:], op0=ALU.mult, op1=ALU.add)) if w == 0 else \
                        V.scalar_tensor_tensor(out=XC[:], in0=Z[:, z:z + T + 1], scalar=tap[:, w:w + 1],
                                               in1=XC[:], op0=ALU.mult, op1=ALU.add).then_inc(S("conv"), 1)
                dve.wait_ge(S("conv"), jj + 1 + 2 * i)

                def cin_lo(b):
                    n = NB * jj + b
                    dve.wait_ge(S("cin_hi"), n + 1 + 2 * NB * i)
                    rest(one(CIN, j)[:, 1, blk(b)], TT[:, n % 2, :], one(CIN, j)[:, 0, blk(b)]
                         ).then_inc(S("cin_lo"), 1)

                for b in range(NB):
                    n = NB * jj + b
                    src = take(q + 6 + b, i, each)
                    if b == 2:
                        dve.wait_ge(S("cin_lo"), n - 1 + 2 * NB * i)
                    V.tensor_tensor(TT[:, n % 2, :], src, RB[:, blk(b)], ALU.mult
                                    ).then_inc(evac, 1)
                    dve.wait_ge(evac, q + 7 + b + each * i)
                    V.tensor_tensor(TT[:, n % 2, :], TT[:, n % 2, :], XC[:, zcols(b)], ALU.mult
                                    ).then_inc(S("cin"), 1)
                    if b:
                        cin_lo(b - 1)
                cin_lo(NB - 1)
            step.leave(2)

        def conv_out(i):
            for par in range(2):
                lo(SLOT0["co"] + par + 1, 2 * i)
                for e in range(2):
                    dve.wait_ge(S(f"co_stored{e}"), 32 * i + 16 * par)
                    for b in range(NB):
                        V.tensor_copy(COS[:, e, blk(b)], take(RES0["co"] + 6 * par + 3 * e + b, i, 12)
                                      ).then_inc(evac, 1)

        with loop(V, 2) as i:
            conv_out(i)

        dve.wait_ge(S("tables_made"), 32)
        tt(DM[0:GP], ident[0:GP, 0:GP].unsqueeze(1).to_broadcast([GP, GROUPS, GP]),
           s5d[0:GP, :].unsqueeze(2).to_broadcast([GP, GROUPS, GP]), ALU.mult)
        for slot in (0, SLOT_S):
            then(V.memset(H[:, slot, :], 0.0))

        def s5a(i):
            for par in range(2):
                it = 2 * i + par
                dve.wait_ge(S("lags"), it + 1)
                dve.wait_ge(S(f"lags_stored{par}"), 16 * i)
                then(V.tensor_copy(LL[0:GP, par], PS[6 + par][0:GP, 0:2 * LAGS * GP].rearrange(
                    "p (g l) -> p g l", g=2)))
                lag0 = LL[0:GP, par, :, (C - 1) * GP:C * GP]
                V.tensor_tensor(lag0, lag0, DM[0:GP, bass.ds(2 * it, 2), :], ALU.add).then_inc(S("lags_staged"), 1)
                dve.wait_ge(S("states_bwd"), it + 1)
                dst = H[:, :, bass.ds(GROUPS + 2 * it, 2)].rearrange("p s g -> p g s")
                src = PS[4 + par][:, 0:2 * NC].rearrange("p (g c) -> p g c", g=2)
                for at_, n, c in ((1, NCP, 0), (SLOT_S + 1, NCS, NCP)):
                    V.tensor_copy(dst[:, :, at_:at_ + n], src[:, :, c:c + n][:, :, ::-1]
                                  ).then_inc(S("h_bwd"), 1)

        with loop(V, 8) as i:
            step.enter(i, 2)
            s5a(i)
            step.leave(8)

        dve.wait_ge(S("h_fwd"), 32)
        dve.wait_ge(S("h_bwd"), 32)
        scan = Count(S("scan"))

        def advance(slot, both):
            def seqs(a, s, p0=0, p1=P):
                a = a[p0:p1, bass.ds(s, SLOT_S + 1 if both else 1), :]
                return a[:, ::SLOT_S, :] if both else a

            n = 2 if both else 1

            def wide(a, p0=0, p1=P):
                return a[p0:p1].unsqueeze(1).to_broadcast([p1 - p0, n, GD])

            half = P // 2
            nxt = seqs(H, slot + 1)
            scan.up(V.tensor_tensor(S1[:, 0:n, :], seqs(H, slot), wide(LR), ALU.mult))
            real = scan.n
            scan.up(V.tensor_tensor(S2[0:half, 0:n, :], seqs(H, slot, half, P), wide(LI, half, P), ALU.mult))
            scan.up(V.tensor_tensor(S2[half:P, 0:n, :], seqs(H, slot, 0, half), wide(LI, 0, half), ALU.mult))
            dve.wait_ge(scan.sem, real)
            scan.up(V.tensor_tensor(nxt, nxt, S1[:, 0:n, :], ALU.add))
            dve.wait_ge(scan.sem, scan.n)
            scan.up(V.tensor_tensor(nxt, nxt, S2[:, 0:n, :], ALU.add))
            dve.wait_ge(scan.sem, scan.n)

        def gates(i, both):
            for par in range(2):
                lo(SLOT0["gate"] + par + 1, 2 * i)
                for b in range(NB):
                    n = NB * par + b
                    src = take(RES0["gate"] + n, i, 2 * NB)
                    if both != "first" or n >= 2:
                        dve.wait_ge(S("gate_made"), n - 1 + 2 * NB * i)
                    V.tensor_tensor(TG[:, n % 2, :], src, RB[:, blk(b)], ALU.mult).then_inc(evac, 1)
                for s in range(8):
                    advance(16 * i + 8 * par + s, both is not False)

        gates(0, "first")
        with V.Fori(1, 4) as i:
            scan.enter(i - 1, 80)
            gates(i, True)
            scan.leave(3)
        with V.Fori(4, 8) as i:
            scan.enter(i - 4, 80)
            gates(i, False)
            scan.leave(4)
        assert scan.n == 5 * SCAN_STEPS

        for k in range(HT):
            dve.wait_ge(S("y_hi"), k + 1)
            V.tensor_tensor(YHL[:, 1, k].rearrange("p (c t) -> p c t", t=C),
                            YL[:, k % 2].rearrange("p t c -> p c t"),
                            YHL[:, 0, k].rearrange("p (c t) -> p c t", t=C).bitcast(F32), ALU.subtract
                            ).then_inc(S("y_lo"), 1)

        with loop(V, 4) as i:
            step.enter(i, 2 * NB)
            for par in range(2):
                j = 2 * i + par
                q = RES0["glu"] + 6 * par
                lo(SLOT0["glu"] + par + 1, 2 * i)
                dve.wait_ge(S("merged_lo"), NB * par + 2 * NB * i)
                for b in range(NB):
                    V.tensor_copy(SB[:, blk(b)], take(q + b, i, 12)).then_inc(evac, 1)

                def merged_lo(b):
                    n = NB * par + b
                    dve.wait_ge(S("merged_hi"), n + 1 + 2 * NB * i)
                    rest(one(XN[:, 1], j)[:, blk(b)], SB[:, blk(b)], one(XN[:, 0], j)[:, blk(b)]
                         ).then_inc(S("merged_lo"), 1)

                for b in range(NB):
                    n = NB * par + b
                    src = take(q + NB + b, i, 12)
                    dve.wait_ge(S("glu_gate"), n + 1 + 2 * NB * i)
                    V.tensor_tensor(SB[:, blk(b)], src, SB[:, blk(b)], ALU.mult).then_inc(evac, 1)
                    dve.wait_ge(evac, q + NB + b + 1 + 12 * i)
                    dve.wait_ge(S(f"glu_in{par}"), 48 * (i + 1))
                    tt(SB[:, blk(b)], SB[:, blk(b)], G1L[:, par, blk(b)], ALU.mult)
                    dve.wait_ge(S("gated_conv"), j + 1)
                    V.tensor_tensor(SB[:, blk(b)], SB[:, blk(b)], G2L[:, par, blk(b)], ALU.add
                                    ).then_inc(S("merged"), 1)
                    if b:
                        merged_lo(b - 1)
                merged_lo(NB - 1)
            step.leave(4)

        def add_squares(norm, k, sq):
            dve.wait_ge(S("squares"), KT * (norm - 1) + k + 1)
            dve.wait_ge(S("squares_added"), KT * (norm - 1) + k)
            V.tensor_tensor(ACC2[:], ACC2[:], sq, ALU.add).then_inc(S("squares_added"), 1)

        def residual(name, norm, first):
            def pair(i):
                for par in range(2):
                    j = 2 * i + par
                    lo(SLOT0[name] + par + 1, 2 * i)
                    if first:
                        dve.wait_ge(S(f"xr_in{par}"), 16 * (i + 1))
                    for b in range(NB):
                        src = take(RES0[name] + NB * par + b, i, 2 * NB)
                        h = one(HR, j)[:, blk(b)]
                        V.tensor_tensor(h, src, XR[:, par, blk(b)] if first else h, ALU.add).then_inc(evac, 1)
                    if par or not isinstance(i, int):
                        add_squares(norm, j - 1, SQ2[:, 1 - par, :])
            then(V.memset(ACC2[:], 0.0))
            pair(0)
            with V.Fori(1, 4) as i:
                pair(i)

        def split_residual(norm):
            for k in range(KT):
                dve.wait_ge(S("hn_hi"), KT * (norm - 1) + k + 1)
                V.scalar_tensor_tensor(out=XN[:, 1, k, :], in0=HR[:, k, :], scalar=gains[:, norm + 1, k:k + 1],
                                       in1=XN[:, 0, k, :].bitcast(F32), op0=ALU.mult, op1=ALU.subtract
                                       ).then_inc(S("hn_lo"), 1)
                if k == 1:
                    add_squares(norm, KT - 1, SQ2[:, 1, :])
            reciprocals(norm)

        dve.wait_ge(S("merged_lo"), NB * KT)
        residual("wo", 1, True)
        split_residual(1)

        with loop(V, 4) as i:
            for par in range(2):
                lo(SLOT0["q"] + par + 1, 2 * i)
                dve.wait_ge(S(f"q_stored{par}"), 16 * i)
                for b in range(NB):
                    V.tensor_tensor(QS[:, par, blk(b)], take(RES0["q"] + NB * par + b, i, 2 * NB), RB[:, blk(b)],
                                    ALU.mult).then_inc(evac, 1)

        def maxima(i, u):
            par, idx = u % 2, 2 * NB * i + u
            for half in range(2):
                dve.wait_ge(S("scores"), 2 * idx + half + 1)
                lts = slice(2 * half, 2 * half + 2)
                then(V.reduce_max(smx[:, par, lts], PS[2 * par + half][:].rearrange("p (l m) -> p l m", l=2), AX.X))
                V.tensor_scalar(snm[:, par, lts], smx[:, par, lts], -SCALE, None, ALU.mult).then_inc(S("maxima"), 1)

        def probs(i, u):
            par, idx = u % 2, 2 * NB * i + u
            dve.wait_ge(S("exps"), 4 * (idx + 1))
            then(V.reciprocal(sri[:, par, :], ssm[:, par, :]))
            for lt in range(4):
                V.tensor_scalar(PB[:, par, lt, :], PB[:, par, lt, :], sri[:, par, lt:lt + 1], None, ALU.mult
                                ).then_inc(S("probs"), 1)

        def outputs(i, u):
            par, idx = u % 2, 2 * NB * i + u
            h, b = 2 * i + u // NB, u % NB
            dve.wait_ge(S("p_turned"), 2 * idx + 1)
            if not (isinstance(i, int) and i == 0 and u < 2):
                dve.wait_ge(S("att_out"), 2 * (idx - 1))
            V.tensor_copy(PT[:, par, 0, :], PS[4][:]).then_inc(S("pt_staged"), 1)
            for e in range(2):
                dve.wait_ge(S("o_hi"), 2 * idx + e + 1)
                V.tensor_tensor(one(XN[:, 1], 2 * h + e)[:, blk(b)], PS[6 + e][:],
                                one(XN[:, 0], 2 * h + e)[:, blk(b)].bitcast(F32), ALU.subtract
                                ).then_inc(S("o_lo"), 1)

        maxima(0, 0)
        for n in range(1, HEADS * NB):
            i, u = divmod(n, 2 * NB)
            probs(*divmod(n - 1, 2 * NB))
            maxima(i, u)
            outputs(*divmod(n - 1, 2 * NB))
        last = divmod(HEADS * NB - 1, 2 * NB)
        probs(*last)
        outputs(*last)

        residual("xo", 2, False)
        split_residual(2)

        def chunk(c, final=False):
            for f in range(4):
                lo(SLOT0["ffn"] + f + 1, CH_SLOTS * c)
                kk, q = f // 2, RES0["ffn"] + NB * f

                def act_lo(b):
                    dve.wait_ge(S("act_hi"), NB * kk + b + 1 + 2 * NB * c)
                    rest(AF[:, 1, kk, blk(b)], TF[:, (b + 1) % 2, :], AF[:, 0, kk, blk(b)]
                         ).then_inc(S("act_lo"), 1)

                for b in range(NB):
                    if f % 2 == 0:
                        src = take(q + b, c, CH_RES)
                        if b == 0:
                            dve.wait_ge(S("act_lo"), NB * kk + 2 * NB * c)
                        if b == 2:
                            dve.wait_ge(S("silu"), NB * kk + 1 + 2 * NB * c)
                        V.tensor_tensor(TF[:, b % 2, :], src, RB[:, blk(b)], ALU.mult).then_inc(evac, 1)
                    else:
                        src = take(q + b, c, CH_RES)
                        dve.wait_ge(S("silu"), NB * kk + min(b + 2, 3) + 2 * NB * c)
                        if b == 2:
                            dve.wait_ge(S("act_lo"), NB * kk + 1 + 2 * NB * c)
                        V.tensor_tensor(TF[:, (b + 1) % 2, :], src, RB[:, blk(b)], ALU.mult).then_inc(evac, 1)
                        dve.wait_ge(evac, q + b + 1 + CH_RES * c)
                        V.tensor_tensor(TF[:, (b + 1) % 2, :], TF[:, (b + 1) % 2, :], SG[:, blk(b)], ALU.mult
                                        ).then_inc(S("act"), 1)
                        if b:
                            act_lo(b - 1)
                if f % 2:
                    act_lo(NB - 1)
            for part in range(2):
                if not (final and part):
                    lo(SLOT0["ffn"] + 5 + part, CH_SLOTS * c)
                for e in range(4):
                    for b in range(NB):
                        q = RES0["ffn"] + 4 * NB + part * 4 * NB + NB * e + b
                        h = HR[:, 4 * part + e, blk(b)]
                        V.tensor_tensor(h, take(q, c, CH_RES), h, ALU.add).then_inc(evac, 1)

        with V.Fori(0, CHUNKS - 1) as c:
            chunk(c)
        then(V.memset(ACC2[:], 0.0))
        chunk(CHUNKS - 1, final=True)
        for k in range(KT):
            add_squares(3, k, SG[:])
        reciprocals(3)
        for k in range(KT):
            if k >= 2:
                dve.wait_ge(S(f"out_stored{k % 2}"), 16 * (k // 2))
            V.scalar_tensor_tensor(out=YO[:, k % 2, :], in0=HR[:, k, :], scalar=gains[:, 4, k:k + 1], in1=RB[:],
                                   op0=ALU.mult, op1=ALU.mult).then_inc(S("y_out"), 1)

    block.__exit__(None, None, None)


def kernel(**inputs):
    import numpy as np
    import concourse.bacc as bacc
    from concourse.bass_utils import run_bass_kernel_spmd

    a = {k: np.asarray(v) for k, v in inputs.items()}

    def tiles(w):
        r, c = w.shape
        return w.reshape(r // P, P, c // P, P).transpose(2, 1, 0, 3).reshape(c // P, P, -1)

    w_in, kv = tiles(a["w_in"][0]), tiles(a["w_kv"][0])
    u, xc, gb, gc, g = (w_in[i:j] for i, j in ((0, 4), (4, 8), (8, 12), (12, 16), (16, 32)))
    conv = np.stack([xc, gc, gb], 1).reshape(-1, P, SLOTW)
    co = tiles(a["w_conv_out"][0]).reshape(4, 2, P, 512).transpose(0, 2, 1, 3).reshape(4, P, SLOTW)
    glu = np.concatenate([tiles(a["w_glu_b"][0]), tiles(a["w_glu_a"][0])], 2)
    gu = tiles(a["w_gate_up"][0])
    down = a["w_down"][0].reshape(CHUNKS, 2, P, 2, 4, P).transpose(0, 3, 2, 4, 1, 5).reshape(CHUNKS, 2, P, SLOTW)
    ffn = []
    for c in range(CHUNKS):
        ffn += [gu[2 * c], gu[FT + 2 * c], gu[2 * c + 1], gu[FT + 2 * c + 1], down[c, 0], down[c, 1]]
    stream = np.concatenate([kv, u, conv, co, g, glu, tiles(a["w_o"][0]), tiles(a["w_q"][0]),
                             tiles(a["w_xo"][0]), np.stack(ffn)])

    def cols(v):
        return v.reshape(-1, P).T

    def states(v):
        v = v.transpose(2, 0, 1).reshape(NS, GD)
        return np.concatenate([v, v])

    def stacked(re, im):
        return np.concatenate([re, im], 1)

    br, bi = (a[k][0].transpose(0, 2, 1, 3) for k in ("s5_b_re", "s5_b_im"))
    cr, ci = (a[k][0].transpose(0, 3, 1, 2) for k in ("s5_c_re", "s5_c_im"))
    f = np.float32
    half = np.where(np.arange(P) < P // 2, -1.0, 1.0)
    arrays = {
        "W_all": stream,
        "xT": np.concatenate([a["x_prompt"][0].T, a["x_sample"][0].T], 1).reshape(KT, P, T),
        "memT": np.concatenate([a["mem_prompt"][0].T, a["mem_sample"][0].T], 1).reshape(KT, P, M2)
        .transpose(1, 0, 2),
        "gains": np.stack([cols(v) for v in (a["norm_mix_g"][0], a["norm_mem_g"][0], a["norm_xattn_g"][0],
                                             a["norm_ffn_g"][0], a["norm_final_g"])], 1),
        "bgate": cols(a["b_gate"][0]),
        "convw": a["conv_w"][0].reshape(3, HT, P).transpose(2, 1, 0),
        "a_re": states(a["s5_a_re"][0]), "a_im": states(a["s5_a_im"][0]),
        "log_dt": np.repeat(a["s5_log_dt"][0].reshape(1, GD), P, 0),
        "s5_d": a["s5_d"][0].reshape(GROUPS, GP).T,
        "BX": stacked(br, bi), "BY": stacked(bi, br), "CX": stacked(cr, ci), "CY": stacked(ci, cr),
        "ones": np.ones((P, P), f), "ident": np.eye(P, dtype=f), "eps": np.full((P, 1), EPS, f),
        "sgn": np.stack([half, -half], 1).astype(f),
    }
    nc = bacc.Bacc("TRN2", target_bir_lowering=False, num_devices=1, dynamic_dma_scratch_size=1024)
    io = {}
    for name, v in arrays.items():
        arrays[name] = np.ascontiguousarray(v)
        io[name] = nc.dram_tensor(name, v.shape, F32, kind="ExternalInput").ap()
    io["yT"] = nc.dram_tensor("yT", (KT, P, T), F32, kind="ExternalOutput").ap()
    shapes = {"U": (DH, C, NC), "CO": (KT, P, T), "G": (2 * KT, P, T), "V": (P, GROUPS, 2, P),
              "W": (P, GROUPS, 2, NPOW * GP), "BB": (2, P, GROUPS, GP), "L": (GP, GROUPS, LAGS * GP),
              "M": (P, GROUPS, P), "Y": (P, GROUPS, NC), "KV": (2 * KT, P, M2), "Q": (KT, P, T)}
    scratch = {k: nc.dram_tensor(f"scratch_{k}", s, F32).ap() for k, s in shapes.items()}
    build(nc, io, scratch)
    r = run_bass_kernel_spmd(nc, [arrays], core_ids=[0])
    y = np.asarray(r.results[0]["yT"]).reshape(D, T).T
    return y[None, :T_PROMPT], y[None, T_PROMPT:]
```

```python
import math

import concourse.bass as bass
from concourse import mybir

F32 = mybir.dt.float32
F32R = mybir.dt.float32r
I32 = mybir.dt.int32
ALU = mybir.AluOpType
ACT = mybir.ActivationFunctionType
AX = mybir.AxisListType

P = 128
D = 1024
KT = D // P
T_PROMPT, T_SAMPLE = 1024, 512
T = T_PROMPT + T_SAMPLE
BLK = 512
NB = T // BLK
NMEM = 256
M2 = 2 * NMEM
HEADS, HD = 4, 256
DH = 512
HT = DH // P
DFF = 2816
FT = DFF // P
EPS = 1e-6
SCALE = HD ** -0.5
GROUPS, GP, NS = 32, 16, 64
GD = 2 * GROUPS
C = 8
NC = T // C
NCP, NCS = T_PROMPT // C, T_SAMPLE // C
SLOTS = NC + 2
SLOT_S = NCP + 1
LAGS = 2 * C - 1
NPOW = C + 1

SLOTW = 1024
RING = 6

STAGES = [("kv", 16, 1), ("u", 4, 3), ("conv", 12, 3), ("co", 4, 6), ("gate", 16, 3), ("glu", 8, 6),
          ("wo", 8, 3), ("q", 8, 3), ("xo", 8, 3)]
SLOT0, RES0 = {}, {}
_n = _q = 0
for _name, _slots, _per in STAGES:
    SLOT0[_name], RES0[_name] = _n, _q
    _n += _slots
    _q += _slots * _per
SLOT0["ffn"], RES0["ffn"] = _n, _q
CHUNKS = FT // 2
CH_SLOTS, CH_RES = 6, 4 * NB + 2 * 4 * NB
NSLOT = _n + CHUNKS * CH_SLOTS

LOG2E = 1.4426950408889634
LN2_HI, LN2_LO = 0.693359375, -2.12194440e-4
SCAN_STEPS = NCP
ROUND = 12582912.0
TWO_PI = (6.28125, 0.0019350051879882812, 3.0199159819185e-07)


class Count:

    def __init__(self, sem):
        self.sem, self.n, self.raised = sem, 0, 0

    def up(self, ins, k=1):
        ins.then_inc(self.sem, k)
        self.n = self.n + k
        self.raised += k
        return self.n

    def enter(self, i, each):
        self.base, self.each, self.raised = self.n, each, 0
        self.n = self.base + i * each

    def leave(self, times):
        assert self.raised == self.each, (self.raised, self.each)
        self.n = self.base + times * self.each


def build(nc, io, scratch):
    base = 2048
    assert nc.sbuf_base <= base

    off = [base]

    def keep(name, shape, dt=F32):
        t = nc.alloc_sbuf_tensor_at(name, [P] + shape, dt, offset=off[0])
        off[0] += -(-4 * math.prod(shape) // 32) * 32
        return t

    XN = keep("XN", [2, KT, T], F32R)
    WR = keep("WR", [2, SLOTW])
    WHI = keep("WHI", [2, SLOTW], F32R)
    WLO = keep("WLO", [2, SLOTW], F32R)
    RB = keep("RB", [T])
    ones = keep("ones", [P])
    ident = keep("ident", [P])
    gains = keep("gains", [5, KT])
    bgate = keep("bgate", [2 * KT])
    bcol = keep("bcol", [2])
    convw = keep("convw", [HT, 3])
    epsc = keep("epsc", [1])
    sgn = keep("sgn", [2])
    rcol = keep("rcol", [4])
    LR = keep("LR", [GD])
    LI = keep("LI", [GD])
    s5d = keep("s5d", [GROUPS])
    smx = keep("smx", [2, 4])
    snm = keep("snm", [2, 4])
    ssm = keep("ssm", [2, 4])
    sri = keep("sri", [2, 4])
    w0 = off[0]
    K = 1024

    def at(name, kb, shape, dt=F32):
        assert w0 + kb * K + 4 * math.prod(shape) <= nc.sbuf_usable_end, name
        return nc.alloc_sbuf_tensor_at(name, [P] + shape, dt, offset=w0 + int(kb * K))

    MN = at("MN", 0, [2, KT, M2], F32R)
    MEM = at("MEM", 32, [KT, M2])
    XS = at("XS", 48, [2, T])
    SQ = at("SQ", 60, [2, T])
    ACC = at("ACC", 72, [T])
    MACC = at("MACC", 78, [M2])
    MSQ = at("MSQ", 80, [2, M2])
    KVS = at("KVS", 32, [2, M2])
    RM = at("RM", 84, [M2])
    NT0 = at("NT0", 86, [BLK])
    PA = at("PA", 88, [16, GD])
    BX, BY, CX, CY, BBX, BBY = (at(n, 36 + 2 * i, [GROUPS, GP]) for i, n in
                                enumerate(("BX", "BY", "CX", "CY", "BBX", "BBY")))
    PVR, PVI, PWR, PWI = (at(n, 64.5 + 2.25 * i, [NPOW, GD]) for i, n in
                          enumerate(("PVR", "PVI", "PWR", "PWI")))
    PR, PI = at("PR", 76, [NPOW, GD]), at("PI", 78.25, [NPOW, GD])
    TB = at("TB", 76, [2, 4 * NPOW * GP])
    TC = at("TC", 80.5, [2, 4 * NPOW * GP])
    TX = at("TX", 85, [4 * NPOW * GP])
    UB = at("UB", 48, [2, C, NC])
    CIN = at("CIN", 0, [HT, 2, T], F32R)
    XC = at("XC", 48, [T + 1])
    Z = at("Z", 54.25, [T + 3])
    TT = at("TT", 60.5, [2, BLK])
    COS = at("COS", 48, [2, T])
    H = at("H", 0, [SLOTS, GD])
    U = at("U", 48.5, [GROUPS, NC])
    VN = at("VN", 72.5, [2, 4, P])
    WK = at("WK", 76.5, [2, 4, P])
    BBL = at("BBL", 80.5, [2, 4, GP])
    VT = at("VT", 81, [2, 4 * P])
    LL = at("LL", 85, [2, 2, LAGS * GP])
    DM = at("DM", 89, [GROUPS, GP])
    S1, S2 = at("S1", 91, [2, GD]), at("S2", 91.5, [2, GD])
    TG = at("TG", 72.5, [2, BLK])
    GS = at("GS", 76.5, [2, T])
    WO = at("WO", 72.5, [2, 4, P])
    ML = at("ML", 76.5, [2, 2, P])
    YS = at("YS", 78.5, [2, 2 * NC])
    YHL = at("YHL", 0, [2, HT, T], F32R)
    YL = at("YL", 48, [2, C, NC])
    G1L, G2L, COL = at("G1L", 48, [2, T]), at("G2L", 60, [2, T]), at("COL", 72, [2, T])
    SB = at("SB", 84, [T])
    HR = at("HR", 0, [KT, T])
    SQ2 = at("SQ2", 48, [2, T])
    ACC2 = at("ACC2", 82, [T])
    NT = at("NT", 88, [BLK])
    QS = at("QS", 66, [2, T])
    XR = at("XR", 66, [2, T])
    KL = at("KL", 48, [2, 2, M2])
    VL = at("VL", 56, [2, 2, 4, P])
    PB = at("PB", 64, [2, 4, NMEM])
    PT = at("PT", 72, [2, 2, BLK])
    QL = at("QL", 80, [2, 2, BLK])
    AF = at("AF", 48, [2, 2, T], F32R)
    SG = at("SG", 72, [T])
    TF = at("TF", 78, [2, BLK])
    YO = at("YO", 48, [2, T])

    U_d, CO_d, G_d, V_d, W_d, BB_d, L_d, M_d, Y_d, KV_d, Q_d = (
        scratch[k] for k in ("U", "CO", "G", "V", "W", "BB", "L", "M", "Y", "KV", "Q"))
    K_d = KV_d[0:KT]
    VV_d = KV_d[KT:2 * KT].rearrange("e p (m d) -> e p m d", d=P)

    VBANKS = [(2, 3, 4, 5), (0, 1, 6, 7)]
    PS = [nc.alloc_psum_tensor(f"bank{i}", [P, BLK], F32) for i in range(8)]

    sem = {}

    def S(name):
        if name not in sem:
            sem[name] = nc.alloc_semaphore(name)
        return sem[name]

    raw = [S("raw_even"), S("raw_odd")]
    whi, wlo = S("weights_hi"), S("weights_lo")
    res, evac = S("results"), S("evacuated")

    def loop(eng, times):
        return eng.Fori(0, times)

    block = nc.Block()
    block.__enter__()

    def zcols(b):
        return slice(b * BLK + (b == 2), (b + 1) * BLK + (b == 2))

    def blk(b):
        return slice(b * BLK, (b + 1) * BLK)

    def bank(q):
        return PS[(q - RES0["u"]) % RING]

    def one(a, i):
        return a[:, i] if isinstance(i, int) else a[:, bass.ds(i, 1)].rearrange(
            {3: "p o a -> p (o a)", 4: "p o a b -> p (o a) b"}[len(a.shape)])

    def tile_of(a, i):
        return a[i] if isinstance(i, int) else a[bass.ds(i, 1)].rearrange("o p t -> p (o t)")

    @block.sync
    def _(sp):
        def weights(n, parity, i=0):
            if not (isinstance(i, int) and n + 2 * i < 2):
                sp.wait_ge(wlo, n - 1 + 2 * i)
            sp.dma_start(WR[:, parity, :], tile_of(io["W_all"], n + 2 * i)).then_inc(raw[parity], 16)

        for j, name in enumerate(("a_re", "a_im", "log_dt")):
            sp.dma_start(PA[:, j, :], io[name]).then_inc(S("params_in"), 16)
        for dst, src in ((ones, "ones"), (gains, "gains"), (epsc, "eps"), (sgn, "sgn"), (ident, "ident"),
                         (bgate, "bgate"), (convw, "convw")):
            sp.dma_start(dst[:], io[src]).then_inc(S("consts_in"), 16)
        sp.dma_start(s5d[0:GP, :], io["s5_d"]).then_inc(S("consts_in"), 16)
        sp.dma_start(MEM[:, 0:4, :], io["memT"][:, 0:4, :]).then_inc(S("mem_in0"), 16)
        weights(0, 0)
        sp.dma_start(MEM[:, 4:8, :], io["memT"][:, 4:8, :]).then_inc(S("mem_in1"), 16)
        weights(1, 1)
        for k in range(2):
            sp.dma_start(XS[:, k, :], io["xT"][k]).then_inc(S(f"x_in{k}"), 16)

        def keys(i, more_x):
            for par in range(2):
                n = 2 * i + par
                weights(SLOT0["kv"] + par + 2, par, i)
                if more_x:
                    sp.wait_ge(S("x_lo"), n + 1)
                    sp.wait_ge(S("x_acc"), n + 1)
                    sp.dma_start(XS[:, par, :], tile_of(io["xT"], n + 2)).then_inc(S(f"x_in{par}"), 16)
                sp.wait_ge(evac, n + 1)
                sp.dma_start(tile_of(KV_d, n), KVS[:, par, :]).then_inc(S(f"kv_stored{par}"), 16)

        with loop(nc.sync, 3) as i:
            keys(i, True)
        keys(3, False)
        def store_values(half):
            for m in range(M2 // P):
                n = KT + 4 * half + m
                sp.wait_ge(evac, n + 1)
                sp.dma_start(VV_d[4 * half:4 * half + 4, :, m, :].rearrange("e p d -> p e d"),
                             KVS[:, n % 2, :].rearrange("p (e d) -> p e d", d=P)).then_inc(S(f"kv_stored{n % 2}"), 16)

        for j in range(8):
            weights(SLOT0["kv"] + KT + j + 2, j % 2)
            if j == 4:
                store_values(0)
        store_values(1)
        for j in range(4):
            weights(SLOT0["u"] + j + 2, j % 2)
            sp.wait_ge(evac, RES0["u"] + NB * (j + 1))
            sp.dma_start(U_d[j * P:(j + 1) * P], UB[:, j % 2]).then_inc(S(f"u_stored{j % 2}"), 16)
        with loop(nc.sync, 6) as i:
            for par in range(2):
                weights(SLOT0["conv"] + par + 2, par, i)
        for j in range(4):
            weights(SLOT0["co"] + j + 2, j % 2)
            for e in range(2):
                sp.wait_ge(evac, RES0["co"] + 6 * j + 3 * (e + 1))
                sp.dma_start(CO_d[2 * j + e], COS[:, e, :]).then_inc(S(f"co_stored{e}"), 16)

        for e in range(2):
            sp.wait_ge(S(f"co_stored{e}"), 64)
        sp.wait_ge(S("tables_made"), 32)
        for par in range(2):
            sp.wait_ge(S(f"tables_stored{par}"), 2 * 4 * 32)
        sp.wait_ge(S("bb_stored"), 32)
        u_rows = U_d.rearrange("(g p) s c -> p s g c", p=GP)
        for s in range(C):
            sp.dma_start(U[GP * s:GP * (s + 1)], u_rows[:, s]).then_inc(S("u_in"), 16)

        def s5a_loads(it, par):
            g = bass.ds(2 * it, 2)
            sem_in = S(f"s5a_in{par}")
            sp.dma_start(VN[:, par], V_d[:, g, :, :].rearrange("p g d c -> p (g d) c")).then_inc(sem_in, 16)
            wk = WK[:, par].rearrange("p (g d) c -> p g d c", d=2)
            sp.dma_start(wk[:, :, 0], W_d[:, g, 0, 0:P]).then_inc(sem_in, 16)
            sp.dma_start(wk[:, :, 1], W_d[:, g, 1, GP:GP + P]).then_inc(sem_in, 16)
            bb = BBL[:, par].rearrange("p (g d) c -> p g d c", d=2)
            for d in range(2):
                sp.dma_start(bb[:, :, d], BB_d[d, :, g, :]).then_inc(sem_in, 16)

        def s5a(i, last=False):
            for par in range(2):
                it = 2 * i + par
                if not (last and par):
                    sp.wait_ge(S("states_bwd"), it)
                    s5a_loads(it + 1, 1 - par)
                sp.wait_ge(S("lags_staged"), it + 1)
                sp.dma_start(L_d[:, bass.ds(2 * it, 2), :], LL[0:GP, par].rearrange("p a b -> p a b")
                             ).then_inc(S(f"lags_stored{par}"), 16)

        s5a_loads(0, 0)
        with loop(nc.sync, 7) as i:
            s5a(i)
        s5a(7, last=True)
        for par in range(2):
            sp.wait_ge(S(f"lags_stored{par}"), 8 * 16)
        for s in range(C):
            sp.dma_start(M_d[GP * s:GP * (s + 1)],
                         L_d[:, :, (C - 1 - s) * GP:(C - 1 - s) * GP + P]).then_inc(S("m_stored"), 16)

        with loop(nc.sync, 8) as i:
            for par in range(2):
                weights(SLOT0["gate"] + par + 2, par, i)
                sp.wait_ge(S("gate_made"), 2 * NB * i + NB * (par + 1))
                sp.dma_start(tile_of(G_d, 2 * i + par), GS[:, par, :]).then_inc(S(f"gate_stored{par}"), 16)

        sp.wait_ge(S("m_stored"), 128)
        for par in range(2):
            sp.wait_ge(S(f"gate_stored{par}"), 128)

        def s5b_loads(it, par):
            g = bass.ds(2 * it, 2)
            wo = WO[:, par].rearrange("p (g d) c -> p g d c", d=2)
            sp.dma_start(wo[:, :, 0], W_d[:, g, 0, GP:GP + P]).then_inc(S(f"s5b_in{par}"), 16)
            sp.dma_start(wo[:, :, 1], W_d[:, g, 1, 0:P]).then_inc(S(f"s5b_in{par}"), 16)
            sp.dma_start(ML[:, par], M_d[:, g, :]).then_inc(S(f"s5b_in{par}"), 16)

        def s5b(i, last=False):
            for par in range(2):
                it = 2 * i + par
                if not (last and par):
                    sp.wait_ge(S("s5_out"), it)
                    s5b_loads(it + 1, 1 - par)
                sp.wait_ge(S("y_made"), it + 1)
                sp.dma_start(Y_d[:, bass.ds(2 * it, 2), :], YS[:, par, :].rearrange("p (g c) -> p g c", g=2)
                             ).then_inc(S(f"y_stored{par}"), 16)

        s5b_loads(0, 0)
        with loop(nc.sync, 7) as i:
            s5b(i)
        s5b(7, last=True)
        for par in range(2):
            sp.wait_ge(S(f"y_stored{par}"), 128)
        y_rows = Y_d.rearrange("(t p) g c -> g p t c", p=GP)
        for k in range(HT):
            if k >= 2:
                sp.wait_ge(S("y_lo"), k - 1)
            for g in range(P // GP):
                sp.dma_start(YL[GP * g:GP * (g + 1), k % 2], y_rows[8 * k + g]).then_inc(S(f"y_in{k % 2}"), 16)

        sp.wait_ge(S("y_lo"), HT)

        def glu_loads(j):
            b = j % 2
            if j >= 2:
                sp.wait_ge(S("merged_lo"), NB * (j - 1))
            for dst, src in ((COL, CO_d[j]), (G2L, G_d[KT + j]), (G1L, G_d[j])):
                sp.dma_start(dst[:, b], src).then_inc(S(f"glu_in{b}"), 16)

        glu_loads(0)
        for j in range(KT):
            weights(SLOT0["glu"] + j + 2, j % 2)
            if j + 1 < KT:
                glu_loads(j + 1)

        sp.wait_ge(S("merged_lo"), NB * KT)
        for k in range(2):
            sp.dma_start(XR[:, k, :], io["xT"][k]).then_inc(S(f"xr_in{k}"), 16)

        def wo(i, more_x):
            for par in range(2):
                weights(SLOT0["wo"] + par + 2, par, i)
                if more_x:
                    sp.wait_ge(evac, RES0["wo"] + NB * (par + 1) + 2 * NB * i)
                    sp.dma_start(XR[:, par, :], tile_of(io["xT"], 2 * i + par + 2)).then_inc(S(f"xr_in{par}"), 16)

        with loop(nc.sync, 3) as i:
            wo(i, True)
        wo(3, False)
        def queries(i):
            for par in range(2):
                weights(SLOT0["q"] + par + 2, par, i)
                sp.wait_ge(evac, RES0["q"] + NB * (par + 1) + 2 * NB * i)
                sp.dma_start(tile_of(Q_d, 2 * i + par), QS[:, par, :]).then_inc(S(f"q_stored{par}"), 16)

        def load_memory(h):
            sp.dma_start(KL[:, h % 2], K_d[2 * h:2 * h + 2].rearrange("e p m -> p e m")
                         ).then_inc(S(f"memory_in{h % 2}"), 16)
            sp.dma_start(VL[:, h % 2], VV_d[2 * h:2 * h + 2].rearrange("e p m d -> p e m d")
                         ).then_inc(S(f"memory_in{h % 2}"), 16)

        def load_queries(n):
            h, b = divmod(n, NB)
            sp.dma_start(QL[:, n % 2], Q_d[2 * h:2 * h + 2, :, blk(b)].rearrange("e p t -> p e t")
                         ).then_inc(S(f"queries_in{n % 2}"), 16)

        queries(0)
        for par in range(2):
            sp.wait_ge(S(f"kv_stored{par}"), 128)
            sp.wait_ge(S(f"q_stored{par}"), 16)
        for n in range(2):
            load_memory(n)
        sp.wait_ge(S("rms"), 2 * NB)
        for n in range(2):
            load_queries(n)
        with nc.sync.Fori(1, 4) as i:
            queries(i)
        for par in range(2):
            sp.wait_ge(S(f"q_stored{par}"), 64)
        for n in range(2, HEADS * NB):
            h, b = divmod(n, NB)
            sp.wait_ge(S("scores"), 2 * (n - 1))
            load_queries(n)
            if b == 0 and h >= 2:
                sp.wait_ge(S("att_out"), 2 * NB * (h - 1))
                load_memory(h)
        with loop(nc.sync, 4) as i:
            for par in range(2):
                weights(SLOT0["xo"] + par + 2, par, i)
        with loop(nc.sync, (NSLOT - 2 - SLOT0["ffn"]) // 2) as i:
            for par in range(2):
                weights(SLOT0["ffn"] + par + 2, par, i)
        for k in range(KT):
            sp.wait_ge(S("y_out"), k + 1)
            sp.dma_start(io["yT"][k], YO[:, k % 2, :]).then_inc(S(f"out_stored{k % 2}"), 16)
        for par in range(2):
            sp.wait_ge(S(f"out_stored{par}"), 16 * KT // 2)

    @block.gpsimd
    def _(pool):
        step = Count(S("pool_step"))

        def then(ins):
            step.up(ins)
            pool.wait_ge(step.sem, step.n)

        def tt(out, a, b, op):
            then(nc.gpsimd.tensor_tensor(out, a, b, op))

        pool.wait_ge(S("consts_in"), 8 * 16)
        pool.wait_ge(S("params_made"), 1)
        pool.wait_ge(S("rms"), NB)
        AR, AI, CR, CI, CIS = (PA[:, j, :] for j in (3, 4, 5, 6, 7))
        T1, T2 = TX[:, 0:GD], TX[:, GD:2 * GD]
        plus, minus = sgn[:, 0:1], sgn[:, 1:2]
        step.up(nc.gpsimd.memset(PR[:, 0, :], 1.0))
        then(nc.gpsimd.memset(PI[:, 0, :], 0.0))
        for k in range(1, NPOW):
            tt(T1, PR[:, k - 1, :], AR, ALU.mult)
            tt(T2, PI[:, k - 1, :], AI, ALU.mult)
            tt(PR[:, k, :], T1, T2, ALU.subtract)
            tt(T1, PR[:, k - 1, :], AI, ALU.mult)
            tt(T2, PI[:, k - 1, :], AR, ALU.mult)
            tt(PI[:, k, :], T1, T2, ALU.add)
        for out, src, n, sign, down in ((PVR, PR, C, 1.0, 0), (PVI, PI, C, plus, 0),
                                        (PWR, PR, NPOW, minus, 1), (PWI, PI, NPOW, -1.0, 1)):
            for d in range(2):
                a = src[:, 0:n, d * GROUPS:(d + 1) * GROUPS]
                then(nc.gpsimd.tensor_scalar(out[:, 0:n, d * GROUPS:(d + 1) * GROUPS],
                                             a[:, ::-1, :] if d == down else a, sign, None, ALU.mult))
        then(nc.gpsimd.tensor_scalar(LR[:], PR[:, C, :], 1.0, None, ALU.mult))
        then(nc.gpsimd.tensor_scalar(LI[:], PI[:, C, :], minus, None, ALU.mult))
        then(nc.gpsimd.tensor_scalar(CIS, CI, plus, None, ALU.mult))

        for d in range(2):
            if d:
                pool.wait_ge(S("bb_stored"), 16)
            for dst, src in ((BX, "BX"), (BY, "BY"), (CX, "CX"), (CY, "CY")):
                pool.dma_start(dst[:], io[src][d]).then_inc(S("bc_in"), 16)
            pool.wait_ge(S("bc_in"), 64 * (d + 1))
            cr, ci = (a[:, d * GROUPS:(d + 1) * GROUPS].unsqueeze(2).to_broadcast([P, GROUPS, GP])
                      for a in (CR, CIS))
            bt = TX[:, 0:GROUPS * GP].rearrange("p (g q) -> p g q", q=GP)
            tt(bt, BY[:], ci, ALU.mult)
            tt(BBX[:], BX[:], cr, ALU.mult)
            tt(BBX[:], BBX[:], bt, ALU.add)
            tt(bt, BX[:], ci, ALU.mult)
            tt(BBY[:], BY[:], cr, ALU.mult)
            tt(BBY[:], BBY[:], bt, ALU.subtract)
            pool.dma_start(BB_d[d], BBX[:]).then_inc(S("bb_stored"), 16)

            with loop(nc.gpsimd, 4) as i:
                step.enter(i, 8)
                for par in range(2):
                    g0 = 8 * i + 4 * par
                    made = 16 * d + 4 * i + 2 * par

                    def powers(a, n):
                        a = a[:, 0:n, bass.ds(d * GROUPS + g0, 4)]
                        return a.rearrange("p k g -> p g k").unsqueeze(3).to_broadcast([P, 4, n, GP])

                    def values(a, n):
                        return a[:, bass.ds(g0, 4), :].unsqueeze(2).to_broadcast([P, 4, n, GP])

                    def cut(a, n):
                        return a[:, 0:4 * n * GP].rearrange("p (g k q) -> p g k q", g=4, q=GP)

                    v, w = cut(TB[:, par, :], C), cut(TC[:, par, :], NPOW)
                    pool.wait_ge(S(f"tables_stored{par}"), 32 * (4 * d + i))
                    tt(v, values(BBX, C), powers(PVR, C), ALU.mult)
                    tt(cut(TX, C), values(BBY, C), powers(PVI, C), ALU.mult)
                    nc.gpsimd.tensor_tensor(v, v, cut(TX, C), ALU.add).then_inc(S("tables_made"), 1)
                    pool.wait_ge(S("tables_made"), made + 1)
                    pool.dma_start(V_d[:, bass.ds(g0, 4), d, :],
                                   TB[:, par, 0:4 * P].rearrange("p (g c) -> p g c", g=4)
                                   ).then_inc(S(f"tables_stored{par}"), 16)
                    tt(w, values(CX, NPOW), powers(PWR, NPOW), ALU.mult)
                    tt(cut(TX, NPOW), values(CY, NPOW), powers(PWI, NPOW), ALU.mult)
                    nc.gpsimd.tensor_tensor(w, w, cut(TX, NPOW), ALU.add).then_inc(S("tables_made"), 1)
                    pool.wait_ge(S("tables_made"), made + 2)
                    pool.dma_start(W_d[:, bass.ds(g0, 4), d, :],
                                   TC[:, par, :].rearrange("p (g c) -> p g c", g=4)
                                   ).then_inc(S(f"tables_stored{par}"), 16)
                step.leave(4)
        with loop(nc.gpsimd, 4) as i:
            for b in range(2):
                pool.wait_ge(S(f"glu_in{b}"), 48 * (i + 1))
                nc.gpsimd.tensor_tensor(G2L[:, b, :], G2L[:, b, :], COL[:, b, :], ALU.mult
                                        ).then_inc(S("gated_conv"), 1)

    @block.tensor
    def _(pe):
        def product(out, w, x, first, last):
            pe_mm = nc.tensor.matmul
            pe_mm(out, w[1], x[0], start=first, stop=False)
            pe_mm(out, w[0], x[1], start=False, stop=False)
            return pe_mm(out, w[0], x[0], start=False, stop=last)

        def wts(par, c):
            return WHI[:, par, c * P:(c + 1) * P], WLO[:, par, c * P:(c + 1) * P]

        def xin(k, b):
            return XN[:, 0, k, blk(b)], XN[:, 1, k, blk(b)]

        def dense(q, i, each, par, tiles, ins):
            for r, (cols, b) in enumerate((t, b) for t in tiles for b in range(NB)):
                pe.wait_ge(evac, q + r - RING + 1 + each * i)
                for k, c in enumerate(cols):
                    last = product(bank(q + r)[:], wts(par, c), ins(k, b), k == 0, k == len(cols) - 1)
                last.then_inc(res, 1)

        def last_pair(name, norm):
            q = RES0[name] + NB * (KT - 2)
            pe.wait_ge(wlo, SLOT0[name] + KT - 1)
            dense(q, 0, 0, 0, K8, xin)
            q += NB
            pe.wait_ge(wlo, SLOT0[name] + KT)
            for k in range(KT):
                for b in range(NB):
                    if k == 0:
                        pe.wait_ge(evac, q + b - RING + 1)
                    last = product(bank(q + b)[:], wts(1, k), xin(k, b), k == 0, k == KT - 1)
                    if k == KT - 1:
                        last.then_inc(res, 1)
                if k < KT - 1:
                    last.then_inc(S("xn_free"), 1)

        def slots(name, times, tiles, ins, first=0):
            per = NB * len(tiles)
            with nc.tensor.Fori(first, times) as i:
                for par in range(2):
                    pe.wait_ge(wlo, SLOT0[name] + par + 1 + 2 * i)
                    dense(RES0[name] + per * par, i, 2 * per, par, tiles, ins)

        K8 = [list(range(KT))]
        K4 = [list(range(HT)), list(range(HT, 2 * HT))]

        def first_pair(name, ready, norm):
            q = RES0[name]
            pe.wait_ge(wlo, SLOT0[name] + 1)
            pe.wait_ge(evac, q - NB if norm else q)
            for k in range(KT):
                pe.wait_ge(*ready(k))
                for b in range(NB):
                    last = product(bank(q + b)[:], wts(0, k), xin(k, b), k == 0, k == KT - 1)
                    if k == KT - 1:
                        last.then_inc(res, 1)
            if norm is not None:
                sums(norm, ACC2)
            pe.wait_ge(wlo, SLOT0[name] + 2)
            dense(q + NB, 0, 0, 1, K8, xin)

        def sums(norm, acc):
            if norm:
                pe.wait_ge(S("squares_added"), KT * norm)
            else:
                pe.wait_ge(S("x_acc"), KT)
            for b in range(NB):
                if b == 2:
                    pe.wait_ge(S("rms"), NB * norm + 1)
                nc.tensor.matmul(PS[6 + b % 2][:], ones[:], acc[:, blk(b)], start=True, stop=True
                                 ).then_inc(S("sums"), 1)

        pe.wait_ge(S("consts_in"), 8 * 16)

        def key(i, par):
            n = 2 * i + par
            pe.wait_ge(wlo, n + 1)
            if not isinstance(i, int) or i:
                pe.wait_ge(evac, n - 1)
            for k in range(KT):
                last = product(PS[par][:], wts(par, k), (MN[:, 0, k, :], MN[:, 1, k, :]), k == 0, k == KT - 1)
            last.then_inc(res, 1)

        def value(half, j):
            par = j % 2
            pe.wait_ge(wlo, KT + 4 * half + j + 1)
            for m in range(M2 // P):
                rows = slice(m * P, (m + 1) * P)
                for kk in range(2):
                    k, cols = 2 * j + kk, slice(kk * BLK, (kk + 1) * BLK)
                    last = product(PS[VBANKS[half][m]][:], (MN[:, 0, k, rows], MN[:, 1, k, rows]),
                                   (WHI[:, par, cols], WLO[:, par, cols]), k == 0, k == KT - 1)
            last.then_inc(res, 1)

        pe.wait_ge(S("mem_lo"), KT)
        key(0, 0)
        pe.wait_ge(S("mem_acc"), KT)
        nc.tensor.matmul(PS[6][:], ones[:], MACC[:], start=True, stop=True).then_inc(S("mem_sums"), 1)
        for m in range(M2 // P):
            last = nc.tensor.matmul(PS[7][:, m:m + 1], MACC[:, m * P:(m + 1) * P], ones[:, 0:1],
                                    start=True, stop=True)
        last.then_inc(S("mem_sums"), 1)
        key(0, 1)
        with nc.tensor.Fori(1, 4) as i:
            key(i, 0)
            key(i, 1)
        pe.wait_ge(S("mem_rms"), 2)
        sums(0, ACC)
        for half in range(2):
            if half:
                pe.wait_ge(evac, KT)
                pe.wait_ge(S("rms"), NB)
            for j in range(4):
                value(half, j)

        pe.wait_ge(evac, RES0["u"])
        first_pair("u", lambda k: (S("x_lo"), k + 1), None)
        slots("u", 2, K8, xin, first=1)
        slots("conv", 6, K8, xin)
        pe.wait_ge(S("cin_lo"), NB * HT)
        slots("co", 2, K4, lambda k, b: (CIN[:, k, 0, blk(b)], CIN[:, k, 1, blk(b)]))

        pe.wait_ge(evac, RES0["gate"])
        pe.wait_ge(S("u_in"), 128)

        def s5a(i):
            for par in range(2):
                it = 2 * i + par
                pe.wait_ge(S(f"s5a_in{par}"), 80 * (i + 1))
                for j in range(4):
                    last = nc.tensor.transpose(PS[par][:, j * P:(j + 1) * P], VN[:, par, j, :], ident[:])
                last.then_inc(S("v_turned"), 1)
                if not isinstance(i, int):
                    pe.wait_ge(S("lags_staged"), it - 1)
                for g in range(2):
                    out = PS[6 + par][0:GP, g * LAGS * GP:(g + 1) * LAGS * GP]
                    (bf, bb), (kf, kb) = ((a[:, par, 2 * g], a[:, par, 2 * g + 1]) for a in (BBL, WK))
                    z = (C - 1) * GP
                    nc.tensor.matmul(out[:, z:z + GP], bb, kb[:, z:], start=True, stop=False)
                    nc.tensor.matmul(out[:, z:z + GP], bf, kf[:, 0:GP], start=False, stop=True)
                    nc.tensor.matmul(out[:, 0:z], bb, kb[:, 0:z], start=True, stop=True)
                    last = nc.tensor.matmul(out[:, z + GP:], bf, kf[:, GP:], start=True, stop=True)
                last.then_inc(S("lags"), 1)
                pe.wait_ge(S("v_staged"), it + 1)
                if not isinstance(i, int):
                    pe.wait_ge(S("h_fwd"), 2 * (it - 1))
                    pe.wait_ge(S("h_bwd"), 2 * (it - 1))
                for g in range(2):
                    u = one(U, 2 * it + g)
                    last = nc.tensor.matmul(PS[2 + par][:, g * NC:(g + 1) * NC], VT[:, par, 2 * g * P:(2 * g + 1) * P],
                                            u, start=True, stop=True)
                last.then_inc(S("states_fwd"), 1)
                for g in range(2):
                    u = one(U, 2 * it + g)
                    out = PS[4 + par][:, g * NC:(g + 1) * NC]
                    w = VT[:, par, (2 * g + 1) * P:(2 * g + 2) * P]
                    last = nc.tensor.matmul(out, w, u, start=True, stop=True)
                last.then_inc(S("states_bwd"), 1)

        s5a(0)
        with nc.tensor.Fori(1, 8) as i:
            s5a(i)

        pe.wait_ge(S("v_staged"), 16)
        pe.wait_ge(S("h_fwd"), 32)
        pe.wait_ge(S("h_bwd"), 32)
        slots("gate", 8, K8, xin)

        pe.wait_ge(evac, RES0["glu"])
        pe.wait_ge(S("scan"), SCAN_STEPS * 5)

        def s5b(i):
            for par in range(2):
                it = 2 * i + par
                pe.wait_ge(S(f"s5b_in{par}"), 48 * (i + 1))
                if not isinstance(i, int):
                    pe.wait_ge(S("y_made"), it - 1)
                for g in range(2):
                    out = PS[par][:, g * NC:(g + 1) * NC]
                    u = one(U, 2 * it + g)
                    for c0, n, slot in ((0, NCP, 0), (NCP, NCS, SLOT_S)):
                        o = out[:, c0:c0 + n]
                        nc.tensor.matmul(o, ML[:, par, g, :], u[:, c0:c0 + n], start=True, stop=False)
                        for d in (1, 0):
                            h = H[:, slot:slot + n, bass.ds(d * GROUPS + 2 * it + g, 1)].rearrange("p s o -> p (s o)")
                            last = nc.tensor.matmul(o[:, ::-1] if d else o,
                                                    WO[:, par, 2 * g + d, :], h, start=False, stop=d == 0)
                last.then_inc(S("s5_out"), 1)

        s5b(0)
        with nc.tensor.Fori(1, 8) as i:
            s5b(i)

        pe.wait_ge(S("y_made"), 16)
        pe.wait_ge(S("y_lo"), HT)
        slots("glu", 4, K4, lambda k, b: (YHL[:, 0, k, blk(b)], YHL[:, 1, k, blk(b)]))
        pe.wait_ge(S("merged_lo"), NB * KT)
        slots("wo", 3, K8, xin)
        last_pair("wo", 1)
        first_pair("q", lambda k: (S("hn_lo"), k + 1), 1)
        slots("q", 4, K8, xin, first=1)

        pe.wait_ge(evac, RES0["xo"])

        def scores(n):
            h, b = divmod(n, NB)
            par, mem = n % 2, slice(b * BLK // T_PROMPT * NMEM, (b * BLK // T_PROMPT + 1) * NMEM)
            pe.wait_ge(S(f"queries_in{par}"), 16 * (n // 2 + 1))
            pe.wait_ge(S(f"memory_in{h % 2}"), 32 * (h // 2 + 1))
            if n >= 2:
                pe.wait_ge(S("exps"), 4 * (n - 1))
            for lt in range(4):
                out = PS[2 * par + lt // 2][:, (lt % 2) * NMEM:(lt % 2 + 1) * NMEM]
                for k in range(2):
                    last = nc.tensor.matmul(out, QL[:, par, k, lt * P:(lt + 1) * P], KL[:, h % 2, k, mem],
                                            start=k == 0, stop=k == 1)
                if lt % 2:
                    last.then_inc(S("scores"), 1)

        def turned(n):
            pe.wait_ge(S("probs"), 4 * (n + 1))
            if n:
                pe.wait_ge(S("pt_staged"), 2 * n)
            for m in range(2):
                for lt in range(4):
                    last = nc.tensor.transpose(PS[4 + m][:, lt * P:(lt + 1) * P],
                                               PB[:, n % 2, lt, m * P:(m + 1) * P], ident[:])
                last.then_inc(S("p_turned"), 1)

        def weighted(n):
            h, b = divmod(n, NB)
            pe.wait_ge(S("pt_staged"), 2 * (n + 1))
            if n:
                pe.wait_ge(S("o_lo"), 2 * n)
            for e in range(2):
                for m in range(2):
                    last = nc.tensor.matmul(PS[6 + e][:], VL[:, h % 2, e, 2 * (b * BLK // T_PROMPT) + m, :],
                                            PT[:, n % 2, m, :], start=m == 0, stop=m == 1)
                last.then_inc(S("att_out"), 1)

        scores(0)
        scores(1)
        for n in range(HEADS * NB):
            turned(n)
            if n + 2 < HEADS * NB:
                scores(n + 2)
            weighted(n)

        pe.wait_ge(S("o_lo"), 2 * HEADS * NB)
        pe.wait_ge(S("exps"), 4 * HEADS * NB)
        slots("xo", 3, K8, xin)
        last_pair("xo", 2)

        def down(c, part, each_q):
            par = part
            q = RES0["ffn"] + 4 * NB + part * 4 * NB
            pe.wait_ge(wlo, SLOT0["ffn"] + 5 + part + CH_SLOTS * c)
            for e0 in (0, 2):
                for k in range(2):
                    for r, (e, b) in enumerate((e, b) for e in (e0, e0 + 1) for b in range(NB)):
                        n = q + 3 * e0 + r
                        if k == 0:
                            pe.wait_ge(evac, n - RING + 1 + CH_RES * c)
                        pe.wait_ge(S("act_lo"), NB * k + b + 1 + 2 * NB * c)
                        last = product(bank(n)[:], wts(par, 2 * e + k), (AF[:, 0, k, blk(b)], AF[:, 1, k, blk(b)]),
                                       k == 0, k == 1)
                        if k == 1:
                            last.then_inc(res, 1)

        def chunk(c):
            for f in range(4):
                if isinstance(c, int) and c == 0 and f < 2:
                    continue
                pe.wait_ge(wlo, SLOT0["ffn"] + f + 1 + CH_SLOTS * c)
                dense(RES0["ffn"] + NB * f, c, CH_RES, f % 2, K8, xin)
            down(c, 0, None)
            down(c, 1, None)

        first_pair("ffn", lambda k: (S("hn_lo"), KT + k + 1), 2)
        chunk(0)
        with nc.tensor.Fori(1, CHUNKS) as c:
            chunk(c)
        sums(3, ACC2)

    @block.scalar
    def _(act):
        def copy(out, in_, scale=1.0):
            return nc.scalar.activation(out, in_, ACT.Copy, scale=scale)

        def hi(m, q, i=0, each=0, di=1):
            par = m % 2
            act.wait_ge(raw[par], 16 * (m // 2 + 1) + 16 * di * i)
            act.wait_ge(res, q + each * i)
            copy(WHI[:, par, :], WR[:, par, :]).then_inc(whi, 1)

        def apart():
            act.wait_ge(whi, 1)

        def root(out, in_):
            return nc.scalar.activation(out, in_, ACT.Abs_reciprocal_sqrt, scale=1.0 / D, bias=epsc[:, 0:1])

        def roots(norm):
            for b in range(NB):
                act.wait_ge(S("sums"), NB * norm + b + 1)
                root(RB[:, blk(b)], PS[6 + b % 2][:]).then_inc(S("root"), 1)

        act.wait_ge(S("angles"), 2)
        nc.scalar.activation(PA[:, 9, :], PA[:, 9, :], ACT.Sin).then_inc(S("sines"), 1)
        nc.scalar.activation(PA[:, 10, :], PA[:, 10, :], ACT.Sin).then_inc(S("sines"), 1)

        act.wait_ge(S("consts_in"), 8 * 16)
        for k in range(KT):
            if k % 4 == 0:
                act.wait_ge(S(f"mem_in{k // 4}"), 16)
            copy(MN[:, 0, k, :], MEM[:, k, :], gains[:, 1, k:k + 1]).then_inc(S("mem_hi"), 1)
            if k >= 2:
                act.wait_ge(S("mem_acc"), k - 1)
            nc.scalar.activation(MSQ[:, k % 2, :], MEM[:, k, :], ACT.Square).then_inc(S("mem_sq"), 1)
        act.wait_ge(raw[0], 16)
        copy(WHI[:, 0, :], WR[:, 0, :]).then_inc(whi, 1)

        def x_tile(i, par):
            n = 2 * i + par
            act.wait_ge(S(f"x_in{par}"), 16 * (i + 1))
            apart()
            copy(one(XN[:, 0], n), XS[:, par, :], gains[:, 0, bass.ds(n, 1)]).then_inc(S("x_hi"), 1)
            if not isinstance(i, int):
                act.wait_ge(S("x_acc"), n - 1)
            nc.scalar.activation(SQ[:, par, :], XS[:, par, :], ACT.Square).then_inc(S("x_sq"), 1)

        act.wait_ge(raw[1], 16)
        copy(WHI[:, 1, :], WR[:, 1, :]).then_inc(whi, 1)
        act.wait_ge(S("mem_sums"), 1)
        root(RM[:], PS[6][:]).then_inc(S("mem_root"), 1)
        act.wait_ge(S("mem_sums"), 2)
        root(rcol[:], PS[7][:, 0:4]).then_inc(S("mem_root"), 1)
        x_tile(0, 0)
        hi(2, 1)
        x_tile(0, 1)
        with nc.scalar.Fori(1, 4) as i:
            hi(1, 0, i, 2)
            x_tile(i, 0)
            hi(2, 1, i, 2)
            x_tile(i, 1)
        roots(0)
        with nc.scalar.Fori(4, 8) as i:
            hi(1, 0, i, 2)
            hi(2, 1, i, 2)

        def hi_pair(name, i, each, par):
            hi(SLOT0[name] + par + 1, RES0[name] + each * par, i, 2 * each)

        for j in range(4):
            hi(SLOT0["u"] + j + 1, RES0["u"] + NB * j)

        with loop(nc.scalar, 2) as i:
            for par in range(2):
                act.wait_ge(S(f"kv_stored{par}"), 128 * i)
            act.wait_ge(S("tables_made"), 32 * i)
            for jj in range(2):
                j = 2 * i + jj
                for part in range(3):
                    m = 3 * jj + part
                    hi(SLOT0["conv"] + m + 1, RES0["conv"] + NB * m, i, 6 * NB, 3)
                    if part == 1:
                        act.wait_ge(S("z"), NB * (jj + 1) + 2 * NB * i)
                        apart()
                        copy(XC[:], Z[:, 1:T + 2], convw[:, bass.ds(j, 1), 1:2].rearrange("p o a -> p (o a)")
                             ).then_inc(S("tap1"), 1)
                    if part == 2:
                        for b in range(NB):
                            n = NB * jj + b
                            act.wait_ge(S("cin"), n + 1 + 2 * NB * i)
                            apart()
                            copy(one(CIN, j)[:, 0, blk(b)], TT[:, n % 2, :]).then_inc(S("cin_hi"), 1)
        with loop(nc.scalar, 2) as i:
            for par in range(2):
                hi_pair("co", i, 6, par)

        def states_away(it, src, d, signal):
            dst = H[:, :, bass.ds(d * GROUPS + 2 * it, 2)].rearrange("p s g -> p g s")
            src = src[:, 0:2 * NC].rearrange("p (g c) -> p g c", g=2)
            for lo, n, c in ((1, NCP, 0), (SLOT_S + 1, NCS, NCP)):
                copy(dst[:, :, lo:lo + n], src[:, :, c:c + n]).then_inc(signal, 1)

        def s5a(i):
            for par in range(2):
                it = 2 * i + par
                act.wait_ge(S("v_turned"), it + 1)
                if not isinstance(i, int):
                    act.wait_ge(S("states_bwd"), it - 1)
                copy(VT[:, par, :], PS[par][:]).then_inc(S("v_staged"), 1)
                act.wait_ge(S("states_fwd"), it + 1)
                apart()
                states_away(it, PS[2 + par], 0, S("h_fwd"))

        s5a(0)
        with nc.scalar.Fori(1, 8) as i:
            s5a(i)

        def gate(i):
            for par in range(2):
                hi_pair("gate", i, NB, par)
                act.wait_ge(S(f"gate_stored{par}"), 16 * i)
                copy(bcol[:, par:par + 1], bgate[:, bass.ds(2 * i + par, 1)]).then_inc(S("bias"), 1)
                act.wait_ge(S("bias"), 2 * i + par + 1)
                for b in range(NB):
                    n = NB * par + b
                    act.wait_ge(evac, RES0["gate"] + n + 1 + 2 * NB * i)
                    nc.scalar.activation(GS[:, par, blk(b)], TG[:, n % 2, :], ACT.Sigmoid, bias=bcol[:, par:par + 1]
                                         ).then_inc(S("gate_made"), 1)

        with loop(nc.scalar, 8) as i:
            gate(i)

        def s5b(i):
            for par in range(2):
                it = 2 * i + par
                act.wait_ge(S("s5_out"), it + 1)
                act.wait_ge(S(f"y_stored{par}"), 16 * i)
                nc.scalar.activation(YS[:, par, :], PS[par][:, 0:2 * NC], ACT.Gelu_apprx_tanh
                                     ).then_inc(S("y_made"), 1)

        with loop(nc.scalar, 8) as i:
            s5b(i)
        for k in range(HT):
            act.wait_ge(S(f"y_in{k % 2}"), 128 * (k // 2 + 1))
            copy(YHL[:, 0, k].rearrange("p (c t) -> p c t", t=C), YL[:, k % 2].rearrange("p t c -> p c t")
                 ).then_inc(S("y_hi"), 1)

        with loop(nc.scalar, 4) as i:
            for par in range(2):
                j = 2 * i + par
                hi_pair("glu", i, 6, par)
                for b in range(NB):
                    act.wait_ge(evac, RES0["glu"] + 6 * par + b + 1 + 12 * i)
                    nc.scalar.activation(SB[:, blk(b)], SB[:, blk(b)], ACT.Sigmoid).then_inc(S("glu_gate"), 1)
                for b in range(NB):
                    act.wait_ge(S("merged"), NB * par + b + 1 + 2 * NB * i)
                    apart()
                    copy(one(XN[:, 0], j)[:, blk(b)], SB[:, blk(b)]).then_inc(S("merged_hi"), 1)

        def residual(name, norm):
            def pair(i):
                for par in range(2):
                    j = 2 * i + par
                    hi_pair(name, i, NB, par)
                    act.wait_ge(evac, RES0[name] + NB * (par + 1) + 2 * NB * i)
                    if not isinstance(i, int):
                        act.wait_ge(S("squares_added"), KT * (norm - 1) + j - 1)
                        apart()
                    nc.scalar.activation(SQ2[:, par, :], one(HR, j), ACT.Square).then_inc(S("squares"), 1)
            pair(0)
            with nc.scalar.Fori(1, 3) as i:
                pair(i)
            hi_pair(name, 3, NB, 0)
            square(norm, KT - 2, RES0[name] + NB * (KT - 1), SQ2[:, 0, :])
            hi_pair(name, 3, NB, 1)

        def square(norm, k, made, out):
            act.wait_ge(evac, made)
            if k >= 2:
                act.wait_ge(S("squares_added"), KT * (norm - 1) + k - 1)
            nc.scalar.activation(out, HR[:, k, :], ACT.Square).then_inc(S("squares"), 1)

        def split_residual(name, norm):
            gain = gains[:, norm + 1, :]
            for k in range(KT):
                if k < KT - 1:
                    act.wait_ge(S("xn_free"), (KT - 1) * (norm - 1) + k + 1)
                else:
                    act.wait_ge(res, RES0[name] + NB * KT)
                    act.wait_ge(evac, RES0[name] + NB * KT)
                copy(XN[:, 0, k, :], HR[:, k, :], gain[:, k:k + 1]).then_inc(S("hn_hi"), 1)
            square(norm, KT - 1, RES0[name] + NB * KT, SQ2[:, 1, :])
            nxt = "q" if norm == 1 else "ffn"
            hi(SLOT0[nxt] + 1, RES0[nxt])
            roots(norm)

        residual("wo", 1)
        split_residual("wo", 1)
        hi_pair("q", 0, NB, 1)
        with nc.scalar.Fori(1, 4) as i:
            for par in range(2):
                hi_pair("q", i, NB, par)

        for par in range(2):
            act.wait_ge(S(f"q_stored{par}"), 64)

        def softmax(n):
            par = n % 2
            for lt in range(4):
                if lt % 2 == 0:
                    act.wait_ge(S("maxima"), 2 * n + lt // 2 + 1)
                nc.scalar.activation(PB[:, par, lt, :], PS[2 * par + lt // 2][:, (lt % 2) * NMEM:(lt % 2 + 1) * NMEM],
                                     ACT.Exp, scale=SCALE, bias=snm[:, par, lt:lt + 1],
                                     accum_out=ssm[:, par, lt:lt + 1]).then_inc(S("exps"), 1)

        softmax(0)
        softmax(1)
        for n in range(HEADS * NB):
            h, b = divmod(n, NB)
            act.wait_ge(S("p_turned"), 2 * n + 2)
            if n >= 2:
                act.wait_ge(S("att_out"), 2 * (n - 1))
            copy(PT[:, n % 2, 1, :], PS[5][:]).then_inc(S("pt_staged"), 1)
            if n + 2 < HEADS * NB:
                softmax(n + 2)
            for e in range(2):
                act.wait_ge(S("att_out"), 2 * n + e + 1)
                copy(XN[:, 0, 2 * h + e, blk(b)], PS[6 + e][:]).then_inc(S("o_hi"), 1)

        residual("xo", 2)
        split_residual("xo", 2)

        def chunk(c, final=False):
            for f in range(4):
                if f or not isinstance(c, int) or c:
                    hi(SLOT0["ffn"] + f + 1, RES0["ffn"] + NB * f, c, CH_RES, 3)
                kk = f // 2
                for b in range(NB):
                    if f % 2 == 0:
                        act.wait_ge(evac, RES0["ffn"] + NB * f + b + 1 + CH_RES * c)
                        nc.scalar.activation(SG[:, blk(b)], TF[:, b % 2, :], ACT.Silu).then_inc(S("silu"), 1)
                    else:
                        act.wait_ge(S("act"), NB * kk + b + 1 + 2 * NB * c)
                        copy(AF[:, 0, kk, blk(b)], TF[:, (b + 1) % 2, :]).then_inc(S("act_hi"), 1)
            for part in range(2):
                if not (final and part):
                    hi(SLOT0["ffn"] + 5 + part, RES0["ffn"] + 4 * NB * (part + 1), c, CH_RES, 3)

        chunk(0)
        with nc.scalar.Fori(1, CHUNKS - 1) as c:
            chunk(c)
        chunk(CHUNKS - 1, final=True)
        q = RES0["ffn"] + CHUNKS * CH_RES - KT * NB
        for k in range(KT):
            act.wait_ge(evac, q + NB * (k + 1))
            if k:
                act.wait_ge(S("squares_added"), 2 * KT + k)
            nc.scalar.activation(SG[:], HR[:, k, :], ACT.Square).then_inc(S("squares"), 1)
        roots(3)

    @block.vector
    def _(dve):
        step = Count(S("vector_step"))

        def then(ins):
            step.up(ins)
            dve.wait_ge(step.sem, step.n)

        V = nc.vector

        def tt(out, a, b, op):
            then(V.tensor_tensor(out, a, b, op))

        def ts(out, a, s1, s2, op0, op1=None):
            then(V.tensor_scalar(out, a, s1, s2, op0, op1) if op1 is not None
                 else V.tensor_scalar(out, a, s1, None, op0))

        def lo(m, di_i=0):
            par = m % 2
            dve.wait_ge(whi, m + 1 + di_i)
            V.tensor_tensor(WLO[:, par, :], WR[:, par, :], WHI[:, par, :].bitcast(F32), ALU.subtract
                            ).then_inc(wlo, 1)

        def rest(out, full, part):
            return V.tensor_tensor(out, full, part.bitcast(F32), ALU.subtract)

        def newton(r, total, scratch):
            t = scratch[:, 0:r.shape[-1]]
            tt(t, r, r, ALU.mult)
            then(V.scalar_tensor_tensor(out=t, in0=total, scalar=D * EPS, in1=t, op0=ALU.add, op1=ALU.mult))
            ts(t, t, -0.5 / D, 1.5, ALU.mult, ALU.add)
            return V.tensor_tensor(r, r, t, ALU.mult)

        def reciprocals(norm):
            for b in range(NB):
                dve.wait_ge(S("root"), NB * norm + b + 1)
                newton(RB[:, blk(b)], PS[6 + b % 2][:], NT if norm else NT0).then_inc(S("rms"), 1)
                dve.wait_ge(S("rms"), NB * norm + b + 1)

        A_RE, A_IM, DT, AR, AI, CR, CI, CIS, E, X9, X10, X11, X12, X13, X14, X15 = (PA[:, j, :] for j in range(16))

        def exp_to(out, x):
            ts(X12, x, 0.5, -87.0, ALU.mult, ALU.max)
            ts(X12, X12, 88.0, None, ALU.min)
            ts(X13, X12, LOG2E, ROUND + 127.0, ALU.mult, ALU.add)
            ts(X14, X13, -(ROUND + 127.0), None, ALU.add)
            then(V.scalar_tensor_tensor(out=X12, in0=X14, scalar=-LN2_HI, in1=X12, op0=ALU.mult, op1=ALU.add))
            then(V.scalar_tensor_tensor(out=X12, in0=X14, scalar=-LN2_LO, in1=X12, op0=ALU.mult, op1=ALU.add))
            ts(X13.bitcast(I32), X13.bitcast(I32), 23, None, ALU.logical_shift_left)
            terms = 9
            ts(X15, X12, 1.0 / math.factorial(terms), None, ALU.mult)
            for n in range(terms - 1, 0, -1):
                then(V.scalar_tensor_tensor(out=X15, in0=X15, scalar=1.0 / math.factorial(n), in1=X12,
                                            op0=ALU.add, op1=ALU.mult))
            then(V.scalar_tensor_tensor(out=X15, in0=X15, scalar=1.0, in1=X13, op0=ALU.add, op1=ALU.mult))
            tt(out, X15, X15, ALU.mult)

        dve.wait_ge(S("params_in"), 48)
        exp_to(DT, DT)
        tt(AR, A_RE, DT, ALU.mult)
        tt(AI, A_IM, DT, ALU.mult)
        ts(X11, AI, 1.0 / (2 * math.pi), ROUND, ALU.mult, ALU.add)
        ts(X11, X11, -ROUND, None, ALU.add)
        for part in TWO_PI:
            then(V.scalar_tensor_tensor(out=AI, in0=X11, scalar=-part, in1=AI, op0=ALU.mult, op1=ALU.add))
        ts(AI, AI, 3.1415925, -3.1415925, ALU.min, ALU.max)
        V.tensor_scalar(X9, AI, 1.0, None, ALU.mult).then_inc(S("angles"), 1)
        V.tensor_scalar(X10, AI, 0.5, None, ALU.mult).then_inc(S("angles"), 1)
        exp_to(E, AR)
        dve.wait_ge(S("sines"), 2)
        tt(X10, X10, X10, ALU.mult)
        ts(X10, X10, -2.0, 1.0, ALU.mult, ALU.add)
        tt(AR, E, X10, ALU.mult)
        tt(AI, E, X9, ALU.mult)
        ts(X11, AR, -1.0, None, ALU.add)
        tt(X12, A_RE, A_RE, ALU.mult)
        tt(X13, A_IM, A_IM, ALU.mult)
        tt(X12, X12, X13, ALU.add)
        then(V.reciprocal(X12, X12))
        tt(X13, X11, A_RE, ALU.mult)
        tt(X14, AI, A_IM, ALU.mult)
        tt(X13, X13, X14, ALU.add)
        tt(CR, X13, X12, ALU.mult)
        tt(X13, AI, A_RE, ALU.mult)
        tt(X14, X11, A_IM, ALU.mult)
        tt(X13, X13, X14, ALU.subtract)
        V.tensor_tensor(CI, X13, X12, ALU.mult).then_inc(S("params_made"), 1)

        V.memset(MACC[:], 0.0).then_inc(S("cleared"), 1)
        V.memset(ACC[:], 0.0).then_inc(S("cleared"), 1)
        dve.wait_ge(S("cleared"), 2)
        dve.wait_ge(S("consts_in"), 8 * 16)
        for k in range(KT):
            dve.wait_ge(S("mem_hi"), k + 1)
            V.scalar_tensor_tensor(out=MN[:, 1, k, :], in0=MEM[:, k, :], scalar=gains[:, 1, k:k + 1],
                                   in1=MN[:, 0, k, :].bitcast(F32), op0=ALU.mult, op1=ALU.subtract
                                   ).then_inc(S("mem_lo"), 1)
            if k:
                dve.wait_ge(S("mem_acc"), k)
            dve.wait_ge(S("mem_sq"), k + 1)
            V.tensor_tensor(MACC[:], MACC[:], MSQ[:, k % 2, :], ALU.add).then_inc(S("mem_acc"), 1)
        lo(0)
        lo(1)

        def kv(i, par):
            n = 2 * i + par
            dve.wait_ge(res, n + 1)
            dve.wait_ge(S(f"kv_stored{par}"), 16 * i)
            V.tensor_tensor(KVS[:, par, :], PS[par][:], RM[:], ALU.mult).then_inc(evac, 1)

        def x_tile(i, par):
            n = 2 * i + par
            dve.wait_ge(S("x_hi"), n + 1)
            V.scalar_tensor_tensor(out=one(XN[:, 1], n), in0=XS[:, par, :], scalar=gains[:, 0, bass.ds(n, 1)],
                                   in1=one(XN[:, 0], n).bitcast(F32), op0=ALU.mult, op1=ALU.subtract
                                   ).then_inc(S("x_lo"), 1)
            dve.wait_ge(S("x_sq"), n + 1)
            dve.wait_ge(S("x_acc"), n)
            V.tensor_tensor(ACC[:], ACC[:], SQ[:, par, :], ALU.add).then_inc(S("x_acc"), 1)

        dve.wait_ge(S("mem_root"), 1)
        newton(RM[:], PS[6][:], NT0).then_inc(S("mem_rms"), 1)
        dve.wait_ge(S("mem_rms"), 1)
        dve.wait_ge(S("mem_root"), 2)
        newton(rcol[:], PS[7][:, 0:4], NT0).then_inc(S("mem_rms"), 1)
        dve.wait_ge(S("mem_rms"), 2)
        x_tile(0, 0)
        kv(0, 0)
        lo(2)
        x_tile(0, 1)
        kv(0, 1)
        with V.Fori(1, 4) as i:
            lo(1, 2 * i)
            x_tile(i, 0)
            kv(i, 0)
            lo(2, 2 * i)
            x_tile(i, 1)
            kv(i, 1)
        reciprocals(0)
        for j in range(8):
            lo(KT + j + 1)
            if j % 4 == 3:
                for m in range(M2 // P):
                    n = KT + j - 3 + m
                    dve.wait_ge(res, KT + j + 1)
                    dve.wait_ge(S(f"kv_stored{n % 2}"), 16 * (n // 2))
                    V.tensor_scalar(KVS[:, n % 2, :], PS[VBANKS[j // 4][m]][:], rcol[:, m:m + 1], None, ALU.mult
                                    ).then_inc(evac, 1)

        def take(q, i=0, each=0):
            dve.wait_ge(res, q + 1 + each * i)
            return bank(q)[:]

        for j in range(4):
            lo(SLOT0["u"] + j + 1)
            if j >= 2:
                dve.wait_ge(S(f"u_stored{j % 2}"), 16)
            for b in range(NB):
                src = take(RES0["u"] + NB * j + b)
                V.tensor_tensor(UB[:, j % 2, :, b * 64:(b + 1) * 64].rearrange("p s c -> p c s"),
                                src.rearrange("p (c s) -> p c s", s=C),
                                RB[:, blk(b)].rearrange("p (c s) -> p c s", s=C), ALU.mult).then_inc(evac, 1)

        for par in range(2):
            dve.wait_ge(S(f"u_stored{par}"), 32)
        for col in (0, T_PROMPT + 1, T + 2):
            step.up(V.memset(Z[:, col:col + 1], 0.0))
        dve.wait_ge(step.sem, step.n)
        with loop(V, 2) as i:
            step.enter(i, 2)
            for jj in range(2):
                j = 2 * i + jj
                q = RES0["conv"] + 9 * jj
                each = 6 * NB
                lo(SLOT0["conv"] + 3 * jj + 1, 6 * i)
                for b in range(NB):
                    V.tensor_tensor(XC[:, zcols(b)], take(q + b, i, each), RB[:, blk(b)], ALU.mult
                                    ).then_inc(evac, 1)
                lo(SLOT0["conv"] + 3 * jj + 2, 6 * i)
                for b in range(NB):
                    V.tensor_tensor(TT[:, b % 2, :], take(q + 3 + b, i, each), RB[:, blk(b)], ALU.mult
                                    ).then_inc(evac, 1)
                    dve.wait_ge(evac, q + 4 + b + each * i)
                    V.tensor_tensor(Z[:, b * BLK + 1 + (b == 2):(b + 1) * BLK + 1 + (b == 2)], TT[:, b % 2, :],
                                    XC[:, zcols(b)], ALU.mult).then_inc(S("z"), 1)
                dve.wait_ge(S("z"), NB * (jj + 1) + 2 * NB * i)
                lo(SLOT0["conv"] + 3 * jj + 3, 6 * i)
                dve.wait_ge(S("tap1"), jj + 1 + 2 * i)
                tap = convw[:, bass.ds(j, 1), :].rearrange("p o a -> p (o a)")
                for w, z in ((0, 0), (2, 2)):
                    then(V.scalar_tensor_tensor(out=XC[:], in0=Z[:, z:z + T + 1], scalar=tap[:, w:w + 1],
                                                in1=XC[:], op0=ALU.mult, op1=ALU.add)) if w == 0 else \
                        V.scalar_tensor_tensor(out=XC[:], in0=Z[:, z:z + T + 1], scalar=tap[:, w:w + 1],
                                               in1=XC[:], op0=ALU.mult, op1=ALU.add).then_inc(S("conv"), 1)
                dve.wait_ge(S("conv"), jj + 1 + 2 * i)

                def cin_lo(b):
                    n = NB * jj + b
                    dve.wait_ge(S("cin_hi"), n + 1 + 2 * NB * i)
                    rest(one(CIN, j)[:, 1, blk(b)], TT[:, n % 2, :], one(CIN, j)[:, 0, blk(b)]
                         ).then_inc(S("cin_lo"), 1)

                for b in range(NB):
                    n = NB * jj + b
                    src = take(q + 6 + b, i, each)
                    if b == 2:
                        dve.wait_ge(S("cin_lo"), n - 1 + 2 * NB * i)
                    V.tensor_tensor(TT[:, n % 2, :], src, RB[:, blk(b)], ALU.mult
                                    ).then_inc(evac, 1)
                    dve.wait_ge(evac, q + 7 + b + each * i)
                    V.tensor_tensor(TT[:, n % 2, :], TT[:, n % 2, :], XC[:, zcols(b)], ALU.mult
                                    ).then_inc(S("cin"), 1)
                    if b:
                        cin_lo(b - 1)
                cin_lo(NB - 1)
            step.leave(2)

        def conv_out(i):
            for par in range(2):
                lo(SLOT0["co"] + par + 1, 2 * i)
                for e in range(2):
                    dve.wait_ge(S(f"co_stored{e}"), 32 * i + 16 * par)
                    for b in range(NB):
                        V.tensor_copy(COS[:, e, blk(b)], take(RES0["co"] + 6 * par + 3 * e + b, i, 12)
                                      ).then_inc(evac, 1)

        with loop(V, 2) as i:
            conv_out(i)

        dve.wait_ge(S("tables_made"), 32)
        tt(DM[0:GP], ident[0:GP, 0:GP].unsqueeze(1).to_broadcast([GP, GROUPS, GP]),
           s5d[0:GP, :].unsqueeze(2).to_broadcast([GP, GROUPS, GP]), ALU.mult)
        for slot in (0, SLOT_S):
            then(V.memset(H[:, slot, :], 0.0))

        def s5a(i):
            for par in range(2):
                it = 2 * i + par
                dve.wait_ge(S("lags"), it + 1)
                dve.wait_ge(S(f"lags_stored{par}"), 16 * i)
                then(V.tensor_copy(LL[0:GP, par], PS[6 + par][0:GP, 0:2 * LAGS * GP].rearrange(
                    "p (g l) -> p g l", g=2)))
                lag0 = LL[0:GP, par, :, (C - 1) * GP:C * GP]
                V.tensor_tensor(lag0, lag0, DM[0:GP, bass.ds(2 * it, 2), :], ALU.add).then_inc(S("lags_staged"), 1)
                dve.wait_ge(S("states_bwd"), it + 1)
                dst = H[:, :, bass.ds(GROUPS + 2 * it, 2)].rearrange("p s g -> p g s")
                src = PS[4 + par][:, 0:2 * NC].rearrange("p (g c) -> p g c", g=2)
                for at_, n, c in ((1, NCP, 0), (SLOT_S + 1, NCS, NCP)):
                    V.tensor_copy(dst[:, :, at_:at_ + n], src[:, :, c:c + n][:, :, ::-1]
                                  ).then_inc(S("h_bwd"), 1)

        with loop(V, 8) as i:
            step.enter(i, 2)
            s5a(i)
            step.leave(8)

        dve.wait_ge(S("h_fwd"), 32)
        dve.wait_ge(S("h_bwd"), 32)
        scan = Count(S("scan"))

        def advance(slot, both):
            def seqs(a, s, p0=0, p1=P):
                a = a[p0:p1, bass.ds(s, SLOT_S + 1 if both else 1), :]
                return a[:, ::SLOT_S, :] if both else a

            n = 2 if both else 1

            def wide(a, p0=0, p1=P):
                return a[p0:p1].unsqueeze(1).to_broadcast([p1 - p0, n, GD])

            half = P // 2
            nxt = seqs(H, slot + 1)
            scan.up(V.tensor_tensor(S1[:, 0:n, :], seqs(H, slot), wide(LR), ALU.mult))
            real = scan.n
            scan.up(V.tensor_tensor(S2[0:half, 0:n, :], seqs(H, slot, half, P), wide(LI, half, P), ALU.mult))
            scan.up(V.tensor_tensor(S2[half:P, 0:n, :], seqs(H, slot, 0, half), wide(LI, 0, half), ALU.mult))
            dve.wait_ge(scan.sem, real)
            scan.up(V.tensor_tensor(nxt, nxt, S1[:, 0:n, :], ALU.add))
            dve.wait_ge(scan.sem, scan.n)
            scan.up(V.tensor_tensor(nxt, nxt, S2[:, 0:n, :], ALU.add))
            dve.wait_ge(scan.sem, scan.n)

        def gates(i, both):
            for par in range(2):
                lo(SLOT0["gate"] + par + 1, 2 * i)
                for b in range(NB):
                    n = NB * par + b
                    src = take(RES0["gate"] + n, i, 2 * NB)
                    if both != "first" or n >= 2:
                        dve.wait_ge(S("gate_made"), n - 1 + 2 * NB * i)
                    V.tensor_tensor(TG[:, n % 2, :], src, RB[:, blk(b)], ALU.mult).then_inc(evac, 1)
                for s in range(8):
                    advance(16 * i + 8 * par + s, both is not False)

        gates(0, "first")
        with V.Fori(1, 4) as i:
            scan.enter(i - 1, 80)
            gates(i, True)
            scan.leave(3)
        with V.Fori(4, 8) as i:
            scan.enter(i - 4, 80)
            gates(i, False)
            scan.leave(4)
        assert scan.n == 5 * SCAN_STEPS

        for k in range(HT):
            dve.wait_ge(S("y_hi"), k + 1)
            V.tensor_tensor(YHL[:, 1, k].rearrange("p (c t) -> p c t", t=C),
                            YL[:, k % 2].rearrange("p t c -> p c t"),
                            YHL[:, 0, k].rearrange("p (c t) -> p c t", t=C).bitcast(F32), ALU.subtract
                            ).then_inc(S("y_lo"), 1)

        with loop(V, 4) as i:
            step.enter(i, 2 * NB)
            for par in range(2):
                j = 2 * i + par
                q = RES0["glu"] + 6 * par
                lo(SLOT0["glu"] + par + 1, 2 * i)
                dve.wait_ge(S("merged_lo"), NB * par + 2 * NB * i)
                for b in range(NB):
                    V.tensor_copy(SB[:, blk(b)], take(q + b, i, 12)).then_inc(evac, 1)

                def merged_lo(b):
                    n = NB * par + b
                    dve.wait_ge(S("merged_hi"), n + 1 + 2 * NB * i)
                    rest(one(XN[:, 1], j)[:, blk(b)], SB[:, blk(b)], one(XN[:, 0], j)[:, blk(b)]
                         ).then_inc(S("merged_lo"), 1)

                for b in range(NB):
                    n = NB * par + b
                    src = take(q + NB + b, i, 12)
                    dve.wait_ge(S("glu_gate"), n + 1 + 2 * NB * i)
                    V.tensor_tensor(SB[:, blk(b)], src, SB[:, blk(b)], ALU.mult).then_inc(evac, 1)
                    dve.wait_ge(evac, q + NB + b + 1 + 12 * i)
                    dve.wait_ge(S(f"glu_in{par}"), 48 * (i + 1))
                    tt(SB[:, blk(b)], SB[:, blk(b)], G1L[:, par, blk(b)], ALU.mult)
                    dve.wait_ge(S("gated_conv"), j + 1)
                    V.tensor_tensor(SB[:, blk(b)], SB[:, blk(b)], G2L[:, par, blk(b)], ALU.add
                                    ).then_inc(S("merged"), 1)
                    if b:
                        merged_lo(b - 1)
                merged_lo(NB - 1)
            step.leave(4)

        def add_squares(norm, k, sq):
            dve.wait_ge(S("squares"), KT * (norm - 1) + k + 1)
            dve.wait_ge(S("squares_added"), KT * (norm - 1) + k)
            V.tensor_tensor(ACC2[:], ACC2[:], sq, ALU.add).then_inc(S("squares_added"), 1)

        def residual(name, norm, first):
            def pair(i):
                for par in range(2):
                    j = 2 * i + par
                    lo(SLOT0[name] + par + 1, 2 * i)
                    if first:
                        dve.wait_ge(S(f"xr_in{par}"), 16 * (i + 1))
                    for b in range(NB):
                        src = take(RES0[name] + NB * par + b, i, 2 * NB)
                        h = one(HR, j)[:, blk(b)]
                        V.tensor_tensor(h, src, XR[:, par, blk(b)] if first else h, ALU.add).then_inc(evac, 1)
                    if par or not isinstance(i, int):
                        add_squares(norm, j - 1, SQ2[:, 1 - par, :])
            then(V.memset(ACC2[:], 0.0))
            pair(0)
            with V.Fori(1, 3) as i:
                pair(i)

            def last(j):
                for b in range(NB):
                    src = take(RES0[name] + NB * j + b)
                    if first and b == 0:
                        dve.wait_ge(S(f"xr_in{j % 2}"), 16 * (j // 2 + 1))
                    h = HR[:, j, blk(b)]
                    V.tensor_tensor(h, src, XR[:, j % 2, blk(b)] if first else h, ALU.add).then_inc(evac, 1)

            def split(k):
                dve.wait_ge(S("hn_hi"), KT * (norm - 1) + k + 1)
                V.scalar_tensor_tensor(out=XN[:, 1, k, :], in0=HR[:, k, :], scalar=gains[:, norm + 1, k:k + 1],
                                       in1=XN[:, 0, k, :].bitcast(F32), op0=ALU.mult, op1=ALU.subtract
                                       ).then_inc(S("hn_lo"), 1)

            lo(SLOT0[name] + KT - 1)
            last(KT - 2)
            add_squares(norm, KT - 3, SQ2[:, 1, :])
            lo(SLOT0[name] + KT)
            split(0)
            add_squares(norm, KT - 2, SQ2[:, 0, :])
            for k in range(1, KT - 1):
                split(k)
            last(KT - 1)
            split(KT - 1)
            lo(SLOT0["q" if norm == 1 else "ffn"] + 1)
            add_squares(norm, KT - 1, SQ2[:, 1, :])
            reciprocals(norm)

        dve.wait_ge(S("merged_lo"), NB * KT)
        residual("wo", 1, True)

        def queries(i, par):
            dve.wait_ge(S(f"q_stored{par}"), 16 * i)
            for b in range(NB):
                V.tensor_tensor(QS[:, par, blk(b)], take(RES0["q"] + NB * par + b, i, 2 * NB), RB[:, blk(b)],
                                ALU.mult).then_inc(evac, 1)

        queries(0, 0)
        lo(SLOT0["q"] + 2)
        queries(0, 1)
        with V.Fori(1, 4) as i:
            for par in range(2):
                lo(SLOT0["q"] + par + 1, 2 * i)
                queries(i, par)

        def maxima(n):
            par = n % 2
            for half in range(2):
                dve.wait_ge(S("scores"), 2 * n + half + 1)
                lts = slice(2 * half, 2 * half + 2)
                then(V.reduce_max(smx[:, par, lts], PS[2 * par + half][:].rearrange("p (l m) -> p l m", l=2), AX.X))
                V.tensor_scalar(snm[:, par, lts], smx[:, par, lts], -SCALE, None, ALU.mult).then_inc(S("maxima"), 1)

        def probs(n):
            par = n % 2
            dve.wait_ge(S("exps"), 4 * (n + 1))
            then(V.reciprocal(sri[:, par, :], ssm[:, par, :]))
            for lt in range(4):
                V.tensor_scalar(PB[:, par, lt, :], PB[:, par, lt, :], sri[:, par, lt:lt + 1], None, ALU.mult
                                ).then_inc(S("probs"), 1)

        for n in range(2):
            maxima(n)
            probs(n)
        for n in range(HEADS * NB):
            h, b = divmod(n, NB)
            dve.wait_ge(S("p_turned"), 2 * n + 1)
            if n >= 2:
                dve.wait_ge(S("att_out"), 2 * (n - 1))
            V.tensor_copy(PT[:, n % 2, 0, :], PS[4][:]).then_inc(S("pt_staged"), 1)
            if n + 2 < HEADS * NB:
                maxima(n + 2)
            for e in range(2):
                dve.wait_ge(S("o_hi"), 2 * n + e + 1)
                V.tensor_tensor(XN[:, 1, 2 * h + e, blk(b)], PS[6 + e][:], XN[:, 0, 2 * h + e, blk(b)].bitcast(F32),
                                ALU.subtract).then_inc(S("o_lo"), 1)
            if n + 2 < HEADS * NB:
                probs(n + 2)

        residual("xo", 2, False)

        def chunk(c, final=False):
            for f in range(4):
                if f or not isinstance(c, int) or c:
                    lo(SLOT0["ffn"] + f + 1, CH_SLOTS * c)
                kk, q = f // 2, RES0["ffn"] + NB * f

                def act_lo(b):
                    dve.wait_ge(S("act_hi"), NB * kk + b + 1 + 2 * NB * c)
                    rest(AF[:, 1, kk, blk(b)], TF[:, (b + 1) % 2, :], AF[:, 0, kk, blk(b)]
                         ).then_inc(S("act_lo"), 1)

                for b in range(NB):
                    if f % 2 == 0:
                        src = take(q + b, c, CH_RES)
                        if b == 0:
                            dve.wait_ge(S("act_lo"), NB * kk + 2 * NB * c)
                        if b == 2:
                            dve.wait_ge(S("silu"), NB * kk + 1 + 2 * NB * c)
                        V.tensor_tensor(TF[:, b % 2, :], src, RB[:, blk(b)], ALU.mult).then_inc(evac, 1)
                    else:
                        src = take(q + b, c, CH_RES)
                        dve.wait_ge(S("silu"), NB * kk + min(b + 2, 3) + 2 * NB * c)
                        if b == 2:
                            dve.wait_ge(S("act_lo"), NB * kk + 1 + 2 * NB * c)
                        V.tensor_tensor(TF[:, (b + 1) % 2, :], src, RB[:, blk(b)], ALU.mult).then_inc(evac, 1)
                        dve.wait_ge(evac, q + b + 1 + CH_RES * c)
                        V.tensor_tensor(TF[:, (b + 1) % 2, :], TF[:, (b + 1) % 2, :], SG[:, blk(b)], ALU.mult
                                        ).then_inc(S("act"), 1)
                        if b:
                            act_lo(b - 1)
                if f % 2:
                    act_lo(NB - 1)
            for part in range(2):
                if not (final and part):
                    lo(SLOT0["ffn"] + 5 + part, CH_SLOTS * c)
                for e in range(4):
                    for b in range(NB):
                        q = RES0["ffn"] + 4 * NB + part * 4 * NB + NB * e + b
                        h = HR[:, 4 * part + e, blk(b)]
                        V.tensor_tensor(h, take(q, c, CH_RES), h, ALU.add).then_inc(evac, 1)

        chunk(0)
        with V.Fori(1, CHUNKS - 1) as c:
            chunk(c)
        then(V.memset(ACC2[:], 0.0))
        chunk(CHUNKS - 1, final=True)
        for k in range(KT):
            add_squares(3, k, SG[:])
        reciprocals(3)
        for k in range(KT):
            if k >= 2:
                dve.wait_ge(S(f"out_stored{k % 2}"), 16 * (k // 2))
            V.scalar_tensor_tensor(out=YO[:, k % 2, :], in0=HR[:, k, :], scalar=gains[:, 4, k:k + 1], in1=RB[:],
                                   op0=ALU.mult, op1=ALU.mult).then_inc(S("y_out"), 1)

    block.__exit__(None, None, None)


def kernel(**inputs):
    import numpy as np
    import concourse.bacc as bacc
    from concourse.bass_utils import run_bass_kernel_spmd

    a = {k: np.asarray(v) for k, v in inputs.items()}

    def tiles(w):
        r, c = w.shape
        return w.reshape(r // P, P, c // P, P).transpose(2, 1, 0, 3).reshape(c // P, P, -1)

    w_in = tiles(a["w_in"][0])
    values = a["w_kv"][0][:, D:].reshape(4, 2, P, 2, BLK).transpose(3, 0, 2, 1, 4).reshape(KT, P, SLOTW)
    kv = np.concatenate([tiles(a["w_kv"][0][:, :D]), values])
    u, xc, gb, gc, g = (w_in[i:j] for i, j in ((0, 4), (4, 8), (8, 12), (12, 16), (16, 32)))
    conv = np.stack([xc, gc, gb], 1).reshape(-1, P, SLOTW)
    co = tiles(a["w_conv_out"][0]).reshape(4, 2, P, 512).transpose(0, 2, 1, 3).reshape(4, P, SLOTW)
    glu = np.concatenate([tiles(a["w_glu_b"][0]), tiles(a["w_glu_a"][0])], 2)
    gu = tiles(a["w_gate_up"][0])
    down = a["w_down"][0].reshape(CHUNKS, 2, P, 2, 4, P).transpose(0, 3, 2, 4, 1, 5).reshape(CHUNKS, 2, P, SLOTW)
    ffn = []
    for c in range(CHUNKS):
        ffn += [gu[2 * c], gu[FT + 2 * c], gu[2 * c + 1], gu[FT + 2 * c + 1], down[c, 0], down[c, 1]]
    stream = np.concatenate([kv, u, conv, co, g, glu, tiles(a["w_o"][0]), tiles(a["w_q"][0]),
                             tiles(a["w_xo"][0]), np.stack(ffn)])

    def cols(v):
        return v.reshape(-1, P).T

    def states(v):
        v = v.transpose(2, 0, 1).reshape(NS, GD)
        return np.concatenate([v, v])

    def stacked(re, im):
        return np.concatenate([re, im], 1)

    br, bi = (a[k][0].transpose(0, 2, 1, 3) for k in ("s5_b_re", "s5_b_im"))
    cr, ci = (a[k][0].transpose(0, 3, 1, 2) for k in ("s5_c_re", "s5_c_im"))
    f = np.float32
    half = np.where(np.arange(P) < P // 2, -1.0, 1.0)
    arrays = {
        "W_all": stream,
        "xT": np.concatenate([a["x_prompt"][0].T, a["x_sample"][0].T], 1).reshape(KT, P, T),
        "memT": np.concatenate([a["mem_prompt"][0].T, a["mem_sample"][0].T], 1).reshape(KT, P, M2)
        .transpose(1, 0, 2),
        "gains": np.stack([cols(v) for v in (a["norm_mix_g"][0], a["norm_mem_g"][0], a["norm_xattn_g"][0],
                                             a["norm_ffn_g"][0], a["norm_final_g"])], 1),
        "bgate": cols(a["b_gate"][0]),
        "convw": a["conv_w"][0].reshape(3, HT, P).transpose(2, 1, 0),
        "a_re": states(a["s5_a_re"][0]), "a_im": states(a["s5_a_im"][0]),
        "log_dt": np.repeat(a["s5_log_dt"][0].reshape(1, GD), P, 0),
        "s5_d": a["s5_d"][0].reshape(GROUPS, GP).T,
        "BX": stacked(br, bi), "BY": stacked(bi, br), "CX": stacked(cr, ci), "CY": stacked(ci, cr),
        "ones": np.ones((P, P), f), "ident": np.eye(P, dtype=f), "eps": np.full((P, 1), EPS, f),
        "sgn": np.stack([half, -half], 1).astype(f),
    }
    nc = bacc.Bacc("TRN2", target_bir_lowering=False, num_devices=1, dynamic_dma_scratch_size=1024)
    io = {}
    for name, v in arrays.items():
        arrays[name] = np.ascontiguousarray(v)
        io[name] = nc.dram_tensor(name, v.shape, F32, kind="ExternalInput").ap()
    io["yT"] = nc.dram_tensor("yT", (KT, P, T), F32, kind="ExternalOutput").ap()
    shapes = {"U": (DH, C, NC), "CO": (KT, P, T), "G": (2 * KT, P, T), "V": (P, GROUPS, 2, P),
              "W": (P, GROUPS, 2, NPOW * GP), "BB": (2, P, GROUPS, GP), "L": (GP, GROUPS, LAGS * GP),
              "M": (P, GROUPS, P), "Y": (P, GROUPS, NC), "KV": (2 * KT, P, M2), "Q": (KT, P, T)}
    scratch = {k: nc.dram_tensor(f"scratch_{k}", s, F32).ap() for k, s in shapes.items()}
    build(nc, io, scratch)
    r = run_bass_kernel_spmd(nc, [arrays], core_ids=[0])
    y = np.asarray(r.results[0]["yT"]).reshape(D, T).T
    return y[None, :T_PROMPT], y[None, T_PROMPT:]
```

```python
import math

import concourse.bass as bass
from concourse import mybir

F32 = mybir.dt.float32
F32R = mybir.dt.float32r
I32 = mybir.dt.int32
ALU = mybir.AluOpType
ACT = mybir.ActivationFunctionType
AX = mybir.AxisListType

P = 128
D = 1024
KT = D // P
T_PROMPT, T_SAMPLE = 1024, 512
T = T_PROMPT + T_SAMPLE
BLK = 512
NB = T // BLK
NMEM = 256
M2 = 2 * NMEM
HEADS, HD = 4, 256
DH = 512
HT = DH // P
DFF = 2816
FT = DFF // P
EPS = 1e-6
SCALE = HD ** -0.5
GROUPS, GP, NS = 32, 16, 64
GD = 2 * GROUPS
C = 8
NC = T // C
NCP, NCS = T_PROMPT // C, T_SAMPLE // C
SLOTS = NC + 2
SLOT_S = NCP + 1
LAGS = 2 * C - 1
NPOW = C + 1

SLOTW = 1024
RING = 6

STAGES = [("kv", 16, 1), ("u", 4, 3), ("conv", 12, 3), ("co", 4, 6), ("gate", 16, 3), ("glu", 8, 6),
          ("wo", 8, 3), ("q", 8, 3), ("xo", 8, 3)]
SLOT0, RES0 = {}, {}
_n = _q = 0
for _name, _slots, _per in STAGES:
    SLOT0[_name], RES0[_name] = _n, _q
    _n += _slots
    _q += _slots * _per
SLOT0["ffn"], RES0["ffn"] = _n, _q
CHUNKS = FT // 2
CH_SLOTS, CH_RES = 6, 4 * NB + 2 * 4 * NB
NSLOT = _n + CHUNKS * CH_SLOTS

LOG2E = 1.4426950408889634
LN2_HI, LN2_LO = 0.693359375, -2.12194440e-4
POOL_TILES = 2
QUAD = 4
WROW = 20 * GP
SCAN_STEPS = NCP
ROUND = 12582912.0
TWO_PI = (6.28125, 0.0019350051879882812, 3.0199159819185e-07)


class Count:

    def __init__(self, sem):
        self.sem, self.n, self.raised = sem, 0, 0

    def up(self, ins, k=1):
        ins.then_inc(self.sem, k)
        self.n = self.n + k
        self.raised += k
        return self.n

    def enter(self, i, each):
        self.base, self.each, self.raised = self.n, each, 0
        self.n = self.base + i * each

    def leave(self, times):
        assert self.raised == self.each, (self.raised, self.each)
        self.n = self.base + times * self.each


def build(nc, io, scratch):
    base = 2048
    assert nc.sbuf_base <= base

    off = [base]

    def keep(name, shape, dt=F32):
        t = nc.alloc_sbuf_tensor_at(name, [P] + shape, dt, offset=off[0])
        off[0] += -(-4 * math.prod(shape) // 32) * 32
        return t

    FSQ = nc.alloc_sbuf_tensor_at("FSQ", [P, KT, T], F32, offset=base)
    XN = keep("XN", [2, KT, T], F32R)
    WR = keep("WR", [2, SLOTW])
    WHI = keep("WHI", [2, SLOTW], F32R)
    WLO = keep("WLO", [2, SLOTW], F32R)
    RB = keep("RB", [T])
    ones = keep("ones", [P])
    ident = keep("ident", [P])
    gains = keep("gains", [5, KT])
    bgate = keep("bgate", [2 * KT])
    bcol = keep("bcol", [2])
    convw = keep("convw", [HT, 3])
    epsc = keep("epsc", [1])
    sgn = keep("sgn", [2])
    rcol = keep("rcol", [4])
    LR = keep("LR", [GD])
    LI = keep("LI", [GD])
    s5d = keep("s5d", [GROUPS])
    smx = keep("smx", [2, 4])
    snm = keep("snm", [2, 4])
    ssm = keep("ssm", [2, 4])
    sri = keep("sri", [2, 4])
    w0 = off[0]
    K = 1024

    def at(name, kb, shape, dt=F32):
        assert w0 + kb * K + 4 * math.prod(shape) <= nc.sbuf_usable_end, name
        return nc.alloc_sbuf_tensor_at(name, [P] + shape, dt, offset=w0 + int(kb * K))

    MN = at("MN", 0, [2, KT, M2], F32R)
    MEM = at("MEM", 32, [KT, M2])
    XS = at("XS", 48, [2, T])
    SQ = at("SQ", 60, [2, T])
    ACC = at("ACC", 72, [T])
    MACC = at("MACC", 78, [M2])
    MSQ = at("MSQ", 80, [2, M2])
    KVS = at("KVS", 32, [2, M2])
    VVS = at("VVS", 48, [4, M2])
    RM = at("RM", 84, [M2])
    NT0 = at("NT0", 86, [BLK])
    PA = at("PA", 88, [16, GD])
    BX, BY, CX, CY, BBX, BBY = (at(n, 36 + 2 * i, [GROUPS, GP]) for i, n in
                                enumerate(("BX", "BY", "CX", "CY", "BBX", "BBY")))
    PVR, PVI, PWR, PWI = (at(n, 64.5 + 2.25 * i, [NPOW, GD]) for i, n in
                          enumerate(("PVR", "PVI", "PWR", "PWI")))
    PR, PI = at("PR", 76, [NPOW, GD]), at("PI", 78.25, [NPOW, GD])
    TB = at("TB", 76, [2, 4 * NPOW * GP])
    TC = at("TC", 80.5, [2, 4 * NPOW * GP])
    TX = at("TX", 85, [4 * NPOW * GP])
    UB = at("UB", 48, [2, C, NC])
    CIN = at("CIN", 0, [HT, 2, T], F32R)
    XC = at("XC", 48, [T + 1])
    Z = at("Z", 54.25, [T + 3])
    TT = at("TT", 60.5, [2, BLK])
    COS = at("COS", 72.5, [2, T])
    H = at("H", 0, [SLOTS, GD])
    U = at("U", 48.5, [GROUPS, NC])
    VT = at("VT", 72.5, [2, 4 * P])
    LL = at("LL", 78.5, [2, 2, LAGS * GP])
    DM = at("DM", 82.5, [GROUPS, GP])
    VN = at("VN", 84.5, [2, 4, P])
    WK = at("WK", 88.5, [2, 4, P])
    BBL = at("BBL", 92.5, [2, 4, GP])
    S1, S2 = at("S1", 91, [2, GD]), at("S2", 92, [2, GD])
    TG = at("TG", 72.5, [2, BLK])
    GS = at("GS", 76.5, [T])
    WO = [at(f"WO{n}", kb, [QUAD, 2, P]) for n, kb in enumerate((82.5, 72.5))]
    ML = [at(f"ML{n}", kb, [QUAD, P]) for n, kb in enumerate((86.5, 76.5))]
    YHL = at("YHL", 0, [2, HT, T], F32R)
    YL = at("YL", 48.5, [HT, C, NC])
    G1L, G2L, COL = at("G1L", 48, [2, T]), at("G2L", 60, [2, T]), at("COL", 72, [2, T])
    SB = at("SB", 84, [T])
    HR = at("HR", 0, [KT, T])
    SQ2 = at("SQ2", 48, [2, T])
    ACC2 = at("ACC2", 82, [T])
    NT = at("NT", 88, [BLK])
    QS = at("QS", 66, [2, T])
    XR = at("XR", 66, [2, T])
    KL = at("KL", 48, [2, 2, M2])
    VL = at("VL", 56, [2, 2, 4, P])
    PB = at("PB", 64, [2, 4, NMEM])
    PT = at("PT", 72, [2, 2, BLK])
    QL = at("QL", 80, [2, 2, BLK])
    AF = at("AF", 48, [2, 2, T], F32R)
    SG = at("SG", 72, [T])
    TF = at("TF", 78, [2, BLK])

    U_d, CO_d, G_d, V_d, W_d, BB_d, L_d, M_d, Y_d, KV_d, Q_d = (
        scratch[k] for k in ("U", "CO", "G", "V", "W", "BB", "L", "M", "Y", "KV", "Q"))
    K_d = KV_d[0:KT]
    VV_d = KV_d[KT:2 * KT].rearrange("e p (m d) -> e p m d", d=P)

    VBANKS = [(2, 3, 0, 1), (4, 5, 6, 7)]
    PS = [nc.alloc_psum_tensor(f"bank{i}", [P, BLK], F32) for i in range(8)]

    sem = {}

    def S(name):
        if name not in sem:
            sem[name] = nc.alloc_semaphore(name)
        return sem[name]

    raw = [S("raw_even"), S("raw_odd")]
    whi, wlo = S("weights_hi"), S("weights_lo")
    res, evac = S("results"), S("evacuated")

    def loop(eng, times):
        return eng.Fori(0, times)

    block = nc.Block()
    block.__enter__()

    def zcols(b):
        return slice(b * BLK + (b == 2), (b + 1) * BLK + (b == 2))

    def blk(b):
        return slice(b * BLK, (b + 1) * BLK)

    def bank(q):
        return PS[(q - RES0["u"]) % RING]

    def key_bank(i, par):
        return PS[par + 2 * (isinstance(i, int) and i == 1)]

    def sums_bank(norm, b):
        return PS[0] if norm == 3 and b == 2 else PS[6 + b % 2]

    def one(a, i):
        return a[:, i] if isinstance(i, int) else a[:, bass.ds(i, 1)].rearrange(
            {3: "p o a -> p (o a)", 4: "p o a b -> p (o a) b"}[len(a.shape)])

    def tile_of(a, i):
        return a[i] if isinstance(i, int) else a[bass.ds(i, 1)].rearrange("o p t -> p (o t)")

    @block.sync
    def _(sp):
        def weights(n, parity, i=0):
            if not (isinstance(i, int) and n + 2 * i < 2):
                sp.wait_ge(wlo, n - 1 + 2 * i)
            sp.dma_start(WR[:, parity, :], tile_of(io["W_all"], n + 2 * i)).then_inc(raw[parity], 16)

        sp.dma_start(gains[:], io["gains"]).then_inc(S("gains_in"), 16)
        for k in range(0, KT, 2):
            sp.dma_start(MEM[:, k:k + 2, :], io["memT"][:, k:k + 2, :]).then_inc(S(f"mem_in{k // 2}"), 16)
            if k < 4:
                weights(k // 2, k // 2)
        for dst, src in ((ones, "ones"), (epsc, "eps"), (sgn, "sgn"), (ident, "ident"),
                         (bgate, "bgate"), (convw, "convw")):
            sp.dma_start(dst[:], io[src]).then_inc(S("consts_in"), 16)
        sp.dma_start(s5d[0:GP, :], io["s5_d"]).then_inc(S("consts_in"), 16)
        for k in range(2):
            sp.dma_start(XS[:, k, :], io["xT"][k]).then_inc(S(f"x_in{k}"), 16)
        for j, name in enumerate(("a_re", "a_im", "log_dt")):
            sp.dma_start(PA[:, j, :], io[name]).then_inc(S("params_in"), 16)

        def keys(i, more_x):
            for par in range(2):
                n = 2 * i + par
                weights(SLOT0["kv"] + par + 2, par, i)
                if more_x:
                    sp.wait_ge(S("x_lo"), n + 1)
                    sp.wait_ge(S("x_acc"), n + 1)
                    sp.dma_start(XS[:, par, :], tile_of(io["xT"], n + 2)).then_inc(S(f"x_in{par}"), 16)
                sp.wait_ge(evac, n + 1)
                sp.dma_start(tile_of(KV_d, n), KVS[:, par, :]).then_inc(S(f"kv_stored{par}"), 16)

        with loop(nc.sync, 3) as i:
            keys(i, True)
        keys(3, False)
        def store_values(half):
            for m in range(M2 // P):
                n = KT + 4 * half + m
                sp.wait_ge(evac, n + 1)
                sp.dma_start(VV_d[4 * half:4 * half + 4, :, m, :].rearrange("e p d -> p e d"),
                             VVS[:, m, :].rearrange("p (e d) -> p e d", d=P)).then_inc(S(f"kv_stored{n % 2}"), 16)

        for j in range(8):
            weights(SLOT0["kv"] + KT + j + 2, j % 2)
            if j == 4:
                store_values(0)
        store_values(1)
        for j in range(4):
            weights(SLOT0["u"] + j + 2, j % 2)
            sp.wait_ge(evac, RES0["u"] + NB * (j + 1))
            sp.dma_start(U_d[j * P:(j + 1) * P], UB[:, j % 2]).then_inc(S(f"u_stored{j % 2}"), 16)
        with loop(nc.sync, 6) as i:
            for par in range(2):
                weights(SLOT0["conv"] + par + 2, par, i)
        u_rows = U_d.rearrange("(g p) s c -> p s g c", p=GP)
        for j in range(4):
            weights(SLOT0["co"] + j + 2, j % 2)
            if j == 0:
                sp.wait_ge(S("cin_lo"), NB * HT)
                sp.wait_ge(S("tables_made"), 32)
                for par in range(2):
                    sp.wait_ge(S(f"u_stored{par}"), 32)
                for s in range(C):
                    sp.dma_start(U[GP * s:GP * (s + 1)], u_rows[:, s]).then_inc(S("u_in"), 16)
            for e in range(2):
                sp.wait_ge(evac, RES0["co"] + 6 * j + 3 * (e + 1))
                sp.dma_start(CO_d[2 * j + e], COS[:, e, :]).then_inc(S(f"co_stored{e}"), 16)

        for par in range(2):
            sp.wait_ge(S(f"tables_stored{par}"), 2 * 4 * 32)
        sp.wait_ge(S("bb_stored"), 32)

        def s5a_loads(it, par):
            g = bass.ds(2 * it, 2)
            sem_in = S(f"s5a_in{par}")
            sp.dma_start(VN[:, par], V_d[:, g, :, :].rearrange("p g d c -> p (g d) c")).then_inc(sem_in, 16)
            sp.dma_start(WK[:, par].rearrange("p (g d) c -> p g d c", d=2),
                         W_d[:, g, :].rearrange("p g (d c) -> p g d c", d=2)[:, :, :, 0:P]).then_inc(sem_in, 16)
            sp.dma_start(BBL[:, par].rearrange("p (d g) c -> p d g c", d=2),
                         BB_d[:, :, g, :].rearrange("d p g c -> p d g c")).then_inc(sem_in, 16)

        def s5a(i, last=False):
            for par in range(2):
                it = 2 * i + par
                if not (last and par):
                    sp.wait_ge(S("states_bwd"), it)
                    s5a_loads(it + 1, 1 - par)
                sp.wait_ge(S("lags_staged"), it + 1)
                sp.dma_start(L_d[:, bass.ds(2 * it, 2), :], LL[0:GP, par].rearrange("p a b -> p a b")
                             ).then_inc(S(f"lags_stored{par}"), 16)

        s5a_loads(0, 0)
        with loop(nc.sync, 7) as i:
            s5a(i)
        s5a(7, last=True)
        for par in range(2):
            sp.wait_ge(S(f"lags_stored{par}"), 8 * 16)
        for s in range(C):
            sp.dma_start(M_d[GP * s:GP * (s + 1)],
                         L_d[:, :, (C - 1 - s) * GP:(C - 1 - s) * GP + P]).then_inc(S("m_stored"), 16)

        def s5b_loads(q):
            g = slice(QUAD * q, QUAD * (q + 1))
            sp.dma_start(WO[q % 2][:].rearrange("p g d c -> p g (d c)"), W_d[:, g, GP:GP + 2 * P]
                         ).then_inc(S(f"s5b_in{q % 2}"), 16)
            sp.dma_start(ML[q % 2][:], M_d[:, g, :]).then_inc(S(f"s5b_in{q % 2}"), 16)

        sp.wait_ge(S("m_stored"), 128)
        sp.wait_ge(S("states_bwd"), 16)
        s5b_loads(0)
        with loop(nc.sync, 8) as i:
            for par in range(2):
                weights(SLOT0["gate"] + par + 2, par, i)
                sp.wait_ge(S("gate_made"), 2 * NB * i + NB * (par + 1))
                sp.dma_start(tile_of(G_d, 2 * i + par), GS[:]).then_inc(S("gate_stored"), 16)

        sp.wait_ge(S("gate_stored"), 16 * 2 * KT)
        s5b_loads(1)
        y_rows = Y_d.rearrange("(t p) g c -> g p t c", p=GP)

        def load_y(k):
            sp.wait_ge(S(f"y_stored{k}"), 32)
            for g in range(P // GP):
                sp.dma_start(YL[GP * g:GP * (g + 1), k], y_rows[8 * k + g]).then_inc(S(f"y_in{k}"), 16)

        quads = GROUPS // QUAD
        for q in range(quads):
            sp.wait_ge(S("y_made"), 2 * (q + 1))
            g = slice(QUAD * q, QUAD * (q + 1))
            sp.dma_start(Y_d[:, g, :], U[:, g, :]).then_inc(S(f"y_stored{q // 2}"), 16)
            if q + 2 < quads:
                s5b_loads(q + 2)
            if q % 2 == 0 and q:
                load_y(q // 2 - 1)
        load_y(HT - 1)

        sp.wait_ge(S("y_lo"), HT)

        def glu_loads(j):
            b = j % 2
            if j >= 2:
                sp.wait_ge(S("merged_lo"), NB * (j - 1))
            for dst, src in ((COL, CO_d[j]), (G2L, G_d[KT + j]), (G1L, G_d[j])):
                sp.dma_start(dst[:, b], src).then_inc(S(f"glu_in{b}"), 16)

        glu_loads(0)
        for j in range(KT):
            weights(SLOT0["glu"] + j + 2, j % 2)
            if j + 1 < KT:
                glu_loads(j + 1)

        sp.wait_ge(S("merged_lo"), NB * KT)
        for k in range(2):
            sp.dma_start(XR[:, k, :], io["xT"][k]).then_inc(S(f"xr_in{k}"), 16)

        def wo(i, more_x):
            for par in range(2):
                weights(SLOT0["wo"] + par + 2, par, i)
                if more_x:
                    sp.wait_ge(evac, RES0["wo"] + NB * (par + 1) + 2 * NB * i)
                    sp.dma_start(XR[:, par, :], tile_of(io["xT"], 2 * i + par + 2)).then_inc(S(f"xr_in{par}"), 16)

        with loop(nc.sync, 3) as i:
            wo(i, True)
        wo(3, False)
        def queries(i):
            for par in range(2):
                weights(SLOT0["q"] + par + 2, par, i)
                sp.wait_ge(evac, RES0["q"] + NB * (par + 1) + 2 * NB * i)
                sp.dma_start(tile_of(Q_d, 2 * i + par), QS[:, par, :]).then_inc(S(f"q_stored{par}"), 16)

        def load_memory(h):
            sp.dma_start(KL[:, h % 2], K_d[2 * h:2 * h + 2].rearrange("e p m -> p e m")
                         ).then_inc(S(f"memory_in{h % 2}"), 16)
            sp.dma_start(VL[:, h % 2], VV_d[2 * h:2 * h + 2].rearrange("e p m d -> p e m d")
                         ).then_inc(S(f"memory_in{h % 2}"), 16)

        def load_queries(n):
            h, b = divmod(n, NB)
            sp.dma_start(QL[:, n % 2], Q_d[2 * h:2 * h + 2, :, blk(b)].rearrange("e p t -> p e t")
                         ).then_inc(S(f"queries_in{n % 2}"), 16)

        queries(0)
        for par in range(2):
            sp.wait_ge(S(f"kv_stored{par}"), 128)
            sp.wait_ge(S(f"q_stored{par}"), 16)
        for n in range(2):
            load_memory(n)
        sp.wait_ge(S("rms"), 2 * NB)
        for n in range(2):
            load_queries(n)
        with nc.sync.Fori(1, 4) as i:
            queries(i)
        for par in range(2):
            sp.wait_ge(S(f"q_stored{par}"), 64)
        for n in range(2, HEADS * NB):
            h, b = divmod(n, NB)
            sp.wait_ge(S("scores"), 2 * (n - 1))
            load_queries(n)
            if b == 0 and h >= 2:
                sp.wait_ge(S("att_out"), 2 * NB * (h - 1))
                load_memory(h)
        with loop(nc.sync, 4) as i:
            for par in range(2):
                weights(SLOT0["xo"] + par + 2, par, i)
        with loop(nc.sync, (NSLOT - 2 - SLOT0["ffn"]) // 2) as i:
            for par in range(2):
                weights(SLOT0["ffn"] + par + 2, par, i)
        for b in range(NB):
            for k in range(0, KT, 2):
                if k >= POOL_TILES:
                    sp.wait_ge(S("y_out"), (KT - POOL_TILES) * b + k + 2 - POOL_TILES)
                else:
                    sp.wait_ge(S("y_out_pool"), POOL_TILES * (b + 1))
                sp.dma_start(io["yT"][k:k + 2, :, blk(b)].rearrange("k p t -> p k t"), HR[:, k:k + 2, blk(b)]
                             ).then_inc(S("out_stored"), 16)
        sp.wait_ge(S("out_stored"), 16 * NB * KT // 2)

    @block.gpsimd
    def _(pool):
        step = Count(S("pool_step"))

        def then(ins):
            step.up(ins)
            pool.wait_ge(step.sem, step.n)

        def tt(out, a, b, op):
            then(nc.gpsimd.tensor_tensor(out, a, b, op))

        then(nc.gpsimd.memset(ACC[:], 0.0))
        with loop(nc.gpsimd, 4) as i:
            for par in range(2):
                n = 2 * i + par
                pool.wait_ge(S("x_sq"), n + 1)
                pool.wait_ge(S("x_acc"), n)
                nc.gpsimd.tensor_tensor(ACC[:], ACC[:], SQ[:, par, :], ALU.add).then_inc(S("x_acc"), 1)

        pool.wait_ge(S("consts_in"), 7 * 16)
        pool.wait_ge(S("params_made"), 1)
        pool.wait_ge(S("rms"), NB)
        AR, AI, CR, CI, CIS = (PA[:, j, :] for j in (3, 4, 5, 6, 7))
        T1, T2 = TX[:, 0:GD], TX[:, GD:2 * GD]
        plus, minus = sgn[:, 0:1], sgn[:, 1:2]
        step.up(nc.gpsimd.memset(PR[:, 0, :], 1.0))
        then(nc.gpsimd.memset(PI[:, 0, :], 0.0))
        for k in range(1, NPOW):
            tt(T1, PR[:, k - 1, :], AR, ALU.mult)
            tt(T2, PI[:, k - 1, :], AI, ALU.mult)
            tt(PR[:, k, :], T1, T2, ALU.subtract)
            tt(T1, PR[:, k - 1, :], AI, ALU.mult)
            tt(T2, PI[:, k - 1, :], AR, ALU.mult)
            tt(PI[:, k, :], T1, T2, ALU.add)
        for out, src, n, sign, down in ((PVR, PR, C, 1.0, 0), (PVI, PI, C, plus, 0),
                                        (PWR, PR, NPOW, minus, 1), (PWI, PI, NPOW, -1.0, 1)):
            for d in range(2):
                a = src[:, 0:n, d * GROUPS:(d + 1) * GROUPS]
                then(nc.gpsimd.tensor_scalar(out[:, 0:n, d * GROUPS:(d + 1) * GROUPS],
                                             a[:, ::-1, :] if d == down else a, sign, None, ALU.mult))
        then(nc.gpsimd.tensor_scalar(LR[:], PR[:, C, :], 1.0, None, ALU.mult))
        then(nc.gpsimd.tensor_scalar(LI[:], PI[:, C, :], minus, None, ALU.mult))
        then(nc.gpsimd.tensor_scalar(CIS, CI, plus, None, ALU.mult))

        for d in range(2):
            if d:
                pool.wait_ge(S("bb_stored"), 16)
            for dst, src in ((BX, "BX"), (BY, "BY"), (CX, "CX"), (CY, "CY")):
                pool.dma_start(dst[:], io[src][d]).then_inc(S("bc_in"), 16)
            pool.wait_ge(S("bc_in"), 64 * (d + 1))
            cr, ci = (a[:, d * GROUPS:(d + 1) * GROUPS].unsqueeze(2).to_broadcast([P, GROUPS, GP])
                      for a in (CR, CIS))
            bt = TX[:, 0:GROUPS * GP].rearrange("p (g q) -> p g q", q=GP)
            tt(bt, BY[:], ci, ALU.mult)
            tt(BBX[:], BX[:], cr, ALU.mult)
            tt(BBX[:], BBX[:], bt, ALU.add)
            tt(bt, BX[:], ci, ALU.mult)
            tt(BBY[:], BY[:], cr, ALU.mult)
            tt(BBY[:], BBY[:], bt, ALU.subtract)
            pool.dma_start(BB_d[d], BBX[:]).then_inc(S("bb_stored"), 16)

            with loop(nc.gpsimd, 4) as i:
                step.enter(i, 8)
                for par in range(2):
                    g0 = 8 * i + 4 * par
                    made = 16 * d + 4 * i + 2 * par

                    def powers(a, n):
                        a = a[:, 0:n, bass.ds(d * GROUPS + g0, 4)]
                        return a.rearrange("p k g -> p g k").unsqueeze(3).to_broadcast([P, 4, n, GP])

                    def values(a, n):
                        return a[:, bass.ds(g0, 4), :].unsqueeze(2).to_broadcast([P, 4, n, GP])

                    def cut(a, n):
                        return a[:, 0:4 * n * GP].rearrange("p (g k q) -> p g k q", g=4, q=GP)

                    v, w = cut(TB[:, par, :], C), cut(TC[:, par, :], NPOW)
                    pool.wait_ge(S(f"tables_stored{par}"), 32 * (4 * d + i))
                    tt(v, values(BBX, C), powers(PVR, C), ALU.mult)
                    tt(cut(TX, C), values(BBY, C), powers(PVI, C), ALU.mult)
                    nc.gpsimd.tensor_tensor(v, v, cut(TX, C), ALU.add).then_inc(S("tables_made"), 1)
                    pool.wait_ge(S("tables_made"), made + 1)
                    pool.dma_start(V_d[:, bass.ds(g0, 4), d, :],
                                   TB[:, par, 0:4 * P].rearrange("p (g c) -> p g c", g=4)
                                   ).then_inc(S(f"tables_stored{par}"), 16)
                    tt(w, values(CX, NPOW), powers(PWR, NPOW), ALU.mult)
                    tt(cut(TX, NPOW), values(CY, NPOW), powers(PWI, NPOW), ALU.mult)
                    nc.gpsimd.tensor_tensor(w, w, cut(TX, NPOW), ALU.add).then_inc(S("tables_made"), 1)
                    pool.wait_ge(S("tables_made"), made + 2)
                    pool.dma_start(W_d[:, bass.ds(g0, 4), NPOW * GP * d:NPOW * GP * (d + 1)],
                                   TC[:, par, :].rearrange("p (g c) -> p g c", g=4)
                                   ).then_inc(S(f"tables_stored{par}"), 16)
                step.leave(4)
        with loop(nc.gpsimd, 4) as i:
            for b in range(2):
                pool.wait_ge(S(f"glu_in{b}"), 48 * (i + 1))
                nc.gpsimd.tensor_tensor(G2L[:, b, :], G2L[:, b, :], COL[:, b, :], ALU.mult
                                        ).then_inc(S("gated_conv"), 1)
        pool.wait_ge(S("gained"), POOL_TILES)
        for b in range(NB):
            pool.wait_ge(S("rms"), NB * 3 + b + 1)
            for k in range(POOL_TILES):
                h = HR[:, k, blk(b)]
                nc.gpsimd.tensor_tensor(h, h, RB[:, blk(b)], ALU.mult).then_inc(S("y_out_pool"), 1)

    @block.tensor
    def _(pe):
        def product(out, w, x, first, last):
            pe_mm = nc.tensor.matmul
            pe_mm(out, w[1], x[0], start=first, stop=False)
            pe_mm(out, w[0], x[1], start=False, stop=False)
            return pe_mm(out, w[0], x[0], start=False, stop=last)

        def wts(par, c):
            return WHI[:, par, c * P:(c + 1) * P], WLO[:, par, c * P:(c + 1) * P]

        def xin(k, b):
            return XN[:, 0, k, blk(b)], XN[:, 1, k, blk(b)]

        def dense(q, i, each, par, tiles, ins):
            for r, (cols, b) in enumerate((t, b) for t in tiles for b in range(NB)):
                pe.wait_ge(evac, q + r - RING + 1 + each * i)
                for k, c in enumerate(cols):
                    last = product(bank(q + r)[:], wts(par, c), ins(k, b), k == 0, k == len(cols) - 1)
                last.then_inc(res, 1)

        def last_pair(name, norm):
            q = RES0[name] + NB * (KT - 2)
            pe.wait_ge(wlo, SLOT0[name] + KT - 1)
            dense(q, 0, 0, 0, K8, xin)
            q += NB
            pe.wait_ge(wlo, SLOT0[name] + KT)
            for k in range(KT):
                for b in range(NB):
                    if k == 0:
                        pe.wait_ge(evac, q + b - RING + 1)
                    last = product(bank(q + b)[:], wts(1, k), xin(k, b), k == 0, k == KT - 1)
                    if k == KT - 1:
                        last.then_inc(res, 1)
                if k < KT - 1:
                    last.then_inc(S("xn_free"), 1)

        def slots(name, times, tiles, ins, first=0):
            per = NB * len(tiles)
            with nc.tensor.Fori(first, times) as i:
                for par in range(2):
                    pe.wait_ge(wlo, SLOT0[name] + par + 1 + 2 * i)
                    dense(RES0[name] + per * par, i, 2 * per, par, tiles, ins)

        K8 = [list(range(KT))]
        K4 = [list(range(HT)), list(range(HT, 2 * HT))]

        def first_pair(name, ready, norm=None):
            q = RES0[name]
            pe.wait_ge(wlo, SLOT0[name] + 1)
            pe.wait_ge(evac, q - 4 if name == "u" else q + NB - RING)
            for k in range(KT):
                pe.wait_ge(*ready(k))
                for b in range(NB):
                    last = product(bank(q + b)[:], wts(0, k), xin(k, b), k == 0, k == KT - 1)
                    if k == KT - 1:
                        last.then_inc(res, 1)
            if norm is not None:
                sums(norm, ACC2, range(2))
            pe.wait_ge(wlo, SLOT0[name] + 2)
            q += NB
            for b in range(NB):
                pe.wait_ge(evac, q + b - RING + 1)
                for k in range(KT):
                    last = product(bank(q + b)[:], wts(1, k), xin(k, b), k == 0, k == KT - 1)
                last.then_inc(res, 1)
                if norm is not None and b == 0:
                    sums(norm, ACC2, range(2, NB))

        def first_half_pair(name, ready, ins):
            q = RES0[name]
            pe.wait_ge(wlo, SLOT0[name] + 1)
            pe.wait_ge(evac, q)
            for k in range(HT):
                pe.wait_ge(*ready(k))
                for n in range(2 * NB):
                    last = product(bank(q + n)[:], wts(0, n // NB * HT + k), ins(k, n % NB), k == 0, k == HT - 1)
                    if k == HT - 1:
                        last.then_inc(res, 1)
            pe.wait_ge(wlo, SLOT0[name] + 2)
            dense(q + 2 * NB, 0, 0, 1, K4, ins)

        def sums(norm, acc, blocks=range(NB)):
            if norm:
                pe.wait_ge(S("squares_added"), KT * norm)
            else:
                pe.wait_ge(S("x_acc"), KT)
            for b in blocks:
                if b == 2 and norm < 3:
                    pe.wait_ge(S("rms"), NB * norm + 1)
                nc.tensor.matmul(sums_bank(norm, b)[:], ones[:], acc[:, blk(b)], start=True, stop=True
                                 ).then_inc(S("sums"), 1)

        def key(i, par):
            n = 2 * i + par
            pe.wait_ge(wlo, n + 1)
            if not isinstance(i, int):
                pe.wait_ge(evac, n - 1)
            for k in range(KT):
                if n == 0 if isinstance(i, int) else False:
                    pe.wait_ge(S("mem_lo"), k + 1)
                last = product(key_bank(i, par)[:], wts(par, k), (MN[:, 0, k, :], MN[:, 1, k, :]), k == 0, k == KT - 1)
            last.then_inc(res, 1)

        def value(half, j):
            par = j % 2
            pe.wait_ge(wlo, KT + 4 * half + j + 1)
            for m in range(M2 // P):
                rows = slice(m * P, (m + 1) * P)
                for kk in range(2):
                    k, cols = 2 * j + kk, slice(kk * BLK, (kk + 1) * BLK)
                    last = product(PS[VBANKS[half][m]][:], (MN[:, 0, k, rows], MN[:, 1, k, rows]),
                                   (WHI[:, par, cols], WLO[:, par, cols]), k == 0, k == KT - 1)
            last.then_inc(res, 1)

        key(0, 0)
        pe.wait_ge(S("consts_in"), 7 * 16)
        pe.wait_ge(S("mem_acc"), KT)
        nc.tensor.matmul(PS[6][:], ones[:], MACC[:], start=True, stop=True).then_inc(S("mem_sums"), 1)
        for m in range(M2 // P):
            last = nc.tensor.matmul(PS[7][:, m:m + 1], MACC[:, m * P:(m + 1) * P], ones[:, 0:1],
                                    start=True, stop=True)
        last.then_inc(S("mem_sums"), 1)
        key(0, 1)
        key(1, 0)
        key(1, 1)
        with nc.tensor.Fori(2, 4) as i:
            key(i, 0)
            key(i, 1)
        pe.wait_ge(evac, KT)
        value(0, 0)
        pe.wait_ge(S("mem_rms"), 2)
        sums(0, ACC)
        for j in range(1, 4):
            value(0, j)
        pe.wait_ge(S("rms"), NB)
        for j in range(4):
            value(1, j)

        first_pair("u", lambda k: (S("x_lo"), k + 1))
        slots("u", 2, K8, xin, first=1)
        slots("conv", 6, K8, xin)
        cin = lambda k, b: (CIN[:, k, 0, blk(b)], CIN[:, k, 1, blk(b)])
        first_half_pair("co", lambda k: (S("cin_lo"), NB * (k + 1)), cin)
        slots("co", 2, K4, cin, first=1)

        pe.wait_ge(evac, RES0["gate"])
        pe.wait_ge(S("u_in"), 128)

        def s5a(i):
            for par in range(2):
                it = 2 * i + par
                pe.wait_ge(S(f"s5a_in{par}"), 48 * (i + 1))
                for j in range(4):
                    last = nc.tensor.transpose(PS[par][:, j * P:(j + 1) * P], VN[:, par, j, :], ident[:])
                last.then_inc(S("v_turned"), 1)
                if not isinstance(i, int):
                    pe.wait_ge(S("lags_staged"), it - 1)
                for g in range(2):
                    out = PS[6 + par][0:GP, g * LAGS * GP:(g + 1) * LAGS * GP]
                    bf, bb = BBL[:, par, g], BBL[:, par, 2 + g]
                    kf, kb = WK[:, par, 2 * g], WK[:, par, 2 * g + 1]
                    z = (C - 1) * GP
                    nc.tensor.matmul(out[:, z:z + GP], bb, kb[:, z:], start=True, stop=False)
                    nc.tensor.matmul(out[:, z:z + GP], bf, kf[:, 0:GP], start=False, stop=True)
                    nc.tensor.matmul(out[:, 0:z], bb, kb[:, 0:z], start=True, stop=True)
                    last = nc.tensor.matmul(out[:, z + GP:], bf, kf[:, GP:], start=True, stop=True)
                last.then_inc(S("lags"), 1)
                pe.wait_ge(S("v_staged"), it + 1)
                if not isinstance(i, int):
                    pe.wait_ge(S("h_fwd"), 2 * (it - 1))
                    pe.wait_ge(S("h_bwd"), 2 * (it - 1))
                for g in range(2):
                    u = one(U, 2 * it + g)
                    last = nc.tensor.matmul(PS[2 + par][:, g * NC:(g + 1) * NC], VT[:, par, 2 * g * P:(2 * g + 1) * P],
                                            u, start=True, stop=True)
                last.then_inc(S("states_fwd"), 1)
                for g in range(2):
                    u = one(U, 2 * it + g)
                    out = PS[4 + par][:, g * NC:(g + 1) * NC]
                    w = VT[:, par, (2 * g + 1) * P:(2 * g + 2) * P]
                    last = nc.tensor.matmul(out, w, u, start=True, stop=True)
                last.then_inc(S("states_bwd"), 1)

        s5a(0)
        with nc.tensor.Fori(1, 8) as i:
            s5a(i)

        pe.wait_ge(S("v_staged"), 16)
        pe.wait_ge(S("h_fwd"), 32)
        pe.wait_ge(S("h_bwd"), 32)
        slots("gate", 8, K8, xin)

        pe.wait_ge(evac, RES0["glu"])
        pe.wait_ge(S("scan"), SCAN_STEPS * 5)

        def s5b(i):
            for par in range(2):
                q = 2 * i + par
                pe.wait_ge(S(f"s5b_in{par}"), 32 * (i + 1))
                for g in range(QUAD):
                    n = g // 2
                    if g % 2 == 0 and not isinstance(i, int):
                        pe.wait_ge(S("y_made"), 2 * (q - 1) + n + 1)
                    out = PS[2 * par + n][:, g % 2 * NC:(g % 2 + 1) * NC]
                    u = one(U, QUAD * q + g)
                    for c0, n, slot in ((0, NCP, 0), (NCP, NCS, SLOT_S)):
                        o = out[:, c0:c0 + n]
                        nc.tensor.matmul(o, ML[par][:, g, :], u[:, c0:c0 + n], start=True, stop=False)
                        for d in (1, 0):
                            h = H[:, slot:slot + n, bass.ds(d * GROUPS + QUAD * q + g, 1)].rearrange("p s o -> p (s o)")
                            last = nc.tensor.matmul(o[:, ::-1] if d else o,
                                                    WO[par][:, g, d, :], h, start=False, stop=d == 0)
                    if g % 2:
                        last.then_inc(S("s5_out"), 1)

        s5b(0)
        with nc.tensor.Fori(1, 4) as i:
            s5b(i)

        yin = lambda k, b: (YHL[:, 0, k, blk(b)], YHL[:, 1, k, blk(b)])
        first_half_pair("glu", lambda k: (S("y_lo"), k + 1), yin)
        slots("glu", 4, K4, yin, first=1)
        first_pair("wo", lambda k: (S("merged_lo"), NB * (k + 1)))
        slots("wo", 3, K8, xin, first=1)
        last_pair("wo", 1)
        first_pair("q", lambda k: (S("hn_lo"), k + 1), 1)
        slots("q", 4, K8, xin, first=1)

        pe.wait_ge(evac, RES0["xo"])

        def scores(n):
            h, b = divmod(n, NB)
            par, mem = n % 2, slice(b * BLK // T_PROMPT * NMEM, (b * BLK // T_PROMPT + 1) * NMEM)
            pe.wait_ge(S(f"queries_in{par}"), 16 * (n // 2 + 1))
            pe.wait_ge(S(f"memory_in{h % 2}"), 32 * (h // 2 + 1))
            if n >= 2:
                pe.wait_ge(S("exps"), 4 * (n - 1))
            for lt in range(4):
                out = PS[2 * par + lt // 2][:, (lt % 2) * NMEM:(lt % 2 + 1) * NMEM]
                for k in range(2):
                    last = nc.tensor.matmul(out, QL[:, par, k, lt * P:(lt + 1) * P], KL[:, h % 2, k, mem],
                                            start=k == 0, stop=k == 1)
                if lt % 2:
                    last.then_inc(S("scores"), 1)

        def turned(n):
            pe.wait_ge(S("probs"), 4 * (n + 1))
            if n:
                pe.wait_ge(S("pt_staged"), 2 * n)
            for m in range(2):
                for lt in range(4):
                    last = nc.tensor.transpose(PS[4 + m][:, lt * P:(lt + 1) * P],
                                               PB[:, n % 2, lt, m * P:(m + 1) * P], ident[:])
                last.then_inc(S("p_turned"), 1)

        def weighted(n):
            h, b = divmod(n, NB)
            pe.wait_ge(S("pt_staged"), 2 * (n + 1))
            if n:
                pe.wait_ge(S("o_lo"), 2 * n)
            for e in range(2):
                for m in range(2):
                    last = nc.tensor.matmul(PS[6 + e][:], VL[:, h % 2, e, 2 * (b * BLK // T_PROMPT) + m, :],
                                            PT[:, n % 2, m, :], start=m == 0, stop=m == 1)
                last.then_inc(S("att_out"), 1)

        scores(0)
        scores(1)
        for n in range(HEADS * NB):
            turned(n)
            if n + 2 < HEADS * NB:
                scores(n + 2)
            weighted(n)

        pe.wait_ge(S("o_lo"), 2 * HEADS * NB)
        pe.wait_ge(S("exps"), 4 * HEADS * NB)
        slots("xo", 3, K8, xin)
        last_pair("xo", 2)

        def down(c, part, each_q):
            par = part
            q = RES0["ffn"] + 4 * NB + part * 4 * NB
            pe.wait_ge(wlo, SLOT0["ffn"] + 5 + part + CH_SLOTS * c)
            for e0 in (0, 2):
                for k in range(2):
                    for r, (e, b) in enumerate((e, b) for e in (e0, e0 + 1) for b in range(NB)):
                        n = q + 3 * e0 + r
                        if k == 0:
                            pe.wait_ge(evac, n - RING + 1 + CH_RES * c)
                        pe.wait_ge(S("act_lo"), NB * k + b + 1 + 2 * NB * c)
                        last = product(bank(n)[:], wts(par, 2 * e + k), (AF[:, 0, k, blk(b)], AF[:, 1, k, blk(b)]),
                                       k == 0, k == 1)
                        if k == 1:
                            last.then_inc(res, 1)

        def chunk(c):
            for f in range(4):
                if isinstance(c, int) and c == 0 and f < 2:
                    continue
                pe.wait_ge(wlo, SLOT0["ffn"] + f + 1 + CH_SLOTS * c)
                dense(RES0["ffn"] + NB * f, c, CH_RES, f % 2, K8, xin)
            down(c, 0, None)
            down(c, 1, None)

        first_pair("ffn", lambda k: (S("hn_lo"), KT + k + 1), 2)
        chunk(0)
        with nc.tensor.Fori(1, CHUNKS) as c:
            chunk(c)
        sums(3, ACC2)

    @block.scalar
    def _(act):
        def copy(out, in_, scale=1.0):
            return nc.scalar.activation(out, in_, ACT.Copy, scale=scale)

        def hi(m, q, i=0, each=0, di=1):
            par = m % 2
            act.wait_ge(raw[par], 16 * (m // 2 + 1) + 16 * di * i)
            act.wait_ge(res, q + each * i)
            copy(WHI[:, par, :], WR[:, par, :]).then_inc(whi, 1)

        def apart():
            act.wait_ge(whi, 1)

        def root(out, in_):
            return nc.scalar.activation(out, in_, ACT.Abs_reciprocal_sqrt, scale=1.0 / D, bias=epsc[:, 0:1])

        def roots(norm):
            for b in range(NB):
                act.wait_ge(S("sums"), NB * norm + b + 1)
                root(RB[:, blk(b)], sums_bank(norm, b)[:]).then_inc(S("root"), 1)

        act.wait_ge(raw[0], 16)
        copy(WHI[:, 0, :], WR[:, 0, :]).then_inc(whi, 1)
        act.wait_ge(S("gains_in"), 16)
        for k in range(KT):
            if k % 2 == 0:
                act.wait_ge(S(f"mem_in{k // 2}"), 16)
            copy(MN[:, 0, k, :], MEM[:, k, :], gains[:, 1, k:k + 1]).then_inc(S("mem_hi"), 1)
            if k >= 2:
                act.wait_ge(S("mem_acc"), k - 1)
            nc.scalar.activation(MSQ[:, k % 2, :], MEM[:, k, :], ACT.Square).then_inc(S("mem_sq"), 1)

        def x_tile(i, par):
            n = 2 * i + par
            act.wait_ge(S(f"x_in{par}"), 16 * (i + 1))
            apart()
            copy(one(XN[:, 0], n), XS[:, par, :], gains[:, 0, bass.ds(n, 1)]).then_inc(S("x_hi"), 1)
            if not isinstance(i, int):
                act.wait_ge(S("x_acc"), n - 1)
            nc.scalar.activation(SQ[:, par, :], XS[:, par, :], ACT.Square).then_inc(S("x_sq"), 1)

        act.wait_ge(raw[1], 16)
        copy(WHI[:, 1, :], WR[:, 1, :]).then_inc(whi, 1)
        act.wait_ge(S("consts_in"), 7 * 16)
        act.wait_ge(S("mem_sums"), 1)
        root(RM[:], PS[6][:]).then_inc(S("mem_root"), 1)
        act.wait_ge(S("mem_sums"), 2)
        root(rcol[:], PS[7][:, 0:4]).then_inc(S("mem_root"), 1)
        x_tile(0, 0)
        hi(2, 1)
        x_tile(0, 1)
        with nc.scalar.Fori(1, 4) as i:
            hi(1, 0, i, 2)
            x_tile(i, 0)
            hi(2, 1, i, 2)
            x_tile(i, 1)
        for j in range(8):
            hi(KT + j + 1, KT + j)
            if j == 0:
                roots(0)
            if j == 4:
                act.wait_ge(S("angles"), 2)
                nc.scalar.activation(PA[:, 9, :], PA[:, 9, :], ACT.Sin).then_inc(S("sines"), 1)
                nc.scalar.activation(PA[:, 10, :], PA[:, 10, :], ACT.Sin).then_inc(S("sines"), 1)

        def hi_pair(name, i, each, par):
            hi(SLOT0[name] + par + 1, RES0[name] + each * par, i, 2 * each)

        for j in range(4):
            hi(SLOT0["u"] + j + 1, RES0["u"] + NB * j)

        with loop(nc.scalar, 2) as i:
            for par in range(2):
                act.wait_ge(S(f"kv_stored{par}"), 128 * i)
            for jj in range(2):
                j = 2 * i + jj
                for part in range(3):
                    m = 3 * jj + part
                    hi(SLOT0["conv"] + m + 1, RES0["conv"] + NB * m, i, 6 * NB, 3)
                    if part == 1:
                        act.wait_ge(S("z"), NB * (jj + 1) + 2 * NB * i)
                        apart()
                        copy(XC[:], Z[:, 1:T + 2], convw[:, bass.ds(j, 1), 1:2].rearrange("p o a -> p (o a)")
                             ).then_inc(S("tap1"), 1)
                    if part == 2:
                        if jj == 1:
                            act.wait_ge(S("tables_made"), 32 * i)
                        for b in range(NB):
                            n = NB * jj + b
                            act.wait_ge(S("cin"), n + 1 + 2 * NB * i)
                            apart()
                            copy(one(CIN, j)[:, 0, blk(b)], TT[:, n % 2, :]).then_inc(S("cin_hi"), 1)
        with loop(nc.scalar, 2) as i:
            for par in range(2):
                hi_pair("co", i, 6, par)

        def states_away(it, src, d, signal):
            dst = H[:, :, bass.ds(d * GROUPS + 2 * it, 2)].rearrange("p s g -> p g s")
            src = src[:, 0:2 * NC].rearrange("p (g c) -> p g c", g=2)
            for lo, n, c in ((1, NCP, 0), (SLOT_S + 1, NCS, NCP)):
                copy(dst[:, :, lo:lo + n], src[:, :, c:c + n]).then_inc(signal, 1)

        def s5a(i):
            for par in range(2):
                it = 2 * i + par
                act.wait_ge(S("v_turned"), it + 1)
                if not isinstance(i, int):
                    act.wait_ge(S("states_bwd"), it - 1)
                copy(VT[:, par, :], PS[par][:]).then_inc(S("v_staged"), 1)
                act.wait_ge(S("states_fwd"), it + 1)
                apart()
                states_away(it, PS[2 + par], 0, S("h_fwd"))

        act.wait_ge(S("co_stored0"), 64)
        s5a(0)
        with nc.scalar.Fori(1, 8) as i:
            s5a(i)

        def gate(i):
            for par in range(2):
                hi_pair("gate", i, NB, par)
                act.wait_ge(S("gate_stored"), 32 * i + 16 * par)
                copy(bcol[:, par:par + 1], bgate[:, bass.ds(2 * i + par, 1)]).then_inc(S("bias"), 1)
                act.wait_ge(S("bias"), 2 * i + par + 1)
                for b in range(NB):
                    n = NB * par + b
                    act.wait_ge(evac, RES0["gate"] + n + 1 + 2 * NB * i)
                    nc.scalar.activation(GS[:, blk(b)], TG[:, n % 2, :], ACT.Sigmoid, bias=bcol[:, par:par + 1]
                                         ).then_inc(S("gate_made"), 1)

        for par in range(2):
            act.wait_ge(S(f"lags_stored{par}"), 128)
        with loop(nc.scalar, 8) as i:
            gate(i)

        for it in range(GROUPS // 2):
            act.wait_ge(S("s5_out"), it + 1)
            nc.scalar.activation(U[:, 2 * it:2 * it + 2, :], PS[it % 4][:, 0:2 * NC].rearrange(
                "p (g c) -> p g c", g=2), ACT.Gelu_apprx_tanh).then_inc(S("y_made"), 1)
        for k in range(HT):
            act.wait_ge(S(f"y_in{k}"), 128)
            copy(YHL[:, 0, k].rearrange("p (c t) -> p c t", t=C), YL[:, k].rearrange("p t c -> p c t")
                 ).then_inc(S("y_hi"), 1)

        with loop(nc.scalar, 4) as i:
            for par in range(2):
                j = 2 * i + par
                hi_pair("glu", i, 6, par)
                for b in range(NB):
                    act.wait_ge(evac, RES0["glu"] + 6 * par + b + 1 + 12 * i)
                    nc.scalar.activation(SB[:, blk(b)], SB[:, blk(b)], ACT.Sigmoid).then_inc(S("glu_gate"), 1)
                for b in range(NB):
                    act.wait_ge(S("merged"), NB * par + b + 1 + 2 * NB * i)
                    apart()
                    copy(one(XN[:, 0], j)[:, blk(b)], SB[:, blk(b)]).then_inc(S("merged_hi"), 1)

        def residual(name, norm):
            def pair(i):
                for par in range(2):
                    j = 2 * i + par
                    hi_pair(name, i, NB, par)
                    act.wait_ge(evac, RES0[name] + NB * (par + 1) + 2 * NB * i)
                    if not isinstance(i, int):
                        act.wait_ge(S("squares_added"), KT * (norm - 1) + j - 1)
                        apart()
                    nc.scalar.activation(SQ2[:, par, :], one(HR, j), ACT.Square).then_inc(S("squares"), 1)
            pair(0)
            with nc.scalar.Fori(1, 3) as i:
                pair(i)
            hi_pair(name, 3, NB, 0)
            square(norm, KT - 2, RES0[name] + NB * (KT - 1), SQ2[:, 0, :])
            hi_pair(name, 3, NB, 1)

        def square(norm, k, made, out):
            act.wait_ge(evac, made)
            if k >= 2:
                act.wait_ge(S("squares_added"), KT * (norm - 1) + k - 1)
            nc.scalar.activation(out, HR[:, k, :], ACT.Square).then_inc(S("squares"), 1)

        def split_residual(name, norm):
            gain = gains[:, norm + 1, :]
            for k in range(KT):
                if k < KT - 1:
                    act.wait_ge(S("xn_free"), (KT - 1) * (norm - 1) + k + 1)
                else:
                    act.wait_ge(res, RES0[name] + NB * KT)
                    act.wait_ge(evac, RES0[name] + NB * KT)
                copy(XN[:, 0, k, :], HR[:, k, :], gain[:, k:k + 1]).then_inc(S("hn_hi"), 1)
            square(norm, KT - 1, RES0[name] + NB * KT, SQ2[:, 1, :])
            nxt = "q" if norm == 1 else "ffn"
            hi(SLOT0[nxt] + 1, RES0[nxt])
            roots(norm)

        residual("wo", 1)
        split_residual("wo", 1)
        hi_pair("q", 0, NB, 1)
        with nc.scalar.Fori(1, 4) as i:
            for par in range(2):
                hi_pair("q", i, NB, par)

        for par in range(2):
            act.wait_ge(S(f"q_stored{par}"), 64)

        def softmax(n):
            par = n % 2
            for lt in range(4):
                if lt % 2 == 0:
                    act.wait_ge(S("maxima"), 2 * n + lt // 2 + 1)
                nc.scalar.activation(PB[:, par, lt, :], PS[2 * par + lt // 2][:, (lt % 2) * NMEM:(lt % 2 + 1) * NMEM],
                                     ACT.Exp, scale=SCALE, bias=snm[:, par, lt:lt + 1],
                                     accum_out=ssm[:, par, lt:lt + 1]).then_inc(S("exps"), 1)

        softmax(0)
        softmax(1)
        for n in range(HEADS * NB):
            h, b = divmod(n, NB)
            act.wait_ge(S("p_turned"), 2 * n + 2)
            if n >= 2:
                act.wait_ge(S("att_out"), 2 * (n - 1))
            copy(PT[:, n % 2, 1, :], PS[5][:]).then_inc(S("pt_staged"), 1)
            if n + 2 < HEADS * NB:
                softmax(n + 2)
            for e in range(2):
                act.wait_ge(S("att_out"), 2 * n + e + 1)
                copy(XN[:, 0, 2 * h + e, blk(b)], PS[6 + e][:]).then_inc(S("o_hi"), 1)

        residual("xo", 2)
        split_residual("xo", 2)

        def chunk(c, final=False):
            for f in range(4):
                if f or not isinstance(c, int) or c:
                    hi(SLOT0["ffn"] + f + 1, RES0["ffn"] + NB * f, c, CH_RES, 3)
                kk = f // 2
                for b in range(NB):
                    if f % 2 == 0:
                        act.wait_ge(evac, RES0["ffn"] + NB * f + b + 1 + CH_RES * c)
                        nc.scalar.activation(SG[:, blk(b)], TF[:, b % 2, :], ACT.Silu).then_inc(S("silu"), 1)
                    else:
                        act.wait_ge(S("act"), NB * kk + b + 1 + 2 * NB * c)
                        copy(AF[:, 0, kk, blk(b)], TF[:, (b + 1) % 2, :]).then_inc(S("act_hi"), 1)
            for part in range(2):
                if not (final and part):
                    hi(SLOT0["ffn"] + 5 + part, RES0["ffn"] + 4 * NB * (part + 1), c, CH_RES, 3)

        chunk(0)
        with nc.scalar.Fori(1, CHUNKS - 1) as c:
            chunk(c)
        chunk(CHUNKS - 1, final=True)
        q = RES0["ffn"] + CHUNKS * CH_RES - KT * NB
        act.wait_ge(res, q)
        for k in range(KT):
            act.wait_ge(evac, q + NB * (k + 1))
            nc.scalar.activation(FSQ[:, k, :], HR[:, k, :], ACT.Square).then_inc(S("squares"), 1)
            if k == HT - 1:
                for g in range(POOL_TILES):
                    act.wait_ge(S("squares"), 2 * KT + g + 1)
                    copy(HR[:, g, :], HR[:, g, :], gains[:, 4, g:g + 1]).then_inc(S("gained"), 1)
        roots(3)

    @block.vector
    def _(dve):
        step = Count(S("vector_step"))

        def then(ins):
            step.up(ins)
            dve.wait_ge(step.sem, step.n)

        V = nc.vector

        def tt(out, a, b, op):
            then(V.tensor_tensor(out, a, b, op))

        def ts(out, a, s1, s2, op0, op1=None):
            then(V.tensor_scalar(out, a, s1, s2, op0, op1) if op1 is not None
                 else V.tensor_scalar(out, a, s1, None, op0))

        def lo(m, di_i=0):
            par = m % 2
            dve.wait_ge(whi, m + 1 + di_i)
            V.tensor_tensor(WLO[:, par, :], WR[:, par, :], WHI[:, par, :].bitcast(F32), ALU.subtract
                            ).then_inc(wlo, 1)

        def rest(out, full, part):
            return V.tensor_tensor(out, full, part.bitcast(F32), ALU.subtract)

        def newton(r, total, scratch):
            t = scratch[:, 0:r.shape[-1]]
            tt(t, r, r, ALU.mult)
            then(V.scalar_tensor_tensor(out=t, in0=total, scalar=D * EPS, in1=t, op0=ALU.add, op1=ALU.mult))
            ts(t, t, -0.5 / D, 1.5, ALU.mult, ALU.add)
            return V.tensor_tensor(r, r, t, ALU.mult)

        def reciprocals(norm):
            for b in range(NB):
                dve.wait_ge(S("root"), NB * norm + b + 1)
                newton(RB[:, blk(b)], sums_bank(norm, b)[:], NT if norm else NT0).then_inc(S("rms"), 1)
                dve.wait_ge(S("rms"), NB * norm + b + 1)

        A_RE, A_IM, DT, AR, AI, CR, CI, CIS, E, X9, X10, X11, X12, X13, X14, X15 = (PA[:, j, :] for j in range(16))

        def exp_range(x):
            ts(X12, x, 0.5, -87.0, ALU.mult, ALU.max)
            ts(X12, X12, 88.0, None, ALU.min)
            ts(X13, X12, LOG2E, ROUND + 127.0, ALU.mult, ALU.add)
            ts(X14, X13, -(ROUND + 127.0), None, ALU.add)
            then(V.scalar_tensor_tensor(out=X12, in0=X14, scalar=-LN2_HI, in1=X12, op0=ALU.mult, op1=ALU.add))
            then(V.scalar_tensor_tensor(out=X12, in0=X14, scalar=-LN2_LO, in1=X12, op0=ALU.mult, op1=ALU.add))
            ts(X13.bitcast(I32), X13.bitcast(I32), 23, None, ALU.logical_shift_left)

        def exp_series(out):
            terms = 9
            ts(X15, X12, 1.0 / math.factorial(terms), None, ALU.mult)
            for n in range(terms - 1, 0, -1):
                then(V.scalar_tensor_tensor(out=X15, in0=X15, scalar=1.0 / math.factorial(n), in1=X12,
                                            op0=ALU.add, op1=ALU.mult))
            then(V.scalar_tensor_tensor(out=X15, in0=X15, scalar=1.0, in1=X13, op0=ALU.add, op1=ALU.mult))
            tt(out, X15, X15, ALU.mult)

        def parameters(part):
            if part == 0:
                dve.wait_ge(S("params_in"), 48)
                exp_range(DT)
            elif part == 1:
                exp_series(DT)
            elif part == 2:
                tt(AR, A_RE, DT, ALU.mult)
                tt(AI, A_IM, DT, ALU.mult)
                ts(X11, AI, 1.0 / (2 * math.pi), ROUND, ALU.mult, ALU.add)
                ts(X11, X11, -ROUND, None, ALU.add)
                for turn in TWO_PI:
                    then(V.scalar_tensor_tensor(out=AI, in0=X11, scalar=-turn, in1=AI, op0=ALU.mult, op1=ALU.add))
                ts(AI, AI, 3.1415925, -3.1415925, ALU.min, ALU.max)
                V.tensor_scalar(X9, AI, 1.0, None, ALU.mult).then_inc(S("angles"), 1)
                V.tensor_scalar(X10, AI, 0.5, None, ALU.mult).then_inc(S("angles"), 1)
            elif part == 3:
                exp_range(AR)
            elif part == 4:
                exp_series(E)
            elif part == 5:
                dve.wait_ge(S("sines"), 2)
                tt(X10, X10, X10, ALU.mult)
                ts(X10, X10, -2.0, 1.0, ALU.mult, ALU.add)
                tt(AR, E, X10, ALU.mult)
                tt(AI, E, X9, ALU.mult)
                ts(X11, AR, -1.0, None, ALU.add)
                tt(X12, A_RE, A_RE, ALU.mult)
                tt(X13, A_IM, A_IM, ALU.mult)
                tt(X12, X12, X13, ALU.add)
                then(V.reciprocal(X12, X12))
            elif part == 6:
                tt(X13, X11, A_RE, ALU.mult)
                tt(X14, AI, A_IM, ALU.mult)
                tt(X13, X13, X14, ALU.add)
                tt(CR, X13, X12, ALU.mult)
                tt(X13, AI, A_RE, ALU.mult)
                tt(X14, X11, A_IM, ALU.mult)
                tt(X13, X13, X14, ALU.subtract)
                V.tensor_tensor(CI, X13, X12, ALU.mult).then_inc(S("params_made"), 1)

        V.memset(MACC[:], 0.0).then_inc(S("cleared"), 1)
        dve.wait_ge(S("cleared"), 1)
        lo(0)
        dve.wait_ge(S("gains_in"), 16)
        for k in range(KT):
            dve.wait_ge(S("mem_hi"), k + 1)
            V.scalar_tensor_tensor(out=MN[:, 1, k, :], in0=MEM[:, k, :], scalar=gains[:, 1, k:k + 1],
                                   in1=MN[:, 0, k, :].bitcast(F32), op0=ALU.mult, op1=ALU.subtract
                                   ).then_inc(S("mem_lo"), 1)
            if k:
                dve.wait_ge(S("mem_acc"), k)
            dve.wait_ge(S("mem_sq"), k + 1)
            V.tensor_tensor(MACC[:], MACC[:], MSQ[:, k % 2, :], ALU.add).then_inc(S("mem_acc"), 1)
        lo(1)

        def kv(i, par):
            n = 2 * i + par
            dve.wait_ge(res, n + 1)
            dve.wait_ge(S(f"kv_stored{par}"), 16 * i)
            V.tensor_tensor(KVS[:, par, :], key_bank(i, par)[:], RM[:], ALU.mult).then_inc(evac, 1)

        def x_tile(i, par):
            n = 2 * i + par
            dve.wait_ge(S("x_hi"), n + 1)
            V.scalar_tensor_tensor(out=one(XN[:, 1], n), in0=XS[:, par, :], scalar=gains[:, 0, bass.ds(n, 1)],
                                   in1=one(XN[:, 0], n).bitcast(F32), op0=ALU.mult, op1=ALU.subtract
                                   ).then_inc(S("x_lo"), 1)

        dve.wait_ge(S("mem_root"), 1)
        newton(RM[:], PS[6][:], NT0).then_inc(S("mem_rms"), 1)
        dve.wait_ge(S("mem_rms"), 1)
        dve.wait_ge(S("mem_root"), 2)
        newton(rcol[:], PS[7][:, 0:4], NT0).then_inc(S("mem_rms"), 1)
        dve.wait_ge(S("mem_rms"), 2)
        x_tile(0, 0)
        kv(0, 0)
        lo(2)
        x_tile(0, 1)
        kv(0, 1)
        lo(3)
        x_tile(1, 0)
        kv(1, 0)
        lo(4)
        x_tile(1, 1)
        kv(1, 1)
        with V.Fori(2, 4) as i:
            lo(1, 2 * i)
            x_tile(i, 0)
            kv(i, 0)
            lo(2, 2 * i)
            x_tile(i, 1)
            kv(i, 1)
        for j in range(8):
            lo(KT + j + 1)
            if j == 0:
                reciprocals(0)
            if j % 4 == 3:
                for m in range(M2 // P):
                    n = KT + j - 3 + m
                    dve.wait_ge(res, KT + j + 1)
                    if j > 3:
                        dve.wait_ge(S(f"kv_stored{n % 2}"), 16 * (KT // 2 + 2))
                    V.tensor_scalar(VVS[:, m, :], PS[VBANKS[j // 4][m]][:], rcol[:, m:m + 1], None, ALU.mult
                                    ).then_inc(evac, 1)
            parameters(j)

        def take(q, i=0, each=0):
            dve.wait_ge(res, q + 1 + each * i)
            return bank(q)[:]

        for par in range(2):
            dve.wait_ge(S(f"kv_stored{par}"), 128)
        for j in range(4):
            lo(SLOT0["u"] + j + 1)
            if j >= 2:
                dve.wait_ge(S(f"u_stored{j % 2}"), 16)
            for b in range(NB):
                src = take(RES0["u"] + NB * j + b)
                V.tensor_tensor(UB[:, j % 2, :, b * 64:(b + 1) * 64].rearrange("p s c -> p c s"),
                                src.rearrange("p (c s) -> p c s", s=C),
                                RB[:, blk(b)].rearrange("p (c s) -> p c s", s=C), ALU.mult).then_inc(evac, 1)

        for par in range(2):
            dve.wait_ge(S(f"u_stored{par}"), 32)
        for col in (0, T_PROMPT + 1, T + 2):
            step.up(V.memset(Z[:, col:col + 1], 0.0))
        dve.wait_ge(step.sem, step.n)
        with loop(V, 2) as i:
            step.enter(i, 2)
            for jj in range(2):
                j = 2 * i + jj
                q = RES0["conv"] + 9 * jj
                each = 6 * NB
                lo(SLOT0["conv"] + 3 * jj + 1, 6 * i)
                for b in range(NB):
                    V.tensor_tensor(XC[:, zcols(b)], take(q + b, i, each), RB[:, blk(b)], ALU.mult
                                    ).then_inc(evac, 1)
                lo(SLOT0["conv"] + 3 * jj + 2, 6 * i)
                for b in range(NB):
                    V.tensor_tensor(TT[:, b % 2, :], take(q + 3 + b, i, each), RB[:, blk(b)], ALU.mult
                                    ).then_inc(evac, 1)
                    dve.wait_ge(evac, q + 4 + b + each * i)
                    V.tensor_tensor(Z[:, b * BLK + 1 + (b == 2):(b + 1) * BLK + 1 + (b == 2)], TT[:, b % 2, :],
                                    XC[:, zcols(b)], ALU.mult).then_inc(S("z"), 1)
                dve.wait_ge(S("z"), NB * (jj + 1) + 2 * NB * i)
                lo(SLOT0["conv"] + 3 * jj + 3, 6 * i)
                dve.wait_ge(S("tap1"), jj + 1 + 2 * i)
                tap = convw[:, bass.ds(j, 1), :].rearrange("p o a -> p (o a)")
                for w, z in ((0, 0), (2, 2)):
                    then(V.scalar_tensor_tensor(out=XC[:], in0=Z[:, z:z + T + 1], scalar=tap[:, w:w + 1],
                                                in1=XC[:], op0=ALU.mult, op1=ALU.add)) if w == 0 else \
                        V.scalar_tensor_tensor(out=XC[:], in0=Z[:, z:z + T + 1], scalar=tap[:, w:w + 1],
                                               in1=XC[:], op0=ALU.mult, op1=ALU.add).then_inc(S("conv"), 1)
                dve.wait_ge(S("conv"), jj + 1 + 2 * i)

                def cin_lo(b):
                    n = NB * jj + b
                    dve.wait_ge(S("cin_hi"), n + 1 + 2 * NB * i)
                    rest(one(CIN, j)[:, 1, blk(b)], TT[:, n % 2, :], one(CIN, j)[:, 0, blk(b)]
                         ).then_inc(S("cin_lo"), 1)

                for b in range(NB):
                    n = NB * jj + b
                    src = take(q + 6 + b, i, each)
                    if b == 2:
                        dve.wait_ge(S("cin_lo"), n - 1 + 2 * NB * i)
                    V.tensor_tensor(TT[:, n % 2, :], src, RB[:, blk(b)], ALU.mult
                                    ).then_inc(evac, 1)
                    dve.wait_ge(evac, q + 7 + b + each * i)
                    V.tensor_tensor(TT[:, n % 2, :], TT[:, n % 2, :], XC[:, zcols(b)], ALU.mult
                                    ).then_inc(S("cin"), 1)
                    if b:
                        cin_lo(b - 1)
                cin_lo(NB - 1)
            step.leave(2)

        def conv_out(i):
            for par in range(2):
                lo(SLOT0["co"] + par + 1, 2 * i)
                for e in range(2):
                    dve.wait_ge(S(f"co_stored{e}"), 32 * i + 16 * par)
                    for b in range(NB):
                        V.tensor_copy(COS[:, e, blk(b)], take(RES0["co"] + 6 * par + 3 * e + b, i, 12)
                                      ).then_inc(evac, 1)

        dve.wait_ge(S("tables_made"), 32)
        for par in range(2):
            dve.wait_ge(S(f"tables_stored{par}"), 2 * 4 * 32)
        with loop(V, 2) as i:
            conv_out(i)

        for e in range(2):
            dve.wait_ge(S(f"co_stored{e}"), 64)
        tt(DM[0:GP], ident[0:GP, 0:GP].unsqueeze(1).to_broadcast([GP, GROUPS, GP]),
           s5d[0:GP, :].unsqueeze(2).to_broadcast([GP, GROUPS, GP]), ALU.mult)
        for slot in (0, SLOT_S):
            then(V.memset(H[:, slot, :], 0.0))

        def s5a(i):
            for par in range(2):
                it = 2 * i + par
                dve.wait_ge(S("lags"), it + 1)
                dve.wait_ge(S(f"lags_stored{par}"), 16 * i)
                then(V.tensor_copy(LL[0:GP, par], PS[6 + par][0:GP, 0:2 * LAGS * GP].rearrange(
                    "p (g l) -> p g l", g=2)))
                lag0 = LL[0:GP, par, :, (C - 1) * GP:C * GP]
                V.tensor_tensor(lag0, lag0, DM[0:GP, bass.ds(2 * it, 2), :], ALU.add).then_inc(S("lags_staged"), 1)
                dve.wait_ge(S("states_bwd"), it + 1)
                dst = H[:, :, bass.ds(GROUPS + 2 * it, 2)].rearrange("p s g -> p g s")
                src = PS[4 + par][:, 0:2 * NC].rearrange("p (g c) -> p g c", g=2)
                for at_, n, c in ((1, NCP, 0), (SLOT_S + 1, NCS, NCP)):
                    V.tensor_copy(dst[:, :, at_:at_ + n], src[:, :, c:c + n][:, :, ::-1]
                                  ).then_inc(S("h_bwd"), 1)

        with loop(V, 8) as i:
            step.enter(i, 2)
            s5a(i)
            step.leave(8)

        dve.wait_ge(S("h_fwd"), 32)
        dve.wait_ge(S("h_bwd"), 32)
        scan = Count(S("scan"))

        def advance(slot, both):
            def seqs(a, s, p0=0, p1=P):
                a = a[p0:p1, bass.ds(s, SLOT_S + 1 if both else 1), :]
                return a[:, ::SLOT_S, :] if both else a

            n = 2 if both else 1

            def wide(a, p0=0, p1=P):
                return a[p0:p1].unsqueeze(1).to_broadcast([p1 - p0, n, GD])

            half = P // 2
            nxt = seqs(H, slot + 1)
            scan.up(V.tensor_tensor(S1[:, 0:n, :], seqs(H, slot), wide(LR), ALU.mult))
            real = scan.n
            scan.up(V.tensor_tensor(S2[0:half, 0:n, :], seqs(H, slot, half, P), wide(LI, half, P), ALU.mult))
            scan.up(V.tensor_tensor(S2[half:P, 0:n, :], seqs(H, slot, 0, half), wide(LI, 0, half), ALU.mult))
            dve.wait_ge(scan.sem, real)
            scan.up(V.tensor_tensor(nxt, nxt, S1[:, 0:n, :], ALU.add))
            dve.wait_ge(scan.sem, scan.n)
            scan.up(V.tensor_tensor(nxt, nxt, S2[:, 0:n, :], ALU.add))
            dve.wait_ge(scan.sem, scan.n)

        def gates(i, both, slot, steps):
            for par in range(2):
                lo(SLOT0["gate"] + par + 1, 2 * i)
                for b in range(NB):
                    n = NB * par + b
                    src = take(RES0["gate"] + n, i, 2 * NB)
                    if both != "first" or n >= 2:
                        dve.wait_ge(S("gate_made"), n - 1 + 2 * NB * i)
                    V.tensor_tensor(TG[:, n % 2, :], src, RB[:, blk(b)], ALU.mult).then_inc(evac, 1)
                for s in range(steps[par]):
                    advance(slot + steps[0] * par + s, both is not False)

        gates(0, "first", 0, (8, 8))
        with V.Fori(1, 4) as i:
            scan.enter(i - 1, 80)
            gates(i, True, 16 * i, (8, 8))
            scan.leave(3)
        with V.Fori(4, 7) as i:
            scan.enter(i - 4, 90)
            gates(i, False, 18 * i - 8, (9, 9))
            scan.leave(3)
        gates(7, False, SCAN_STEPS - 10, (10, 0))
        assert scan.n == 5 * SCAN_STEPS

        for k in range(HT):
            dve.wait_ge(S("y_hi"), k + 1)
            V.tensor_tensor(YHL[:, 1, k].rearrange("p (c t) -> p c t", t=C),
                            YL[:, k].rearrange("p t c -> p c t"),
                            YHL[:, 0, k].rearrange("p (c t) -> p c t", t=C).bitcast(F32), ALU.subtract
                            ).then_inc(S("y_lo"), 1)

        with loop(V, 4) as i:
            step.enter(i, 2 * NB)
            for par in range(2):
                j = 2 * i + par
                q = RES0["glu"] + 6 * par
                lo(SLOT0["glu"] + par + 1, 2 * i)
                dve.wait_ge(S("merged_lo"), NB * par + 2 * NB * i)
                for b in range(NB):
                    V.tensor_copy(SB[:, blk(b)], take(q + b, i, 12)).then_inc(evac, 1)

                def merged_lo(b):
                    n = NB * par + b
                    dve.wait_ge(S("merged_hi"), n + 1 + 2 * NB * i)
                    rest(one(XN[:, 1], j)[:, blk(b)], SB[:, blk(b)], one(XN[:, 0], j)[:, blk(b)]
                         ).then_inc(S("merged_lo"), 1)

                for b in range(NB):
                    n = NB * par + b
                    src = take(q + NB + b, i, 12)
                    dve.wait_ge(S("glu_gate"), n + 1 + 2 * NB * i)
                    V.tensor_tensor(SB[:, blk(b)], src, SB[:, blk(b)], ALU.mult).then_inc(evac, 1)
                    dve.wait_ge(evac, q + NB + b + 1 + 12 * i)
                    dve.wait_ge(S(f"glu_in{par}"), 48 * (i + 1))
                    tt(SB[:, blk(b)], SB[:, blk(b)], G1L[:, par, blk(b)], ALU.mult)
                    dve.wait_ge(S("gated_conv"), j + 1)
                    V.tensor_tensor(SB[:, blk(b)], SB[:, blk(b)], G2L[:, par, blk(b)], ALU.add
                                    ).then_inc(S("merged"), 1)
                    if b:
                        merged_lo(b - 1)
                merged_lo(NB - 1)
            step.leave(4)

        def add_squares(norm, k, sq):
            dve.wait_ge(S("squares"), KT * (norm - 1) + k + 1)
            dve.wait_ge(S("squares_added"), KT * (norm - 1) + k)
            V.tensor_tensor(ACC2[:], ACC2[:], sq, ALU.add).then_inc(S("squares_added"), 1)

        def residual(name, norm, first):
            def pair(i):
                for par in range(2):
                    j = 2 * i + par
                    lo(SLOT0[name] + par + 1, 2 * i)
                    if first:
                        dve.wait_ge(S(f"xr_in{par}"), 16 * (i + 1))
                    for b in range(NB):
                        src = take(RES0[name] + NB * par + b, i, 2 * NB)
                        h = one(HR, j)[:, blk(b)]
                        V.tensor_tensor(h, src, XR[:, par, blk(b)] if first else h, ALU.add).then_inc(evac, 1)
                    if par or not isinstance(i, int):
                        add_squares(norm, j - 1, SQ2[:, 1 - par, :])
            then(V.memset(ACC2[:], 0.0))
            pair(0)
            with V.Fori(1, 3) as i:
                pair(i)

            def last(j):
                for b in range(NB):
                    src = take(RES0[name] + NB * j + b)
                    if first and b == 0:
                        dve.wait_ge(S(f"xr_in{j % 2}"), 16 * (j // 2 + 1))
                    h = HR[:, j, blk(b)]
                    V.tensor_tensor(h, src, XR[:, j % 2, blk(b)] if first else h, ALU.add).then_inc(evac, 1)

            def split(k):
                dve.wait_ge(S("hn_hi"), KT * (norm - 1) + k + 1)
                V.scalar_tensor_tensor(out=XN[:, 1, k, :], in0=HR[:, k, :], scalar=gains[:, norm + 1, k:k + 1],
                                       in1=XN[:, 0, k, :].bitcast(F32), op0=ALU.mult, op1=ALU.subtract
                                       ).then_inc(S("hn_lo"), 1)

            lo(SLOT0[name] + KT - 1)
            last(KT - 2)
            add_squares(norm, KT - 3, SQ2[:, 1, :])
            lo(SLOT0[name] + KT)
            split(0)
            add_squares(norm, KT - 2, SQ2[:, 0, :])
            for k in range(1, KT - 1):
                split(k)
            last(KT - 1)
            split(KT - 1)
            lo(SLOT0["q" if norm == 1 else "ffn"] + 1)
            add_squares(norm, KT - 1, SQ2[:, 1, :])
            reciprocals(norm)

        dve.wait_ge(S("merged_lo"), NB * KT)
        residual("wo", 1, True)

        def queries(i, par):
            dve.wait_ge(S(f"q_stored{par}"), 16 * i)
            for b in range(NB):
                V.tensor_tensor(QS[:, par, blk(b)], take(RES0["q"] + NB * par + b, i, 2 * NB), RB[:, blk(b)],
                                ALU.mult).then_inc(evac, 1)

        queries(0, 0)
        lo(SLOT0["q"] + 2)
        queries(0, 1)
        with V.Fori(1, 4) as i:
            for par in range(2):
                lo(SLOT0["q"] + par + 1, 2 * i)
                queries(i, par)

        def maxima(n):
            par = n % 2
            for half in range(2):
                dve.wait_ge(S("scores"), 2 * n + half + 1)
                lts = slice(2 * half, 2 * half + 2)
                then(V.reduce_max(smx[:, par, lts], PS[2 * par + half][:].rearrange("p (l m) -> p l m", l=2), AX.X))
                V.tensor_scalar(snm[:, par, lts], smx[:, par, lts], -SCALE, None, ALU.mult).then_inc(S("maxima"), 1)

        def probs(n):
            par = n % 2
            dve.wait_ge(S("exps"), 4 * (n + 1))
            then(V.reciprocal(sri[:, par, :], ssm[:, par, :]))
            for lt in range(4):
                V.tensor_scalar(PB[:, par, lt, :], PB[:, par, lt, :], sri[:, par, lt:lt + 1], None, ALU.mult
                                ).then_inc(S("probs"), 1)

        for n in range(2):
            maxima(n)
            probs(n)
        for n in range(HEADS * NB):
            h, b = divmod(n, NB)
            dve.wait_ge(S("p_turned"), 2 * n + 1)
            if n >= 2:
                dve.wait_ge(S("att_out"), 2 * (n - 1))
            V.tensor_copy(PT[:, n % 2, 0, :], PS[4][:]).then_inc(S("pt_staged"), 1)
            if n + 2 < HEADS * NB:
                maxima(n + 2)
            for e in range(2):
                dve.wait_ge(S("o_hi"), 2 * n + e + 1)
                V.tensor_tensor(XN[:, 1, 2 * h + e, blk(b)], PS[6 + e][:], XN[:, 0, 2 * h + e, blk(b)].bitcast(F32),
                                ALU.subtract).then_inc(S("o_lo"), 1)
            if n + 2 < HEADS * NB:
                probs(n + 2)

        residual("xo", 2, False)

        def chunk(c, final=False):
            for f in range(4):
                if f or not isinstance(c, int) or c:
                    lo(SLOT0["ffn"] + f + 1, CH_SLOTS * c)
                kk, q = f // 2, RES0["ffn"] + NB * f

                def act_lo(b):
                    dve.wait_ge(S("act_hi"), NB * kk + b + 1 + 2 * NB * c)
                    rest(AF[:, 1, kk, blk(b)], TF[:, (b + 1) % 2, :], AF[:, 0, kk, blk(b)]
                         ).then_inc(S("act_lo"), 1)

                for b in range(NB):
                    if f % 2 == 0:
                        src = take(q + b, c, CH_RES)
                        if b == 0:
                            dve.wait_ge(S("act_lo"), NB * kk + 2 * NB * c)
                        if b == 2:
                            dve.wait_ge(S("silu"), NB * kk + 1 + 2 * NB * c)
                        V.tensor_tensor(TF[:, b % 2, :], src, RB[:, blk(b)], ALU.mult).then_inc(evac, 1)
                    else:
                        src = take(q + b, c, CH_RES)
                        dve.wait_ge(S("silu"), NB * kk + min(b + 2, 3) + 2 * NB * c)
                        if b == 2:
                            dve.wait_ge(S("act_lo"), NB * kk + 1 + 2 * NB * c)
                        V.tensor_tensor(TF[:, (b + 1) % 2, :], src, RB[:, blk(b)], ALU.mult).then_inc(evac, 1)
                        dve.wait_ge(evac, q + b + 1 + CH_RES * c)
                        V.tensor_tensor(TF[:, (b + 1) % 2, :], TF[:, (b + 1) % 2, :], SG[:, blk(b)], ALU.mult
                                        ).then_inc(S("act"), 1)
                        if b:
                            act_lo(b - 1)
                if f % 2:
                    act_lo(NB - 1)
            for part in range(2):
                if not (final and part):
                    lo(SLOT0["ffn"] + 5 + part, CH_SLOTS * c)
                for e in range(4):
                    for b in range(NB):
                        q = RES0["ffn"] + 4 * NB + part * 4 * NB + NB * e + b
                        h = HR[:, 4 * part + e, blk(b)]
                        V.tensor_tensor(h, take(q, c, CH_RES), h, ALU.add).then_inc(evac, 1)
                    if final and part:
                        for k in (2 * e, 2 * e + 1):
                            add_squares(3, k, FSQ[:, k, :])

        chunk(0)
        with V.Fori(1, CHUNKS - 1) as c:
            chunk(c)
        then(V.memset(ACC2[:], 0.0))
        chunk(CHUNKS - 1, final=True)
        for b in range(NB):
            dve.wait_ge(S("root"), NB * 3 + b + 1)
            newton(RB[:, blk(b)], sums_bank(3, b)[:], NT).then_inc(S("rms"), 1)
            dve.wait_ge(S("rms"), NB * 3 + b + 1)
            for k in range(POOL_TILES, KT):
                h = HR[:, k, blk(b)]
                V.scalar_tensor_tensor(out=h, in0=h, scalar=gains[:, 4, k:k + 1], in1=RB[:, blk(b)],
                                       op0=ALU.mult, op1=ALU.mult).then_inc(S("y_out"), 1)

    block.__exit__(None, None, None)


def kernel(**inputs):
    import numpy as np
    import concourse.bacc as bacc
    from concourse.bass_utils import run_bass_kernel_spmd

    a = {k: np.asarray(v) for k, v in inputs.items()}

    def tiles(w):
        r, c = w.shape
        return w.reshape(r // P, P, c // P, P).transpose(2, 1, 0, 3).reshape(c // P, P, -1)

    w_in = tiles(a["w_in"][0])
    values = a["w_kv"][0][:, D:].reshape(4, 2, P, 2, BLK).transpose(3, 0, 2, 1, 4).reshape(KT, P, SLOTW)
    kv = np.concatenate([tiles(a["w_kv"][0][:, :D]), values])
    u, xc, gb, gc, g = (w_in[i:j] for i, j in ((0, 4), (4, 8), (8, 12), (12, 16), (16, 32)))
    conv = np.stack([xc, gc, gb], 1).reshape(-1, P, SLOTW)
    co = tiles(a["w_conv_out"][0]).reshape(4, 2, P, 512).transpose(0, 2, 1, 3).reshape(4, P, SLOTW)
    glu = np.concatenate([tiles(a["w_glu_b"][0]), tiles(a["w_glu_a"][0])], 2)
    gu = tiles(a["w_gate_up"][0])
    down = a["w_down"][0].reshape(CHUNKS, 2, P, 2, 4, P).transpose(0, 3, 2, 4, 1, 5).reshape(CHUNKS, 2, P, SLOTW)
    ffn = []
    for c in range(CHUNKS):
        ffn += [gu[2 * c], gu[FT + 2 * c], gu[2 * c + 1], gu[FT + 2 * c + 1], down[c, 0], down[c, 1]]
    stream = np.concatenate([kv, u, conv, co, g, glu, tiles(a["w_o"][0]), tiles(a["w_q"][0]),
                             tiles(a["w_xo"][0]), np.stack(ffn)])

    def cols(v):
        return v.reshape(-1, P).T

    def states(v):
        v = v.transpose(2, 0, 1).reshape(NS, GD)
        return np.concatenate([v, v])

    def stacked(re, im):
        return np.concatenate([re, im], 1)

    br, bi = (a[k][0].transpose(0, 2, 1, 3) for k in ("s5_b_re", "s5_b_im"))
    cr, ci = (a[k][0].transpose(0, 3, 1, 2) for k in ("s5_c_re", "s5_c_im"))
    f = np.float32
    half = np.where(np.arange(P) < P // 2, -1.0, 1.0)
    arrays = {
        "W_all": stream,
        "xT": np.concatenate([a["x_prompt"][0].T, a["x_sample"][0].T], 1).reshape(KT, P, T),
        "memT": np.concatenate([a["mem_prompt"][0].T, a["mem_sample"][0].T], 1).reshape(KT, P, M2)
        .transpose(1, 0, 2),
        "gains": np.stack([cols(v) for v in (a["norm_mix_g"][0], a["norm_mem_g"][0], a["norm_xattn_g"][0],
                                             a["norm_ffn_g"][0], a["norm_final_g"])], 1),
        "bgate": cols(a["b_gate"][0]),
        "convw": a["conv_w"][0].reshape(3, HT, P).transpose(2, 1, 0),
        "a_re": states(a["s5_a_re"][0]), "a_im": states(a["s5_a_im"][0]),
        "log_dt": np.repeat(a["s5_log_dt"][0].reshape(1, GD), P, 0),
        "s5_d": a["s5_d"][0].reshape(GROUPS, GP).T,
        "BX": stacked(br, bi), "BY": stacked(bi, br), "CX": stacked(cr, ci), "CY": stacked(ci, cr),
        "ones": np.ones((P, P), f), "ident": np.eye(P, dtype=f), "eps": np.full((P, 1), EPS, f),
        "sgn": np.stack([half, -half], 1).astype(f),
    }
    nc = bacc.Bacc("TRN2", target_bir_lowering=False, num_devices=1, dynamic_dma_scratch_size=1024)
    io = {}
    for name, v in arrays.items():
        arrays[name] = np.ascontiguousarray(v)
        io[name] = nc.dram_tensor(name, v.shape, F32, kind="ExternalInput").ap()
    io["yT"] = nc.dram_tensor("yT", (KT, P, T), F32, kind="ExternalOutput").ap()
    shapes = {"U": (DH, C, NC), "CO": (KT, P, T), "G": (2 * KT, P, T), "V": (P, GROUPS, 2, P),
              "W": (P, GROUPS, WROW), "BB": (2, P, GROUPS, GP), "L": (GP, GROUPS, LAGS * GP),
              "M": (P, GROUPS, P), "Y": (P, GROUPS, NC), "KV": (2 * KT, P, M2), "Q": (KT, P, T)}
    scratch = {k: nc.dram_tensor(f"scratch_{k}", s, F32).ap() for k, s in shapes.items()}
    build(nc, io, scratch)
    r = run_bass_kernel_spmd(nc, [arrays], core_ids=[0])
    y = np.asarray(r.results[0]["yT"]).reshape(D, T).T
    return y[None, :T_PROMPT], y[None, T_PROMPT:]
```
